# Optimizing a Trainium2 kernel written in Bass

```python
import jax, jax.numpy as jnp
from jax import lax
import numpy as np
import math

D_MODEL = 1024
BATCH = 1
SEQ = 1024
DEPTH = 1

HEAD_DIM = D_MODEL // 16
ATTN_HEADS = 6
ATTN_WIDTH = ATTN_HEADS * HEAD_DIM
ATTN_PATTERNS = ((128, 1), (512, 4), (2048, 16))
HEADS_PER_PATTERN = ATTN_HEADS // len(ATTN_PATTERNS)
CONV_GROUPS = 4
CONV_WIDTH = CONV_GROUPS * HEAD_DIM
CONV_TAPS = 31
LRU_HEADS = 6
LRU_WIDTH = LRU_HEADS * HEAD_DIM
LRU_CONV_TAPS = 4
LRU_C = 8.0
MIX_WIDTH = ATTN_WIDTH + CONV_WIDTH + LRU_WIDTH
D_FF = 4 * D_MODEL
RMS_EPS = 1e-6
LN_EPS = 1e-5

Q0 = 0
K0 = Q0 + ATTN_WIDTH
V0 = K0 + ATTN_WIDTH
CA0 = V0 + ATTN_WIDTH
CG0 = CA0 + CONV_WIDTH
LG0 = CG0 + CONV_WIDTH
LX0 = LG0 + LRU_WIDTH
IN_COLS = LX0 + LRU_WIDTH


def rmsnorm(x, g):
    xf = x.astype(jnp.float32)
    y = xf * lax.rsqrt(jnp.mean(xf * xf, axis=-1, keepdims=True) + RMS_EPS)
    return y.astype(x.dtype) * g

def layernorm(x, g, b):
    xf = x.astype(jnp.float32)
    mu = jnp.mean(xf, axis=-1, keepdims=True)
    var = jnp.mean(jnp.square(xf - mu), axis=-1, keepdims=True)
    y = (xf - mu) * lax.rsqrt(var + LN_EPS)
    return y.astype(x.dtype) * g + b

def alibi_slopes(n):
    return jnp.asarray(2.0 ** (-8.0 * np.arange(1, n + 1) / n), dtype=jnp.float32)

def causal_depthwise_conv(x, w, b):
    K, C = w.shape
    y = lax.conv_general_dilated(x, w[:, None, :], window_strides=(1,), padding=[(K - 1, 0)],
                                 dimension_numbers=("NWC", "WIO", "NWC"), feature_group_count=C)
    return y + b

def dilated_window_attention(q, k, v, slopes, window, dilation):
    B, S, H, Dh = q.shape
    W = window // dilation
    L = S // dilation
    nb = -(-L // W)
    Lp = nb * W

    def to_blocks(t):
        t = t.reshape(B, L, dilation, H, Dh).transpose(0, 2, 3, 1, 4)
        t = jnp.pad(t, ((0, 0), (0, 0), (0, 0), (0, Lp - L), (0, 0)))
        return t.reshape(B, dilation, H, nb, W, Dh)

    def with_prev(t):
        prev = jnp.pad(t, ((0, 0), (0, 0), (0, 0), (1, 0), (0, 0), (0, 0)))[:, :, :, :-1]
        return jnp.concatenate([prev, t], axis=4)

    qb = to_blocks(q)
    kb = with_prev(to_blocks(k))
    vb = with_prev(to_blocks(v))
    s = jnp.einsum("brhnqc,brhnkc->brhnqk", qb, kb).astype(jnp.float32) * (Dh ** -0.5)
    qi = jnp.arange(W)[:, None]
    kj = jnp.arange(2 * W)[None, :]
    dist = qi + W - kj
    band = (dist >= 0) & (dist <= W)
    has_prev = (jnp.arange(nb)[:, None, None] > 0) | (kj[None] >= W)
    valid = band[None] & has_prev
    bias = -slopes[:, None, None] * (dilation * dist).astype(jnp.float32)[None]
    s = jnp.where(valid[None, None, None], s + bias[None, None, :, None], -jnp.inf)
    m = jnp.max(s, axis=-1, keepdims=True)
    p = jnp.exp(s - m)
    l = jnp.sum(p, axis=-1, keepdims=True)
    o = jnp.einsum("brhnqk,brhnkc->brhnqc", p, vb.astype(jnp.float32)) / l
    lse = (m + jnp.log(l))[..., 0]
    o = o.reshape(B, dilation, H, Lp, Dh)[:, :, :, :L].transpose(0, 3, 1, 2, 4).reshape(B, S, H, Dh)
    lse = lse.reshape(B, dilation, H, Lp)[..., :L].transpose(0, 3, 1, 2).reshape(B, S, H)
    return o, lse

def attention_mixer(q, k, v):
    B, S = q.shape[:2]
    slopes = alibi_slopes(ATTN_HEADS)
    outs, lses = [], []
    for g, (window, dilation) in enumerate(ATTN_PATTERNS):
        sl = slice(g * HEADS_PER_PATTERN, (g + 1) * HEADS_PER_PATTERN)
        o, lse = dilated_window_attention(q[:, :, sl], k[:, :, sl], v[:, :, sl], slopes[sl], window, dilation)
        outs.append(o)
        lses.append(lse)
    o = jnp.stack(outs, axis=2)
    lse = jnp.stack(lses, axis=2)
    alpha = jax.nn.softmax(lse, axis=2)
    return (o * alpha[..., None]).reshape(B, S, ATTN_WIDTH).astype(q.dtype)

def conv_module(a, gate, dw_w, dw_b, ln_g, ln_b):
    u = a * jax.nn.sigmoid(gate)
    u = causal_depthwise_conv(u, dw_w, dw_b)
    u = layernorm(u, ln_g, ln_b)
    return jax.nn.silu(u)

def rg_lru(x, w_a, b_a, w_x, b_x, lam):
    B, S, C = x.shape
    xh = x.reshape(B, S, LRU_HEADS, C // LRU_HEADS)
    r = jax.nn.sigmoid(jnp.einsum("bshi,hio->bsho", xh, w_a).reshape(B, S, C) + b_a)
    i = jax.nn.sigmoid(jnp.einsum("bshi,hio->bsho", xh, w_x).reshape(B, S, C) + b_x)
    log_a = -LRU_C * r.astype(jnp.float32) * jax.nn.softplus(-lam.astype(jnp.float32))
    a = jnp.exp(log_a)
    b = jnp.sqrt(-jnp.expm1(2.0 * log_a)) * (i * x).astype(jnp.float32)

    def combine(left, right):
        a1, b1 = left
        a2, b2 = right
        return a1 * a2, a2 * b1 + b2

    _, h = lax.associative_scan(combine, (a, b), axis=1)
    return h.astype(x.dtype)

def recurrent_mixer(gate, xr, cw, cb, w_a, b_a, w_x, b_x, lam):
    u = causal_depthwise_conv(xr, cw, cb)
    return jax.nn.gelu(gate) * rg_lru(u, w_a, b_a, w_x, b_x, lam)

def hybrid_layer(x, norm1_g, w_in, conv_dw_w, conv_dw_b, conv_ln_g, conv_ln_b,
                 lru_conv_w, lru_conv_b, lru_wa, lru_ba, lru_wx, lru_bx, lru_lambda,
                 w_out, norm2_g, w_up, w_down):
    B, S, _ = x.shape
    h = rmsnorm(x, norm1_g)
    z = jnp.einsum("bsd,dc->bsc", h, w_in)
    q = z[..., Q0:K0].reshape(B, S, ATTN_HEADS, HEAD_DIM)
    k = z[..., K0:V0].reshape(B, S, ATTN_HEADS, HEAD_DIM)
    v = z[..., V0:CA0].reshape(B, S, ATTN_HEADS, HEAD_DIM)
    y_attn = attention_mixer(q, k, v)
    y_conv = conv_module(z[..., CA0:CG0], z[..., CG0:LG0], conv_dw_w, conv_dw_b, conv_ln_g, conv_ln_b)
    y_lru = recurrent_mixer(z[..., LG0:LX0], z[..., LX0:IN_COLS], lru_conv_w, lru_conv_b,
                            lru_wa, lru_ba, lru_wx, lru_bx, lru_lambda)
    mix = jnp.concatenate([y_attn, y_conv, y_lru], axis=-1)
    x = x + jnp.einsum("bsc,cd->bsd", mix, w_out)
    h2 = rmsnorm(x, norm2_g)
    ff = jnp.square(jax.nn.relu(jnp.einsum("bsd,df->bsf", h2, w_up)))
    return x + jnp.einsum("bsf,fd->bsd", ff, w_down)

def first_inputs(seed: int = 0) -> dict:
    key = jax.random.key(seed)
    ks = jax.random.split(key, 20)
    n = jax.random.normal
    f32 = jnp.float32
    x = n(ks[0], (BATCH, SEQ, D_MODEL), f32)
    norm1_g = 1.0 + 0.02 * n(ks[1], (DEPTH, D_MODEL), f32)
    w_in = n(ks[2], (DEPTH, D_MODEL, IN_COLS), f32) * D_MODEL ** -0.5
    conv_dw_w = n(ks[3], (DEPTH, CONV_TAPS, CONV_WIDTH), f32) * CONV_TAPS ** -0.5
    conv_dw_b = 0.02 * n(ks[4], (DEPTH, CONV_WIDTH), f32)
    conv_ln_g = 1.0 + 0.02 * n(ks[5], (DEPTH, CONV_WIDTH), f32)
    conv_ln_b = 0.02 * n(ks[6], (DEPTH, CONV_WIDTH), f32)
    lru_conv_w = n(ks[7], (DEPTH, LRU_CONV_TAPS, LRU_WIDTH), f32) * LRU_CONV_TAPS ** -0.5
    lru_conv_b = 0.02 * n(ks[8], (DEPTH, LRU_WIDTH), f32)
    blk = LRU_WIDTH // LRU_HEADS
    lru_wa = n(ks[9], (DEPTH, LRU_HEADS, blk, blk), f32) * blk ** -0.5
    lru_ba = 0.02 * n(ks[10], (DEPTH, LRU_WIDTH), f32)
    lru_wx = n(ks[11], (DEPTH, LRU_HEADS, blk, blk), f32) * blk ** -0.5
    lru_bx = 0.02 * n(ks[12], (DEPTH, LRU_WIDTH), f32)
    a_c = jax.random.uniform(ks[13], (DEPTH, LRU_WIDTH), f32, 0.9, 0.999)
    a0 = a_c ** (1.0 / LRU_C)
    lru_lambda = jnp.log(a0) - jnp.log1p(-a0)
    w_out = n(ks[14], (DEPTH, MIX_WIDTH, D_MODEL), f32) * MIX_WIDTH ** -0.5
    norm2_g = 1.0 + 0.02 * n(ks[15], (DEPTH, D_MODEL), f32)
    w_up = n(ks[16], (DEPTH, D_MODEL, D_FF), f32) * D_MODEL ** -0.5
    w_down = n(ks[17], (DEPTH, D_FF, D_MODEL), f32) * D_FF ** -0.5
    final_g = 1.0 + 0.02 * n(ks[18], (D_MODEL,), f32)
    return {"x": x, "norm1_g": norm1_g, "w_in": w_in, "conv_dw_w": conv_dw_w, "conv_dw_b": conv_dw_b,
            "conv_ln_g": conv_ln_g, "conv_ln_b": conv_ln_b, "lru_conv_w": lru_conv_w, "lru_conv_b": lru_conv_b,
            "lru_wa": lru_wa, "lru_ba": lru_ba, "lru_wx": lru_wx, "lru_bx": lru_bx, "lru_lambda": lru_lambda,
            "w_out": w_out, "norm2_g": norm2_g, "w_up": w_up, "w_down": w_down, "final_g": final_g}

def first_block(x, norm1_g, w_in, conv_dw_w, conv_dw_b, conv_ln_g, conv_ln_b, lru_conv_w, lru_conv_b,
              lru_wa, lru_ba, lru_wx, lru_bx, lru_lambda, w_out, norm2_g, w_up, w_down, final_g):
    for l in range(DEPTH):
        x = hybrid_layer(x, norm1_g[l], w_in[l], conv_dw_w[l], conv_dw_b[l], conv_ln_g[l], conv_ln_b[l],
                         lru_conv_w[l], lru_conv_b[l], lru_wa[l], lru_ba[l], lru_wx[l], lru_bx[l], lru_lambda[l],
                         w_out[l], norm2_g[l], w_up[l], w_down[l])
    return rmsnorm(x, final_g)


DEPTH_2 = 2

N_META = 16
POOL_WIDTH = D_MODEL // 2
POOL_WINDOWS = (2, 4, 8, 16)
POOL_GROUPS = len(POOL_WINDOWS)
POOL_GROUP_DIM = POOL_WIDTH // POOL_GROUPS
N_HEADS = 8
QK_NOPE_DIM = 64
QK_ROPE_DIM = 32
QK_HEAD_DIM = QK_NOPE_DIM + QK_ROPE_DIM
V_HEAD_DIM = 64
MLA_WIDTH = N_HEADS * V_HEAD_DIM
KV_LORA_RANK = 256
Q_LORA_RANK = 768
ROPE_THETA = 10000.0
NORM_EPS = 1e-6
Q_BLOCK = 128
MASK_VALUE = -1e30

IN_SPLITS = (POOL_WIDTH, POOL_WIDTH, Q_LORA_RANK, KV_LORA_RANK, QK_ROPE_DIM, MLA_WIDTH, D_MODEL, D_MODEL)
D_IN = sum(IN_SPLITS)
IN_SPLIT_POINTS = tuple(int(v) for v in np.cumsum(IN_SPLITS)[:-1])


def rmsnorm_2(x, gain):
    xf = x.astype(jnp.float32)
    inv = lax.rsqrt(jnp.mean(xf * xf, axis=-1, keepdims=True) + NORM_EPS)
    return (xf * inv * gain.astype(jnp.float32)).astype(x.dtype)

def apply_rope(x, pos):
    half = x.shape[-1] // 2
    inv_freq = ROPE_THETA ** (-jnp.arange(half, dtype=jnp.float32) / half)
    ang = pos.astype(jnp.float32)[..., None] * inv_freq
    cos = jnp.cos(ang)[:, :, None, :]
    sin = jnp.sin(ang)[:, :, None, :]
    xf = x.astype(jnp.float32)
    x1, x2 = xf[..., :half], xf[..., half:]
    return jnp.concatenate([x1 * cos - x2 * sin, x2 * cos + x1 * sin], axis=-1).astype(x.dtype)

def pool_mix(u, w_group, scale):
    B, L, _ = u.shape
    ug = u.reshape(B, L, POOL_GROUPS, POOL_GROUP_DIM).astype(jnp.float32)
    csum = jnp.cumsum(ug, axis=1)
    t1 = jnp.arange(1, L + 1, dtype=jnp.float32)
    means = []
    for g, w in enumerate(POOL_WINDOWS):
        s = csum[:, :, g]
        lag = jnp.pad(s, ((0, 0), (w, 0), (0, 0)))[:, :L]
        cnt = jnp.minimum(t1, float(w))[None, :, None]
        means.append((s - lag) / cnt)
    mixed = (jnp.stack(means, axis=2) - ug).astype(u.dtype)
    y = jnp.einsum('blgc,gcd->blgd', mixed, w_group)
    return y.reshape(B, L, POOL_WIDTH) * scale

def causal_block_attention(q, k, v):
    B, L = q.shape[0], q.shape[1]
    pad_front = (-N_META) % Q_BLOCK
    pad_back = (-(L + pad_front)) % Q_BLOCK
    padw = ((0, 0), (pad_front, pad_back), (0, 0), (0, 0))
    q, k, v = jnp.pad(q, padw), jnp.pad(k, padw), jnp.pad(v, padw)
    n_blocks = q.shape[1] // Q_BLOCK
    scale = 1.0 / math.sqrt(QK_HEAD_DIM)
    outs = []
    for i in range(n_blocks):
        q0 = i * Q_BLOCK
        kend = q0 + Q_BLOCK
        s = jnp.einsum('bqhd,bkhd->bhqk', q[:, q0:kend], k[:, :kend]).astype(jnp.float32) * scale
        qi = jnp.arange(q0, kend)[:, None]
        ki = jnp.arange(kend)[None, :]
        valid = (ki <= qi) & (ki >= pad_front)
        s = jnp.where(valid, s, MASK_VALUE)
        p = jax.nn.softmax(s, axis=-1).astype(v.dtype)
        outs.append(jnp.einsum('bhqk,bkhd->bqhd', p, v[:, :kend]))
    o = jnp.concatenate(outs, axis=1)
    return o[:, pad_front:pad_front + L]

def mla(c_q_raw, c_kv_raw, k_rope_raw, pos, g_qa, g_kva, w_q_b, w_kv_b, g_qn, g_kn):
    B, L, _ = c_q_raw.shape
    c_q = rmsnorm_2(c_q_raw, g_qa)
    c_kv = rmsnorm_2(c_kv_raw, g_kva)
    q = (c_q @ w_q_b).reshape(B, L, N_HEADS, QK_HEAD_DIM)
    kv = (c_kv @ w_kv_b).reshape(B, L, N_HEADS, QK_NOPE_DIM + V_HEAD_DIM)
    k_nope, v = kv[..., :QK_NOPE_DIM], kv[..., QK_NOPE_DIM:]
    k_pe = jnp.broadcast_to(k_rope_raw[:, :, None, :], (B, L, N_HEADS, QK_ROPE_DIM))
    k = jnp.concatenate([k_nope, k_pe], axis=-1)
    q = rmsnorm_2(q, g_qn)
    k = rmsnorm_2(k, g_kn)
    q = jnp.concatenate([q[..., :QK_NOPE_DIM], apply_rope(q[..., QK_NOPE_DIM:], pos)], axis=-1)
    k = jnp.concatenate([k[..., :QK_NOPE_DIM], apply_rope(k[..., QK_NOPE_DIM:], pos)], axis=-1)
    o = causal_block_attention(q, k, v)
    return o.reshape(B, L, MLA_WIDTH)

def second_inputs(seed: int = 0) -> dict:
    key = jax.random.key(seed)
    ks = jax.random.split(key, 18)
    f32 = jnp.float32

    def nrm(k, shape, scale):
        return jax.random.normal(k, shape, f32) * scale

    def gain(k, shape):
        return 1.0 + 0.02 * jax.random.normal(k, shape, f32)

    x = jax.random.normal(ks[0], (BATCH, SEQ, D_MODEL), f32)
    offset = jax.random.randint(ks[1], (BATCH, 1), 0, 4096, dtype=jnp.int32)
    positions = offset + jnp.arange(SEQ, dtype=jnp.int32)[None, :]
    return {
        "x": x,
        "positions": positions,
        "meta_tokens": nrm(ks[2], (N_META, D_MODEL), 1.0),
        "norm_gain": gain(ks[3], (DEPTH_2, D_MODEL)),
        "w_in": nrm(ks[4], (DEPTH_2, D_MODEL, D_IN), D_MODEL ** -0.5),
        "pool_w_group": nrm(ks[5], (DEPTH_2, POOL_GROUPS, POOL_GROUP_DIM, POOL_GROUP_DIM), POOL_GROUP_DIM ** -0.5),
        "pool_scale": gain(ks[6], (DEPTH_2, POOL_WIDTH)),
        "pool_w_up": nrm(ks[7], (DEPTH_2, POOL_WIDTH, D_MODEL), POOL_WIDTH ** -0.5),
        "q_a_norm_gain": gain(ks[8], (DEPTH_2, Q_LORA_RANK)),
        "kv_a_norm_gain": gain(ks[9], (DEPTH_2, KV_LORA_RANK)),
        "w_q_b": nrm(ks[10], (DEPTH_2, Q_LORA_RANK, N_HEADS * QK_HEAD_DIM), Q_LORA_RANK ** -0.5),
        "w_kv_b": nrm(ks[11], (DEPTH_2, KV_LORA_RANK, N_HEADS * (QK_NOPE_DIM + V_HEAD_DIM)), KV_LORA_RANK ** -0.5),
        "q_norm_gain": gain(ks[12], (DEPTH_2, QK_HEAD_DIM)),
        "k_norm_gain": gain(ks[13], (DEPTH_2, QK_HEAD_DIM)),
        "mla_w_up": nrm(ks[14], (DEPTH_2, MLA_WIDTH, D_MODEL), MLA_WIDTH ** -0.5),
        "w_out": nrm(ks[15], (DEPTH_2, D_MODEL, D_MODEL), (D_MODEL * 2 * DEPTH_2) ** -0.5),
    }

def second_block(x, positions, meta_tokens, norm_gain, w_in, pool_w_group, pool_scale, pool_w_up,
              q_a_norm_gain, kv_a_norm_gain, w_q_b, w_kv_b, q_norm_gain, k_norm_gain, mla_w_up, w_out):
    B = x.shape[0]
    meta = jnp.broadcast_to(meta_tokens[None].astype(x.dtype), (B, N_META, D_MODEL))
    h_res = jnp.concatenate([meta, x], axis=1)
    meta_pos = jnp.broadcast_to(jnp.arange(N_META, dtype=jnp.int32)[None], (B, N_META))
    pos = jnp.concatenate([meta_pos, positions + N_META], axis=1)

    for l in range(DEPTH_2):
        h = rmsnorm_2(h_res, norm_gain[l])
        proj = h @ w_in[l]
        u_pool, z_pool, c_q, c_kv, k_rope, z_mla, g_pool, g_mla = jnp.split(proj, IN_SPLIT_POINTS, axis=-1)
        y_pool = (pool_mix(u_pool, pool_w_group[l], pool_scale[l]) * jax.nn.silu(z_pool)) @ pool_w_up[l]
        o_mla = mla(c_q, c_kv, k_rope, pos, q_a_norm_gain[l], kv_a_norm_gain[l], w_q_b[l], w_kv_b[l],
                    q_norm_gain[l], k_norm_gain[l])
        y_mla = (o_mla * jax.nn.silu(z_mla)) @ mla_w_up[l]
        merged = jax.nn.sigmoid(g_pool) * y_pool + jax.nn.sigmoid(g_mla) * y_mla
        h_res = h_res + merged @ w_out[l]

    return h_res[:, N_META:]


def setup_inputs(seed=0):
    out = dict(first_inputs(seed))
    for name, value in second_inputs(seed + 1).items():
        if name != "x":
            out[name + "_2"] = value
    return out


def reference(
    x, norm1_g, w_in, conv_dw_w, conv_dw_b, conv_ln_g, conv_ln_b, lru_conv_w, lru_conv_b,
    lru_wa, lru_ba, lru_wx, lru_bx, lru_lambda, w_out, norm2_g, w_up, w_down, final_g,
    positions_2, meta_tokens_2, norm_gain_2, w_in_2, pool_w_group_2, pool_scale_2, pool_w_up_2,
    q_a_norm_gain_2, kv_a_norm_gain_2, w_q_b_2, w_kv_b_2, q_norm_gain_2, k_norm_gain_2,
    mla_w_up_2, w_out_2,
):
    x = first_block(
        x, norm1_g, w_in, conv_dw_w, conv_dw_b, conv_ln_g, conv_ln_b, lru_conv_w, lru_conv_b,
        lru_wa, lru_ba, lru_wx, lru_bx, lru_lambda, w_out, norm2_g, w_up, w_down, final_g,
    )
    return second_block(
        x, positions_2, meta_tokens_2, norm_gain_2, w_in_2, pool_w_group_2, pool_scale_2,
        pool_w_up_2, q_a_norm_gain_2, kv_a_norm_gain_2, w_q_b_2, w_kv_b_2, q_norm_gain_2,
        k_norm_gain_2, mla_w_up_2, w_out_2,
    )


_drawn_inputs = setup_inputs


def setup_inputs(seed=0):
    import zlib

    import numpy as np

    out = dict(_drawn_inputs(seed))
    spreads = {}
    factors = {'norm1_g': 5.015,
     'conv_dw_b': 4.877,
     'conv_ln_g': 7.251,
     'conv_ln_b': 8.0,
     'lru_ba': 8.0,
     'lru_bx': 8.0,
     'norm2_g': 3.235,
     'final_g': 2.85,
     'meta_tokens_2': 4.621,
     'norm_gain_2': 8.0,
     'pool_scale_2': 8.0,
     'q_a_norm_gain_2': 8.0,
     'kv_a_norm_gain_2': 8.0,
     'w_q_b_2': 2.707,
     'q_norm_gain_2': 8.0,
     'k_norm_gain_2': 8.0}
    for name, (base, spread) in spreads.items():
        noise = np.random.default_rng([zlib.crc32(name.encode()), seed]).standard_normal(out[name].shape)
        drawn = base * np.exp(spread * noise) if base else spread * noise
        out[name] = __import__('jax').numpy.asarray(drawn.astype(out[name].dtype))
    for name, factor in factors.items():
        out[name] = (out[name] * factor).astype(out[name].dtype)
    return out
```

```python
from contextlib import ExitStack

import numpy as np

import concourse.bass as bass
from concourse import mybir

F32 = mybir.dt.float32
F32R = mybir.dt.float32r
I32 = mybir.dt.int32
ALU = mybir.AluOpType
ACT = mybir.ActivationFunctionType
AX = mybir.AxisListType.X

P = 128
DM = 1024
KC = DM // P
T1 = 1024
META = 16
T2 = T1 + META
TP = 1044
TB = -(-TP // P)
LAYERS = 2
PIECES1 = (2, 512)
PIECES2 = (3, 348)
RW = 1064
NR = 18
NEG = -1e30

ATTN_HEADS, HD = 6, 64
PATTERNS = ((128, 1), (512, 4), (2048, 16))
CONV_TAPS, LRU_TAPS = 31, 4
DFF = 4096
FG = 4
GROUPS = DFF // P // FG

MH, NOPE, ROPE, VD = 8, 64, 32, 64
QKD = NOPE + ROPE
QR, KVR = 768, 256
POOLW = (2, 4, 8, 16)

UW = 1024

PARAM_COLS = {}


def _columns():
    at = 0
    for name, n in (("norm1", 8), ("cdw", 62), ("cdb", 2), ("clg", 2), ("clb", 2), ("lcw", 12), ("lcb", 3),
                    ("lba", 3), ("lbx", 3), ("lam", 3), ("norm2", 8), ("final", 8),
                    ("n2_0", 8), ("n2_1", 8), ("ps_0", 4), ("ps_1", 4), ("qa_0", 6), ("qa_1", 6),
                    ("kva_0", 2), ("kva_1", 2), ("qn_0", 1), ("qn_1", 1), ("kn_0", 1), ("kn_1", 1),
                    ("freq", 1)):
        PARAM_COLS[name] = at
        at += n
    return at


NPARAM = _columns()

CONST_COLS = dict(ident=0, ones=128, rot=256, causal=352, invcnt=480)
NCONST = 480 + 64 + 16


def shape_constants():
    c = np.zeros((P, NCONST), np.float32)
    c[:, 0:128] = np.eye(P)
    c[:, 128:256] = 1.0
    half = ROPE // 2
    for i in range(half):
        c[NOPE + half + i, 256 + NOPE + i] = -1.0
        c[NOPE + i, 256 + NOPE + half + i] = 1.0
    q, k = np.arange(P)[:, None], np.arange(P)[None, :]
    c[:, 352:480] = np.where(k <= q, 0.0, NEG)
    for g, w in enumerate(POOLW):
        c[:, 480 + 16 * g:480 + 16 * g + 16] = 1.0 / np.minimum(np.arange(16) + 1, w)
    c[:, 544:560] = np.arange(META)
    slopes = 2.0 ** (-8.0 * np.arange(1, ATTN_HEADS + 1) / ATTN_HEADS)
    band = np.full((P, ATTN_HEADS, 2 * P), NEG, np.float32)
    for h in range(ATTN_HEADS):
        g = h // 2
        d = PATTERNS[g][1]
        dist = q + P - np.arange(2 * P)[None, :]
        ok = (dist >= 0) & (dist <= P)
        if g == 2:
            own = np.arange(2 * P)[None, :] - P
            ok = (own >= 0) & (own <= q) & (own // 64 == q // 64)
        band[:, h] = np.where(ok, -np.float32(slopes[h]) * (d * dist).astype(np.float32), NEG)
    return c, band.reshape(P, -1)


class Count:

    def __init__(self, sem):
        self.sem, self.n, self.reg, self.per = sem, 0, None, 0

    def step(self, k=1):
        self.n += k

    def value(self, back=0):
        n = self.n - back
        return n if self.reg is None else self.reg * self.per + n

    def wait(self, eng, back=0):
        if self.reg is None and self.n - back <= 0:
            return
        eng.wait_ge(self.sem, self.value(back))


class Loop:

    def __init__(self, reg, times, counts):
        self.times, self.counts = times, counts
        for c, per in counts:
            c.reg, c.per, c.start = reg, per, c.n

    def end(self):
        for c, per in self.counts:
            assert c.n - c.start == per, (c.sem, c.n - c.start, per)
            c.reg, c.n = None, c.start + per * self.times


UNITS_Z = 19
N_UNITS1 = UNITS_Z + KC + GROUPS * (FG + 4)
N_UNITS2 = 4 + 4 + 1 + 12 + 6 + 2 + 1 + 4 + 8 + 8 + 4 + 8
N_UNITS = N_UNITS1 + LAYERS * N_UNITS2


def build(nc, xT, metaT, pos, params, consts, bands, lru_w, wstream, outT):
    with ExitStack() as ctx:
        def sem(name):
            return ctx.enter_context(nc.semaphore(name))

        start = -(-nc.sbuf_base // 64) * 64
        at = [start]

        def place(name, cols, dt=F32, offset=None):
            if offset is None:
                offset = at[0] = -(-at[0] // 32) * 32
                at[0] += 4 * cols
            return nc.alloc_sbuf_tensor_at(name, [P, cols], dt, offset=offset), offset

        def chunks(t, n, w):
            return t[:].rearrange("p (c t) -> p c t", c=n)

        X_, _ = place("residual", KC * TP)
        Ah_, _ = place("act_hi", KC * TP, F32R)
        Al_, _ = place("act_lo", KC * TP, F32R)
        Wraw_, _ = place("w_raw", 2 * UW)
        Wh_, _ = place("w_hi", 2 * UW, F32R)
        Wl_, _ = place("w_lo", 2 * UW, F32R)
        C_, _ = place("shape_consts", NCONST)
        V_, _ = place("params", NPARAM)
        S_, _ = place("small", 64)
        R_, r_at = place("work", NR * RW)
        F_, _ = place("ff_split", 8 * RW, F32R, offset=r_at)
        G_, _ = place("pool_split", 8 * RW, F32R, offset=r_at + 4 * 8 * RW)
        assert at[0] <= nc.sbuf_usable_end, (at[0], nc.sbuf_usable_end)
        X, Ah, Al = chunks(X_, KC, TP), chunks(Ah_, KC, TP), chunks(Al_, KC, TP)
        Wraw, Wh, Wl = chunks(Wraw_, 2, UW), chunks(Wh_, 2, UW), chunks(Wl_, 2, UW)
        R, F, G = chunks(R_, NR, RW), chunks(F_, 8, RW), chunks(G_, 8, RW)
        ident, ones = C_[:, 0:128], C_[:, 128:256]
        rot = C_[:, 256:256 + QKD]
        causal = C_[:, 352:480]

        def param(name, i=0, rows=slice(0, P)):
            c = PARAM_COLS[name] + i
            return V_[rows, c:c + 1]

        acc = ctx.enter_context(nc.psum_tensor("acc", [P, 2, 3, 512], F32))
        aux = ctx.enter_context(nc.psum_tensor("aux", [P, 2, 512], F32))

        spill_x = nc.dram_tensor("spill_x", (P, KC * TP), F32, kind="Internal").ap()
        spill_m = nc.dram_tensor("spill_m", (P, KC * TP), F32, kind="Internal").ap()
        spill_g = nc.dram_tensor("spill_g", (P, KC * TP), F32, kind="Internal").ap()

        sems = {}
        for name in (
            "consts_in", "x_in", "meta_in", "lru_in", "bands_in", "xre_in",
            "w_in0", "w_in1", "w_hi_done", "w_lo_done", "unit_done",
            "ready0", "ready1", "free0", "free1",
            "aux_ready0", "aux_ready1", "aux_free0", "aux_free1",
            "a_ready",
            "f_ready",
            "sq_ready", "sq_free", "rs_ready", "x_ready",
            "dve_step", "act_step",
            "to_dve", "to_act", "to_pe",
            "act_to_pe", "pe_read",
            "spilled", "m_spilled", "g_spilled", "mg_in", "sg_in", "stored", "pos_in",
        ):
            sems[name] = sem(name)
        block = ctx.enter_context(nc.Block())

        def counts():
            return {k: Count(v) for k, v in sems.items()}

        def acc_view(s, pieces, rows=slice(0, P)):
            n, w = pieces
            return acc[rows, s, 0:n, 0:w]

        def cut(ap, pieces):
            n, w = pieces
            return ap[:, 0:n * w].rearrange("p (a b) -> p a b", a=n)

        z_order = ["gate0", "gate1", "a0", "a1", "lx0", "lx1", "lx2", "lg0", "lg1", "lg2"] + \
            [f"{m}{g}" for g in range(3) for m in "qkv"]

        @block.sync
        def _(sp):
            c = counts()
            sp.dma_start(C_[:], consts).then_inc(sems["consts_in"], 16)
            sp.dma_start(V_[:], params).then_inc(sems["consts_in"], 16)
            w_in = (sems["w_in0"], sems["w_in1"])

            def load(n, s):
                sp.dma_start(Wraw[:, s, :], wstream[n, :, :] if isinstance(n, int) else
                             wstream[bass.ds(n, 1), :, :].rearrange("o p f -> (o p) f")).then_inc(w_in[s], 16)

            load(0, 0)
            load(1, 1)
            with sp.Fori(1, N_UNITS // 2) as i:
                for s in range(2):
                    sp.wait_ge(sems["w_lo_done"], i * 2 + (s - 1))
                    load(i * 2 + s, s)
            if N_UNITS % 2:
                sp.wait_ge(sems["w_lo_done"], N_UNITS - 2)
                load(N_UNITS - 1, 0)

        @block.gpsimd
        def _(pool):
            w_in = (sems["w_in0"], sems["w_in1"])

            def split(n, s, landed):
                pool.wait_ge(w_in[s], landed)
                if not isinstance(n, int) or n >= 2:
                    pool.wait_ge(sems["unit_done"], n - 1)
                nc.gpsimd.tensor_copy(Wh[:, s, :], Wraw[:, s, :]).then_inc(sems["w_hi_done"], 1)
                pool.wait_ge(sems["w_hi_done"], n + 1)
                nc.gpsimd.tensor_tensor(Wl[:, s, :], Wraw[:, s, :], Wh[:, s, :].bitcast(F32),
                                        ALU.subtract).then_inc(sems["w_lo_done"], 1)

            pool.wait_ge(sems["consts_in"], 32)
            split(0, 0, 16)
            split(1, 1, 16)
            with pool.Fori(1, N_UNITS // 2) as i:
                for s in range(2):
                    pool.wait_ge(w_in[s], i * 16 + 16)
                    pool.wait_ge(sems["unit_done"], i * 2 + (s - 1))
                    nc.gpsimd.tensor_tensor(S_[:, 62:63], C_[:, 128:129], C_[:, 128:129], ALU.add)
                    nc.gpsimd.tensor_copy(Wh[:, s, :], Wraw[:, s, :]).then_inc(sems["w_hi_done"], 1)
                    pool.wait_ge(sems["w_hi_done"], i * 2 + (s + 1))
                    nc.gpsimd.tensor_tensor(Wl[:, s, :], Wraw[:, s, :], Wh[:, s, :].bitcast(F32),
                                            ALU.subtract).then_inc(sems["w_lo_done"], 1)
            if N_UNITS % 2:
                split(N_UNITS - 1, 0, 16 * (N_UNITS // 2 + 1))

        @block.tensor
        def _(pe):
            c = counts()
            free = (c["free0"], c["free1"])
            ready = (sems["ready0"], sems["ready1"])
            aux_free = (c["aux_free0"], c["aux_free1"])
            aux_ready = (sems["aux_ready0"], sems["aux_ready1"])
            unit = Count(sems["w_lo_done"])

            def take(s):
                free[s].wait(pe)
                free[s].step()

            def take_aux(s):
                aux_free[s].wait(pe)
                aux_free[s].step()

            def matrix(s, ws, w0, ks, m, hi, lo, pieces, arrive=None, last=None):
                n, w = pieces
                take(s)
                for j, k in enumerate(ks):
                    if arrive is not None:
                        pe.wait_ge(arrive[0], arrive[1] + j + 1)
                    for t, (wt, x) in enumerate(((Wh, hi), (Wh, lo), (Wl, hi))):
                        for p in range(n):
                            ins = nc.tensor.matmul(
                                acc[0:m, s, p, 0:w], wt[:, ws, w0 + j * m:w0 + j * m + m],
                                x[:, k, p * w:p * w + w],
                                start=(j == 0 and t == 0), stop=(j == len(ks) - 1 and t == 2))
                ins.then_inc(last if last is not None else ready[s], 1)

            def next_unit():
                unit.step()
                unit.wait(pe)

            def wide(s, ws, pieces, arrive=None, ks=range(KC), m=P):
                next_unit()
                matrix(s, ws, 0, ks, m, Ah, Al, pieces, arrive, sems["unit_done"])

            def narrow_pair(ws, lo_hi, pieces, arrive=None):
                next_unit()
                for s in range(2):
                    matrix(s, ws, s * 512, range(4), P, lo_hi, lo_hi_lo(lo_hi), pieces,
                           arrive, None if s == 0 else sems["unit_done"])

            def lo_hi_lo(t):
                return t[:, 4:8, :]

            def norm_sum(s, n, pieces, rows=P, slots=None):
                take(s)
                np_, w = pieces
                for j in range(n):
                    c["sq_ready"].step()
                    c["sq_ready"].wait(pe)
                    for p in range(np_):
                        ins = nc.tensor.matmul(acc[:, s, p, 0:w], ones, slots[j % 2][:, p * w:p * w + w],
                                               start=(j == 0), stop=(j == n - 1))
                    if j < n - 1:
                        ins.then_inc(sems["sq_free"], 1)
                ins.then_inc(ready[s], 1)

            pe.wait_ge(sems["consts_in"], 32)
            a0 = 0
            norm_sum(0, KC, PIECES1, slots=(R[:, 8, :], R[:, 9, :]))
            for s in range(2):
                wide(s, s, PIECES1, (sems["a_ready"], a0) if s == 0 else None)
            with pe.Fori(0, UNITS_Z // 2 - 1) as i:
                loop = Loop(i, UNITS_Z // 2 - 1, [(unit, 2), (free[0], 1), (free[1], 1)])
                for s in range(2):
                    wide(s, s, PIECES1)
                loop.end()
            wide(0, 0, PIECES1)
            pe.wait_ge(sems["lru_in"], 16)
            for j in range(3):
                c["to_pe"].step()
                c["to_pe"].wait(pe)
                for s, col in ((1, 0), (0, 384)):
                    take(s)
                    for p in range(2):
                        ins = nc.tensor.matmul(acc[:, s, p, :], R[:, 17, col + 128 * j:col + 128 * j + 128],
                                               X[:, 4 + j, p * 512:p * 512 + 512], start=True, stop=True)
                    ins.then_inc(ready[s], 1)
            for rnd in range(2):
                c["to_pe"].step()
                c["to_pe"].wait(pe)
                take(rnd)
                for j in range(2):
                    src = X[:, 2 + j, :] if rnd == 0 else R[:, 2 + j, :]
                    for p in range(2):
                        ins = nc.tensor.matmul(acc[:, rnd, p, :], ones, src[:, p * 512:p * 512 + 512],
                                               start=(j == 0), stop=(j == 1))
                ins.then_inc(ready[rnd], 1)
            PT, Vt = X[:, 3, :], X[:, 0, :]
            DG = X[:, 5, :]

            def scores(g, j, b):
                rows = slice(64 * j, 64 * j + 64)
                take(b)
                q, k = R[:, 8 + 3 * g, :], R[:, 9 + 3 * g, :]
                for i in range(4):
                    t = 4 * b + i
                    bank = acc[:, b, i // 2, 256 * (i % 2):256 * (i % 2) + 256]
                    has = (t > 0) if g == 0 else (t % 2 == 1)
                    if g < 2:
                        kt = t - 1 if has else t
                        nc.tensor.matmul(bank[:, 0:128], q[rows, 128 * t:128 * t + 128],
                                         k[rows, 128 * kt:128 * kt + 128], start=True, stop=True)
                    ins = nc.tensor.matmul(bank[:, 128:256], q[rows, 128 * t:128 * t + 128],
                                           k[rows, 128 * t:128 * t + 128], start=True, stop=True)
                ins.then_inc(ready[b], 1)

            for g in range(3):
                for half in range(2):
                    take_aux(half)
                    for i in range(4):
                        t = 4 * half + i
                        ins = nc.tensor.transpose(aux[:, half, 128 * i:128 * i + 128],
                                                  R[:, 10 + 3 * g, 128 * t:128 * t + 128], ident)
                    ins.then_inc(aux_ready[half], 1)
                for j in range(2):
                    for b in range(2):
                        scores(g, j, b)
                    for b in range(2):
                        c["to_pe"].step()
                        c["to_pe"].wait(pe)
                        parts = (0, 1) if g < 2 else (1,)
                        for part in parts:
                            take_aux(part)
                            for i in range(4):
                                ins = nc.tensor.transpose(
                                    aux[:, part, 128 * i:128 * i + 128],
                                    X[:, 1 + b, 256 * i + 128 * part:256 * i + 128 * part + 128], ident)
                            ins.then_inc(aux_ready[part], 1)
                        for part in range(2):
                            aux_free[part].wait(pe)
                        take(b)
                        for i in range(4):
                            t = 4 * b + i
                            has = g < 2
                            kt = (t - 1 if ((t > 0) if g == 0 else (t % 2 == 1)) else t)
                            out = acc[64 * j:64 * j + 64, b, 2, 128 * i:128 * i + 128]
                            if has:
                                nc.tensor.matmul(out, Vt[:, 128 * kt + 64 * j:128 * kt + 64 * j + 64],
                                                 PT[:, 128 * i:128 * i + 128], start=True, stop=False)
                            ins = nc.tensor.matmul(out, Vt[:, 128 * t + 64 * j:128 * t + 64 * j + 64],
                                                   PT[:, 512 + 128 * i:512 + 128 * i + 128],
                                                   start=not has, stop=True)
                        ins.then_inc(ready[b], 1)
                        c["to_pe"].step()
                        c["to_pe"].wait(pe)
                        take_aux(0)
                        nc.tensor.matmul(aux[64 * j:64 * j + 64, 0, :], ones[:, 0:64], DG[:, 0:512],
                                         start=True, stop=True).then_inc(aux_ready[0], 1)
            for j in range(KC):
                wide((j + 1) % 2, (j + 1) % 2, PIECES1, (sems["a_ready"], 8) if j == 0 else None)
            norm_sum(1, KC, PIECES1, slots=(R[:, 8, :], R[:, 9, :]))
            with pe.Fori(0, GROUPS) as i:
                loop = Loop(i, GROUPS, [(unit, FG + 4), (free[0], FG // 2 + 4), (free[1], FG // 2 + 4),
                                        (c["f_ready"], FG)])
                for j in range(FG):
                    wide((j + 1) % 2, (j + 1) % 2, PIECES1, (sems["a_ready"], 16) if j == 0 else None)
                for j in range(4):
                    next_unit()
                    ws = (j + 1) % 2
                    for s in range(2):
                        if j == 0 and s == 0:
                            c["f_ready"].step(FG)
                            c["f_ready"].wait(pe)
                        matrix(s, ws, s * 512, range(4), P, F, F[:, 4:8, :], PIECES1, None,
                               None if s == 0 else sems["unit_done"])
                loop.end()
            norm_sum(0, KC, PIECES1, slots=(R[:, 8, :], R[:, 9, :]))
            a_count = 24
            ws0 = N_UNITS1 % 2
            for l in range(LAYERS):
                u = [ws0]

                def ws():
                    u[0] ^= 1
                    return u[0] ^ 1

                norm_sum(0, KC, PIECES2, slots=(R[:, 8, :], R[:, 9, :]))
                for j in range(8):
                    wide(j % 2, ws(), PIECES2, (sems["a_ready"], a_count) if j == 0 else None)
                a_count += 8
                next_unit()
                w = ws()
                for j in range(4):
                    c["f_ready"].step()
                    c["f_ready"].wait(pe)
                    matrix(j % 2, w, j * 128, [j], P, G, G[:, 4:8, :], PIECES2, None,
                           None if j < 3 else sems["unit_done"])
                for j in range(4):
                    wide(0, ws(), PIECES2)
                    wide(1, ws(), PIECES2)
                    if j == 0:
                        c["f_ready"].step(4)
                        c["f_ready"].wait(pe)
                    next_unit()
                    w = ws()
                    for s in range(2):
                        matrix(s, w, s * 512, range(4), P, G, G[:, 4:8, :], PIECES2, None,
                               None if s == 0 else sems["unit_done"])
                for j in range(8):
                    wide(j % 2, ws(), PIECES2)
                wide(0, ws(), PIECES2, m=QKD)
                for j in range(4):
                    wide(1 - j % 2, ws(), PIECES2)
                norm_sum(1, 6, PIECES2, slots=(R[:, 6, :], R[:, 7, :]))
                norm_sum(0, 2, PIECES2, slots=(R[:, 6, :], R[:, 7, :]))
                c["act_to_pe"].step()
                c["act_to_pe"].wait(pe)
                take(1)
                for p in range(3):
                    ins = nc.tensor.matmul(acc[0:QKD, 1, p, 0:348], rot[NOPE:QKD, :],
                                           X[NOPE:QKD, 7, p * 348:p * 348 + 348], start=True, stop=True)
                ins.then_inc(ready[1], 1)
                for j in range(8):
                    wide(j % 2, ws(), PIECES2)
                for h in range(MH):
                    w = ws()
                    next_unit()
                    matrix(0, w, 0, range(6), QKD, Ah, Al, PIECES2,
                           (sems["a_ready"], a_count) if h == 0 else None)
                    matrix(1, w, 6 * QKD, (6, 7), P, Ah, Al, PIECES2,
                           (sems["a_ready"], a_count + 6) if h == 0 else None, sems["unit_done"])
                    for s, slot in ((0, 9), (1, 15)):
                        take(s)
                        for p in range(3):
                            ins = nc.tensor.matmul(acc[0:QKD, s, p, 0:348], ones[0:QKD, 0:QKD],
                                                   R[0:QKD, slot, p * 348:p * 348 + 348], start=True, stop=True)
                        ins.then_inc(ready[s], 1)
                    take(0)
                    for p in range(3):
                        ins = nc.tensor.matmul(acc[0:QKD, 0, p, 0:348], rot[0:QKD, :],
                                               R[0:QKD, 8, p * 348:p * 348 + 348], start=True, stop=True)
                    ins.then_inc(ready[0], 1)
                    for half in range(2):
                        take_aux(half)
                        for t in (range(8) if half == 0 else (8,)):
                            n = min(P, TP - P * t)
                            ins = nc.tensor.transpose(aux[0:n, half, 64 * (t % 8):64 * (t % 8) + 64],
                                                      R[64:128, 13, P * t:P * t + n], ident[64:128, 64:128])
                        ins.then_inc(aux_ready[half], 1)
                    c["to_pe"].step()
                    c["to_pe"].wait(pe)
                    q, k, v = R[:, 10, :], R[:, 11, :], R[:, 12, :]
                    half_aux = 0

                    def mla_scores(i):
                        s = i % 2
                        nq, nk = min(P, TP - P * i), min(P * (i + 1), TP)
                        take(s)
                        for p in range(-(-nk // 512)):
                            n = min(512, nk - 512 * p)
                            ins = nc.tensor.matmul(acc[0:nq, s, p, 0:n], q[0:QKD, P * i:P * i + nq],
                                                   k[0:QKD, 512 * p:512 * p + n], start=True, stop=True)
                        ins.then_inc(ready[s], 1)

                    mla_scores(0)
                    for i in range(TB):
                        if i + 1 < TB:
                            mla_scores(i + 1)
                        s = i % 2
                        nq, nk = min(P, TP - P * i), min(P * (i + 1), TP)
                        c["to_pe"].step()
                        c["to_pe"].wait(pe)
                        pr = R[:, 4 + s, :]
                        out = acc[64 * (h % 2):64 * (h % 2) + 64, s, 2, 128:128 + nq]
                        batches = [range(b, min(b + 4, i + 1)) for b in range(0, i + 1, 4)]
                        copied = []
                        for b, tiles in enumerate(batches):
                            take_aux(b % 2)
                            for t in tiles:
                                n = min(P, TP - P * t)
                                ins = nc.tensor.transpose(aux[0:n, b % 2, P * (t % 4):P * (t % 4) + nq],
                                                          pr[0:nq, P * t:P * t + n], ident[0:nq, 0:nq])
                            ins.then_inc(aux_ready[b % 2], 1)
                            copied.append(aux_free[b % 2].value())
                        for b, tiles in enumerate(batches):
                            pe.wait_ge(sems[f"aux_free{b % 2}"], copied[b])
                            if b == 0:
                                take(s)
                            for t in tiles:
                                n = min(P, TP - P * t)
                                ins = nc.tensor.matmul(out, v[0:n, 64 * t:64 * t + 64],
                                                       R[0:n, 6 + b % 2, P * (t % 4):P * (t % 4) + nq],
                                                       start=(t == 0), stop=(t == i))
                            ins.then_inc(ready[s] if b == len(batches) - 1 else sems["pe_read"], 1)
                a_count += 8
                for j in range(4):
                    next_unit()
                    w = ws()
                    for s in range(2):
                        if j == 0 and s == 0:
                            c["f_ready"].step(4)
                            c["f_ready"].wait(pe)
                        matrix(s, w, s * 512, range(4), P, G, G[:, 4:8, :], PIECES2, None,
                               None if s == 0 else sems["unit_done"])
                for j in range(KC):
                    wide(j % 2, ws(), PIECES2, (sems["a_ready"], a_count) if j == 0 else None)
                a_count += 8
                ws0 = u[0]

        @block.scalar
        def _(act):
            c = counts()
            free = (c["free0"], c["free1"])
            ready = (c["ready0"], c["ready1"])
            aux_free = (c["aux_free0"], c["aux_free1"])
            aux_ready = (c["aux_ready0"], c["aux_ready1"])
            unit = c["unit_done"]

            def do(ins, name="act_step"):
                ins.then_inc(sems[name], 1)
                c[name].step()

            def after(name="act_step"):
                c[name].wait(act)

            def await_unit(s):
                unit.step()
                unit.wait(act)

            def await_ready(s):
                ready[s].step()
                ready[s].wait(act)

            def release(ins, s):
                do(ins, f"free{s}")

            def copy(out, in_, scale=1.0):
                return nc.scalar.activation(out, in_, ACT.Copy, scale=scale)

            def norm_stats(src, n, width, pieces, s, slots, rs, dim, eps, arrive):
                for j in range(n):
                    arrive(j)
                    if j >= 2:
                        c["sq_free"].step()
                        c["sq_free"].wait(act)
                    do(nc.scalar.activation(slots[j % 2][:, 0:width], src(j), ACT.Square), "sq_ready")
                c["sq_free"].step(1 if n >= 2 else 0)
                await_ready(s)
                release(nc.scalar.activation(cut(rs, pieces), acc_view(s, pieces), ACT.Ln,
                                             scale=1.0 / dim, bias=eps_col(eps, P)), s)
                after(f"free{s}")
                do(nc.scalar.activation(rs[:, 0:width], rs[:, 0:width], ACT.Exp, scale=-0.5), "rs_ready")

            def eps_col(eps, rows):
                col = 60 if eps == 1e-6 else 61
                return S_[0:rows, col:col + 1]

            act.dma_start(X[:, :, META:T2], xT.rearrange("(c p) t -> p c t", p=P)).then_inc(sems["x_in"], 16)
            act.dma_start(R[:, 17, 0:768], lru_w).then_inc(sems["lru_in"], 16)
            act.wait_ge(sems["consts_in"], 32)
            c["to_act"].step()
            c["to_act"].wait(act)
            do(nc.scalar.activation(S_[:, 6:9], V_[:, PARAM_COLS["lam"]:PARAM_COLS["lam"] + 3], ACT.Abs))
            after()
            do(nc.scalar.activation(S_[:, 6:9], S_[:, 6:9], ACT.Exp, scale=-1.0))
            after()
            do(nc.scalar.activation(S_[:, 6:9], S_[:, 6:9], ACT.Ln, bias=1.0), "to_dve")
            act.wait_ge(sems["x_in"], 16)
            norm_stats(lambda j: X[:, j, META:T2], KC, T1, PIECES1, 0, (R[:, 8, :], R[:, 9, :]), R[:, 10, :],
                       DM, 1e-6, lambda j: None)
            for n, what in enumerate(z_order):
                s = n % 2
                await_unit(s)
                if what.startswith("gate"):
                    release(nc.scalar.activation(cut(X[:, n, :], PIECES1), acc_view(s, PIECES1),
                                                 ACT.Sigmoid), s)
                elif what[0] == "a":
                    free[s].step()
                elif what.startswith("lx"):
                    j = int(what[2])
                    release(copy(cut(R[:, 2 + j, LRU_TAPS - 1:], PIECES1), acc_view(s, PIECES1)), s)
                elif what.startswith("lg"):
                    release(copy(cut(R[:, 5 + int(what[2]), :], PIECES1), acc_view(s, PIECES1)), s)
                else:
                    g = int(what[1])
                    d = PATTERNS[g][1]
                    slot = R[:, 8 + 3 * g + "qkv".index(what[0]), 0:T1]
                    if d == 1:
                        release(copy(cut(slot, PIECES1), acc_view(s, PIECES1)), s)
                    else:
                        u = 512 // d
                        to = slot.rearrange("p (r u) -> p u r", r=d)
                        for p in range(2):
                            ins = copy(to[:, u * p:u * p + u, :],
                                       acc[:, s, p, :].rearrange("p (u r) -> p u r", r=d))
                            if p == 0:
                                do(ins)
                        release(ins, s)
            for j in range(3):
                if j:
                    act.wait_ge(sems["a_ready"], 8 + j)
                await_ready(1)
                release(nc.scalar.activation(cut(X[:, 7, :], PIECES1), acc_view(1, PIECES1), ACT.Sigmoid,
                                             bias=param("lba", j)), 1)
                await_ready(0)
                release(nc.scalar.activation(cut(X[:, 0, :], PIECES1), acc_view(0, PIECES1), ACT.Sigmoid,
                                             bias=param("lbx", j)), 0)
                if j == 0:
                    c["to_act"].step()
                    c["to_act"].wait(act)
                do(nc.scalar.activation(R[:, 1, 0:T1], R[:, 5 + j, 0:T1], ACT.Gelu_apprx_tanh), "to_dve")
                c["to_act"].step()
                c["to_act"].wait(act)
                do(nc.scalar.activation(R[:, 0, 0:T1], X[:, 1, 0:T1], ACT.Exp, scale=-1.0))
                do(nc.scalar.activation(R[:, 2, 0:T1], X[:, 1, 0:T1], ACT.Tanh), "to_dve")
                c["to_act"].step()
                c["to_act"].wait(act)
                do(nc.scalar.activation(R[:, 3, 0:T1], R[:, 2, 0:T1], ACT.Sqrt), "to_dve")
            await_ready_only = ready[0]
            await_ready_only.step()
            free[0].step()
            await_ready(1)
            release(nc.scalar.activation(cut(R[:, 4, :], PIECES1), acc_view(1, PIECES1), ACT.Ln,
                                         scale=1.0 / 256, bias=eps_col(1e-5, P)), 1)
            after("free1")
            do(nc.scalar.activation(R[:, 4, 0:T1], R[:, 4, 0:T1], ACT.Exp, scale=-0.5), "rs_ready")
            for j in range(2):
                c["to_act"].step()
                c["to_act"].wait(act)
                do(nc.scalar.activation(R[:, 2 + j, 0:T1], X[:, 2 + j, 0:T1], ACT.Sigmoid), "to_dve")
            act.wait_ge(sems["a_ready"], 8 + 3)
            act.dma_start(X_[:, 6 * TP:6 * TP + 6 * 256], bands).then_inc(sems["bands_in"], 16)
            for g in range(3):
                for half in range(2):
                    aux_ready[half].step()
                    aux_ready[half].wait(act)
                    if half == 0 and g:
                        ready[1].wait(act)
                    do(copy(X[:, 0, 512 * half:512 * half + 512], aux[:, half, :]), f"aux_free{half}")
                for j in range(2):
                    for b in range(2):
                        ready[b].step()
                        free[b].step()

                    def exps(b):
                        c["to_act"].step()
                        c["to_act"].wait(act)
                        lo, hi = (0, 256) if g < 2 else (128, 256)
                        for i in range(4):
                            do(nc.scalar.activation(X[:, 1 + b, 256 * i + lo:256 * i + hi],
                                                    X[:, 1 + b, 256 * i + lo:256 * i + hi], ACT.Exp,
                                                    bias=S_[:, 16 + 4 * b + i:17 + 4 * b + i],
                                                    accum_out=S_[:, 24 + 4 * b + i:25 + 4 * b + i]))
                        after()
                        do(nc.scalar.activation(S_[:, 32 + 4 * b:36 + 4 * b], S_[:, 24 + 4 * b:28 + 4 * b],
                                                ACT.Ln), "to_dve")

                    exps(0)
                    exps(1)
                    for b in range(2):
                        if not (g == 0 and j == 0 and b == 0):
                            ready[1 - b].wait(act)
                        for part in ((0, 1) if g < 2 else (1,)):
                            aux_ready[part].step()
                            aux_ready[part].wait(act)
                            do(copy(X[:, 3, 512 * part:512 * part + 512], aux[:, part, :]), f"aux_free{part}")
                        await_ready(b)
                        rows = slice(64 * j, 64 * j + 64)
                        d = PATTERNS[g][1]
                        nat = R[rows, g, 0:T1]
                        src = acc[rows, b, 2, :]
                        if d == 1:
                            release(copy(nat[:, 512 * b:512 * b + 512], src), b)
                        else:
                            release(copy(nat.rearrange("p (u r) -> p r u", r=d)[:, b * d // 2:(b + 1) * d // 2, :],
                                         src.rearrange("p (r u) -> p r u", r=d // 2)), b)
                        aux_ready[0].step()
                        aux_free[0].step()
            c["to_act"].step()
            c["to_act"].wait(act)
            act.dma_start(X[:, :, META:T2], xT.rearrange("(c p) t -> p c t", p=P)).then_inc(sems["xre_in"], 16)
            for g in range(3):
                ins = nc.scalar.activation(R[:, 3 + g, 0:T1], R[:, 3 + g, 0:T1], ACT.Exp)
                do(ins, "to_dve" if g == 2 else "act_step")

            def updated(s):
                unit.step()
                free[s].step()
                free[s].wait(act)

            norm_stats(lambda j: X[:, j, META:T2], KC, T1, PIECES1, 1, (R[:, 8, :], R[:, 9, :]), R[:, 10, :],
                       DM, 1e-6, lambda j: updated((j + 1) % 2))
            act.dma_start(X[:, :, 0:META], metaT.rearrange("(c p) t -> p c t", p=P)).then_inc(sems["meta_in"], 16)
            act.wait_ge(sems["a_ready"], 24)
            act.dma_start(R[:, 8, META:T2].bitcast(I32), pos).then_inc(sems["pos_in"], 16)
            for slot in (17, 16):
                c["to_act"].step()
                c["to_act"].wait(act)
                do(nc.scalar.activation(R[:, slot, 0:TP], R[:, slot, 0:TP], ACT.Sin), "to_dve")
            with act.Fori(0, GROUPS) as i:
                loop = Loop(i, GROUPS, [(unit, FG + 4), (free[0], FG // 2 + 4), (free[1], FG // 2 + 4),
                                        (ready[0], 4)])
                for j in range(FG):
                    s = (j + 1) % 2
                    await_unit(s)
                    release(nc.scalar.activation(cut(R[:, 12 + j, :], PIECES1), acc_view(s, PIECES1),
                                                 ACT.Relu), s)
                unit.step(4)
                ready[0].step(4)
                free[0].step(4)
                free[1].step(4)
                loop.end()

            def both_free():
                for s in range(2):
                    free[s].wait(act)

            both_free()
            norm_stats(lambda j: X[:, j, META:T2], KC, T1, PIECES1, 0, (R[:, 8, :], R[:, 9, :]), R[:, 10, :],
                       DM, 1e-6, lambda j: None)

            def by_signal(j):
                c["to_act"].step()
                c["to_act"].wait(act)

            for l in range(LAYERS):
                last = l == LAYERS - 1
                if l == 0:
                    act.wait_ge(sems["meta_in"], 16)
                norm_stats(lambda j: X[:, j, :], KC, TP, PIECES2, 0, (R[:, 8, :], R[:, 9, :]), R[:, 10, :],
                           DM, 1e-6, by_signal if l == 0 else lambda j: updated(j % 2))
                act.dma_start(spill_x, X_[:]).then_inc(sems["spilled"], 16)
                for j in range(4):
                    await_unit(j % 2)
                    if j == 0:
                        by_signal(0)
                    release(copy(cut(R[:, j, 16:], PIECES2), acc_view(j % 2, PIECES2)), j % 2)
                for j in range(4):
                    await_unit(j % 2)
                    do(nc.scalar.activation(cut(R[:, 4 + j, :], PIECES2), acc_view(j % 2, PIECES2),
                                            ACT.Sigmoid), "to_dve")
                    free[j % 2].step()
                for j in range(4):
                    if j < 3:
                        ready[j % 2].step()
                    free[j % 2].step()
                unit.step()
                for j in range(4):
                    for s in range(2):
                        await_unit(s)
                        if j:
                            free[s].wait(act)
                        release(nc.scalar.activation(cut(R[:, s, :], PIECES2), acc_view(s, PIECES2),
                                                     ACT.Sigmoid), s)
                    unit.step()
                    ready[0].step()
                    for s in range(2):
                        free[s].step()
                for s in range(2):
                    free[s].wait(act)
                act.dma_start(spill_m, X_[:]).then_inc(sems["m_spilled"], 16)
                for j in range(8):
                    await_unit(j % 2)
                    release(copy(cut(R[:, 8 + j, :], PIECES2), acc_view(j % 2, PIECES2)), j % 2)
                await_unit(0)
                act.wait_ge(sems["m_spilled"], 16 * (l + 1))
                rr = slice(NOPE, QKD)
                do(nc.scalar.activation(cut(X[rr, 6, :], PIECES2), acc_view(0, PIECES2, rr), ACT.Square))
                do(copy(cut(X[rr, 7, :], PIECES2), acc_view(0, PIECES2, rr), param(f"kn_{l}", 0, rr)),
                   "act_to_pe")
                do(nc.scalar.activation(S_[:, 59:60], S_[:, 60:61], ACT.Copy), "free0")
                for j in range(4):
                    s = 1 - j % 2
                    await_unit(s)
                    do(nc.scalar.activation(cut(X[:, j, :], PIECES2), acc_view(s, PIECES2), ACT.Sigmoid),
                       "to_dve")
                    free[s].step()
                norm_stats(lambda j: R[:, 8 + j, 0:TP], 6, TP, PIECES2, 1, (R[:, 6, :], R[:, 7, :]), R[:, 4, :],
                           QR, 1e-6, lambda j: None)
                norm_stats(lambda j: R[:, 14 + j, 0:TP], 2, TP, PIECES2, 0, (R[:, 6, :], R[:, 7, :]), R[:, 5, :],
                           KVR, 1e-6, lambda j: None)
                ready[1].step()
                free[1].step()
                by_signal(0)
                for j in range(8):
                    await_unit(j % 2)
                    release(nc.scalar.activation(cut(R[:, j, :], PIECES2), acc_view(j % 2, PIECES2),
                                                 ACT.Sigmoid), j % 2)
                by_signal(0)
                act.dma_start(spill_g, R[:, 0:8, 0:TP]).then_inc(sems["g_spilled"], 16)
                q96 = slice(0, QKD)
                for h in range(MH):
                    await_ready(0)
                    if h == 0:
                        by_signal(0)
                        act.wait_ge(sems["g_spilled"], 16 * (l + 1))
                    do(nc.scalar.activation(cut(R[q96, 9, :], PIECES2), acc_view(0, PIECES2, q96), ACT.Square))
                    release(copy(cut(R[q96, 8, :], PIECES2), acc_view(0, PIECES2, q96),
                                 param(f"qn_{l}", 0, q96)), 0)
                    await_unit(1)
                    do(nc.scalar.activation(cut(R[0:64, 15, :], PIECES2), acc_view(1, PIECES2, slice(0, 64)),
                                            ACT.Square))
                    do(copy(cut(R[0:64, 14, :], PIECES2), acc_view(1, PIECES2, slice(0, 64)),
                            param(f"kn_{l}", 0, slice(0, 64))))
                    release(copy(cut(R[64:128, 13, :], PIECES2), acc_view(1, PIECES2, slice(64, 128))), 1)
                    for s in range(2):
                        await_ready(s)
                        release(nc.scalar.activation(cut(R[q96, s, :], PIECES2), acc_view(s, PIECES2, q96),
                                                     ACT.Ln, scale=1.0 / QKD, bias=eps_col(1e-6, QKD)), s)
                        after(f"free{s}")
                        do(nc.scalar.activation(R[q96, s, 0:TP], R[q96, s, 0:TP], ACT.Exp, scale=-0.5), "to_dve")
                    ready[0].step()
                    free[0].step()
                    for half in range(2):
                        aux_ready[half].step()
                        aux_ready[half].wait(act)
                        if half == 0:
                            do(copy(R[:, 12, 0:512], aux[:, 0, :]), "aux_free0")
                        else:
                            n = TP - P * (TB - 1)
                            do(copy(R[0:n, 12, 512:576], aux[0:n, 1, 0:64]), "aux_free1")

                    def exp_block(i):
                        s = i % 2
                        nq, nk = min(P, TP - P * i), min(P * (i + 1), TP)
                        ready[s].step()
                        by_signal(0)
                        release(nc.scalar.activation(R[0:nq, 4 + s, 0:nk],
                                                     acc[0:nq, s, :, :].rearrange("p a b -> p (a b)")[:, 0:nk],
                                                     ACT.Exp, bias=S_[0:nq, 16 + s:17 + s],
                                                     accum_out=S_[0:nq, 18 + s:19 + s]), s)

                    exp_block(0)
                    for i in range(TB):
                        s = i % 2
                        nq = min(P, TP - P * i)
                        nb = -(-(i + 1) // 4)
                        for b in range(nb):
                            aux_ready[b % 2].step()
                            aux_ready[b % 2].wait(act)
                            if b >= 2:
                                c["pe_read"].wait(act, back=nb - 1 - (b - 1))
                            elif b == 0 and i:
                                ready[1 - s].wait(act)
                            if b == 0:
                                c["pe_read"].step(nb - 1)
                            k = min(4, i + 1 - 4 * b)
                            rows = P if P * (4 * b + k) <= TP else TP - P * (4 * b)
                            out = R[0:rows, 6 + b % 2, 0:P * k].rearrange("p (t q) -> p t q", q=P)[:, :, 0:nq]
                            src = aux[0:rows, b % 2, 0:P * k].rearrange("p (t q) -> p t q", q=P)[:, :, 0:nq]
                            ins = copy(out, src)
                            do(ins, f"aux_free{b % 2}")
                        if i + 1 < TB:
                            exp_block(i + 1)
                        ready[s].step()
                        free[s].step()
                by_signal(0)
                act.dma_start(R[:, 0:8, 0:TP], spill_g.rearrange("p (c t) -> p c t", c=8)) \
                   .then_inc(sems["sg_in"], 16)
                by_signal(0)
                act.dma_start(X_[:], spill_m).then_inc(sems["mg_in"], 16)
                for j in range(4):
                    unit.step()
                    ready[0].step()
                    free[0].step()
                    free[1].step()
                by_signal(0)
                act.wait_ge(sems["spilled"], 16 * (l + 1))
                act.dma_start(X_[:], spill_x).then_inc(sems["xre_in"], 16)
                if last:
                    for j in range(KC):
                        updated(j % 2)
                        act.dma_start(outT[P * j:P * j + P, :], X[:, j, META:T2]).then_inc(sems["stored"], 16)
                    act.wait_ge(sems["stored"], 16 * KC)

        @block.vector
        def _(dve):
            c = counts()
            free = (c["free0"], c["free1"])
            ready = (c["ready0"], c["ready1"])
            aux_free = (c["aux_free0"], c["aux_free1"])
            aux_ready = (c["aux_ready0"], c["aux_ready1"])
            unit = c["unit_done"]
            vec = nc.vector

            def do(ins, name="dve_step"):
                ins.then_inc(sems[name], 1)
                c[name].step()
                c[name].wait(dve)

            def await_unit():
                unit.step()
                unit.wait(dve)

            def await_ready(s):
                ready[s].step()
                ready[s].wait(dve)

            def await_free(s):
                free[s].step()
                free[s].wait(dve)

            def from_act():
                c["to_dve"].step()
                c["to_dve"].wait(dve)

            def split(src, hi, lo, name):
                do(vec.tensor_copy(hi, src))
                do(vec.tensor_tensor(lo, src, hi.bitcast(F32), ALU.subtract), name)

            def normalise(n, src, gain, rs, y, width):
                c["rs_ready"].step()
                c["rs_ready"].wait(dve)
                for j in range(n):
                    do(vec.scalar_tensor_tensor(y[:, 0:width], src(j), param(gain, j), rs[:, 0:width],
                                                ALU.mult, ALU.mult))
                    split(y[:, 0:width], Ah[:, j, 0:width], Al[:, j, 0:width], "a_ready")

            dve.wait_ge(sems["consts_in"], 32)
            do(vec.memset(S_[:, 0:62], 1e-6))
            do(vec.memset(S_[:, 61:62], 1e-5), "to_act")
            do(vec.tensor_scalar(S_[:, 9:12], V_[:, PARAM_COLS["lam"]:PARAM_COLS["lam"] + 3], -1.0, 0.0,
                                 ALU.mult, ALU.max))
            from_act()
            do(vec.tensor_tensor(S_[:, 9:12], S_[:, 9:12], S_[:, 6:9], ALU.add))
            do(vec.tensor_scalar_mul(S_[:, 9:12], S_[:, 9:12], 8.0))
            do(vec.memset(R[:, 0:2, 0:CONV_TAPS - 1], 0.0))
            do(vec.memset(R[:, 2:5, 0:LRU_TAPS - 1], 0.0))
            dve.wait_ge(sems["x_in"], 16)
            ready[0].step()
            free[0].step()
            normalise(KC, lambda j: X[:, j, META:T2], "norm1", R[:, 10, :], R[:, 11, :], T1)
            for n in range(2):
                unit.step()
                await_free(n)
            for n in range(2):
                await_unit()
                do(vec.tensor_tensor(cut(R[:, n, CONV_TAPS - 1:], PIECES1), acc_view(n, PIECES1),
                                     cut(X[:, n, :], PIECES1), ALU.mult), f"free{n}")

            def convolve(out, src, taps, w, b, name):
                do(vec.tensor_scalar(out, src[:, 0:T1], V_[:, w:w + 1], b, ALU.mult, ALU.add))
                for k in range(1, taps):
                    do(vec.scalar_tensor_tensor(out, src[:, k:k + T1], V_[:, w + k:w + k + 1], out,
                                                ALU.mult, ALU.add), name if k == taps - 1 else "dve_step")

            for n in range(4, 7):
                unit.step()
                await_free(n % 2)
                j = n - 4
                convolve(X[:, 4 + j, 0:T1], R[:, 2 + j, :], LRU_TAPS, PARAM_COLS["lcw"] + LRU_TAPS * j,
                         param("lcb", j), "to_pe")
            for j in range(2):
                convolve(X[:, 2 + j, 0:T1], R[:, j, :], CONV_TAPS, PARAM_COLS["cdw"] + CONV_TAPS * j,
                         param("cdb", j), "dve_step" if j == 0 else "to_act")
            for n in range(7, UNITS_Z):
                unit.step()
                free[n % 2].step()
            for s in range(2):
                free[s].wait(dve)
            full = slice(0, T1)
            for j in range(3):
                ready[1].step()
                await_free(1)
                do(vec.tensor_scalar(X[:, 1, full], X[:, 7, full], S_[:, 9 + j:10 + j], None, ALU.mult), "to_act")
                ready[0].step()
                await_free(0)
                do(vec.tensor_tensor(X[:, 0, full], X[:, 0, full], X[:, 4 + j, full], ALU.mult))
                from_act()
                from_act()
                do(vec.tensor_scalar_add(X[:, 1, full], R[:, 2, full], 1.0))
                do(vec.reciprocal(X[:, 1, full], X[:, 1, full]))
                do(vec.scalar_tensor_tensor(R[:, 2, full], R[:, 2, full], 2.0, X[:, 1, full], ALU.mult, ALU.mult),
                   "to_act")
                from_act()
                do(vec.tensor_tensor(X[:, 0, full], X[:, 0, full], R[:, 3, full], ALU.mult))
                do(vec.tensor_tensor_scan(X[:, 1, full], R[:, 0, full], X[:, 0, full], 0.0, ALU.mult, ALU.add))
                do(vec.tensor_tensor(R[:, 4, full], R[:, 1, full], X[:, 1, full], ALU.mult))
                split(R[:, 4, full], Ah[:, j, full], Al[:, j, full], "a_ready")
                if j == 2:
                    do(vec.tensor_copy(S_[:, 40:41], S_[:, 60:61]), "to_pe")
            await_ready(0)
            for j in range(2):
                do(vec.scalar_tensor_tensor(cut(X[:, 2 + j, :], PIECES1), acc_view(0, PIECES1), -1.0 / 256,
                                            cut(X[:, 2 + j, :], PIECES1), ALU.mult, ALU.add),
                   "dve_step" if j == 0 else "free0")
            for j in range(2):
                do(vec.tensor_tensor(R[:, 2 + j, full], X[:, 2 + j, full], X[:, 2 + j, full], ALU.mult),
                   "dve_step" if j == 0 else "to_pe")
            ready[1].step()
            free[1].step()
            c["rs_ready"].step()
            c["rs_ready"].wait(dve)
            for j in range(2):
                y = X[:, 2 + j, full]
                do(vec.scalar_tensor_tensor(y, y, param("clg", j), R[:, 4, full], ALU.mult, ALU.mult))
                do(vec.tensor_scalar(y, y, param("clb", j), None, ALU.add), "to_act")
            for j in range(2):
                y = X[:, 2 + j, full]
                from_act()
                do(vec.tensor_tensor(y, y, R[:, 2 + j, full], ALU.mult))
                split(y, Ah[:, 3 + j, full], Al[:, 3 + j, full], "a_ready")
            dve.wait_ge(sems["bands_in"], 16)
            pend = []

            def take_lse():
                g, j, b = pend.pop()
                aux_ready[0].step()
                aux_ready[0].wait(dve)
                rows = slice(64 * j, 64 * j + 64)
                d = PATTERNS[g][1]
                nat = R[rows, 3 + g, full]
                src = aux[rows, 0, :]
                if d == 1:
                    ins = vec.tensor_copy(nat[:, 512 * b:512 * b + 512], src)
                else:
                    ins = vec.tensor_copy(nat.rearrange("p (u r) -> p r u", r=d)[:, b * d // 2:(b + 1) * d // 2, :],
                                          src.rearrange("p (r u) -> p r u", r=d // 2))
                do(ins, "aux_free0")

            for g in range(3):
                lo = 0 if g < 2 else 128
                for half in range(2):
                    aux_ready[half].step()
                    aux_free[half].step()
                for j in range(2):
                    def stats(b):
                        await_ready(b)
                        pb = X[:, 1 + b, 0:1024].rearrange("p (i k) -> p i k", k=256)
                        if pend:
                            pass
                        sc = acc[:, b, 0:2, :].rearrange("p a (c k) -> p (a c) k", c=2)
                        h = 2 * g + j
                        band = X_[:, 6 * TP + 256 * h + lo:6 * TP + 256 * h + 256].unsqueeze(1) \
                            .to_broadcast([P, 4, 256 - lo])
                        do(vec.scalar_tensor_tensor(pb[:, :, lo:256], sc[:, :, lo:256], HD ** -0.5, band,
                                                    ALU.mult, ALU.add), f"free{b}")
                        if g == 0 and b == 0:
                            do(vec.memset(pb[:, 0:1, 0:128], NEG))
                        if g == 1:
                            do(vec.memset(X[:, 1 + b, 0:1024].rearrange("p (a x) -> p a x", x=512)[:, :, 0:128],
                                          NEG))
                        do(vec.tensor_reduce(S_[:, 16 + 4 * b:20 + 4 * b], pb[:, :, lo:256], AX, ALU.max,
                                             negate=True), "to_act")

                    def finish(b):
                        from_act()
                        pb = X[:, 1 + b, 0:1024].rearrange("p (i k) -> p i k", k=256)[:, :, lo:256]
                        do(vec.reciprocal(S_[:, 44 + 4 * b:48 + 4 * b], S_[:, 24 + 4 * b:28 + 4 * b]))
                        rl = S_[:, 44 + 4 * b:48 + 4 * b].unsqueeze(2).to_broadcast([P, 4, 256 - lo])
                        do(vec.tensor_tensor(pb, pb, rl, ALU.mult), "to_pe")
                        lse = S_[:, 32 + 4 * b:36 + 4 * b]
                        do(vec.tensor_tensor(lse, lse, S_[:, 16 + 4 * b:20 + 4 * b], ALU.subtract))
                        if pend:
                            take_lse()
                        do(vec.tensor_tensor(X[:, 5, 0:512].rearrange("p (i q) -> p i q", q=P),
                                             ident.unsqueeze(1).to_broadcast([P, 4, P]),
                                             lse.unsqueeze(2).to_broadcast([P, 4, P]), ALU.mult), "to_pe")
                        pend.append((g, j, b))

                    stats(0)
                    stats(1)
                    for b in range(2):
                        finish(b)
                        for part in ((0, 1) if g < 2 else (1,)):
                            aux_ready[part].step()
                            aux_free[part].step()
                        ready[b].step()
                        free[b].step()
                    take_lse()
            for b in range(2):
                free[b].wait(dve)
            top = R[:, 6, full]
            do(vec.tensor_tensor(top, R[:, 3, full], R[:, 4, full], ALU.max))
            do(vec.tensor_tensor(top, top, R[:, 5, full], ALU.max))
            for g in range(3):
                do(vec.tensor_tensor(R[:, 3 + g, full], R[:, 3 + g, full], top, ALU.subtract),
                   "to_act" if g == 2 else "dve_step")
            from_act()
            do(vec.tensor_tensor(top, R[:, 3, full], R[:, 4, full], ALU.add))
            do(vec.tensor_tensor(top, top, R[:, 5, full], ALU.add))
            do(vec.reciprocal(top, top))
            for g in range(3):
                do(vec.tensor_tensor(R[:, 3 + g, full], R[:, 3 + g, full], top, ALU.mult))
                do(vec.tensor_tensor(R[:, g, full], R[:, g, full], R[:, 3 + g, full], ALU.mult))
                split(R[:, g, full], Ah[:, 5 + g, full], Al[:, 5 + g, full], "a_ready")

            def add_to_residual(j, s, pieces, c0, width):
                x = X[:, j, c0:c0 + width].rearrange("p (a b) -> p a b", a=pieces[0])
                do(vec.tensor_tensor(x, acc_view(s, pieces), x, ALU.add), f"free{s}")

            dve.wait_ge(sems["xre_in"], 16)
            for j in range(KC):
                await_unit()
                add_to_residual(j, (j + 1) % 2, PIECES1, META, T1)
            ready[1].step()
            free[1].step()
            normalise(KC, lambda j: X[:, j, META:T2], "norm2", R[:, 10, :], R[:, 11, :], T1)
            dve.wait_ge(sems["pos_in"], 16)
            do(vec.tensor_scalar(R[:, 9, META:T2], R[:, 8, META:T2].bitcast(I32), float(META), None, ALU.add))
            do(vec.tensor_copy(R[:, 9, 0:META], C_[:, 544:560]))
            do(vec.memset(R[:, 9, T2:TP], 0.0))
            ang, k, sn, cs = R[:, 9, 0:TP], R[:, 8, 0:TP], R[:, 17, 0:TP], R[:, 16, 0:TP]
            magic, pi = 12582912.0, 3.1415925
            do(vec.tensor_scalar(ang, ang, param("freq"), None, ALU.mult))
            do(vec.tensor_scalar(k, ang, float(1 / (2 * np.pi)), magic, ALU.mult, ALU.add))
            do(vec.tensor_scalar_add(k, k, -magic))
            c1, c2 = 6.28125, 2029 / 2 ** 20
            c3 = float(2 * np.pi - c1 - c2)
            do(vec.scalar_tensor_tensor(ang, k, -c1, ang, ALU.mult, ALU.add))
            do(vec.scalar_tensor_tensor(ang, k, -c2, ang, ALU.mult, ALU.add))
            do(vec.scalar_tensor_tensor(ang, k, -c3, ang, ALU.mult, ALU.add))
            do(vec.tensor_scalar(sn, ang, pi, -pi, ALU.min, ALU.max), "to_act")
            do(vec.tensor_scalar_add(ang, ang, float(np.pi / 2)))
            do(vec.tensor_scalar(k, ang, float(np.pi), float(-2 * np.pi), ALU.is_gt, ALU.mult))
            do(vec.tensor_tensor(ang, ang, k, ALU.add))
            do(vec.tensor_scalar(cs, ang, pi, -pi, ALU.min, ALU.max), "to_act")
            from_act()
            from_act()
            with dve.Fori(0, GROUPS) as i:
                loop = Loop(i, GROUPS, [(unit, FG + 4), (free[0], FG // 2 + 4), (free[1], FG // 2 + 4),
                                        (ready[0], 4), (c["f_ready"], FG), (c["dve_step"], 2 * FG)])
                for j in range(FG):
                    unit.step()
                    await_free((j + 1) % 2)
                    do(vec.tensor_tensor(R[:, 11, full], R[:, 12 + j, full], R[:, 12 + j, full], ALU.mult))
                    split(R[:, 11, full], F[:, j, full], F[:, 4 + j, full], "f_ready")
                for j in range(KC):
                    if j % 2:
                        await_unit()
                    else:
                        await_ready(0)
                    add_to_residual(j, j % 2, PIECES1, META, T1)
                loop.end()
            ready[0].step()
            free[0].step()
            c["rs_ready"].step()
            c["rs_ready"].wait(dve)
            do(vec.memset(X[:, :, T2:TP], 0.0))
            for j in range(KC):
                do(vec.scalar_tensor_tensor(X[:, j, META:T2], X[:, j, META:T2], param("final", j),
                                            R[:, 10, full], ALU.mult, ALU.mult), "to_act")
            wide = slice(0, TP)
            dve.wait_ge(sems["meta_in"], 16)
            for l in range(LAYERS):
                last = l == LAYERS - 1
                ready[0].step()
                free[0].step()
                normalise(KC, lambda j: X[:, j, :], f"n2_{l}", R[:, 10, :], R[:, 11, :], TP)
                do(vec.memset(R[:, 0:4, 0:16], 0.0), "to_act")
                dve.wait_ge(sems["spilled"], 16 * (l + 1))
                for g in range(4):
                    unit.step()
                    await_free(g % 2)
                    u = R[:, g, :]
                    bufs = (X_[:, 4 * TP:4 * TP + 1060], X_[:, 6 * TP:6 * TP + 1060])
                    cur, first = u, 0
                    for k in range(g + 1):
                        first += 2 ** k
                        to = bufs[k % 2]
                        do(vec.tensor_tensor(to[:, first:1060], cur[:, first:1060],
                                             cur[:, first - 2 ** k:1060 - 2 ** k], ALU.add))
                        cur = to
                    w = POOLW[g]
                    y = X[:, 2, :]
                    do(vec.scalar_tensor_tensor(y, cur[:, 16:1060], 1.0 / w, u[:, 16:1060], ALU.mult,
                                                ALU.subtract))
                    do(vec.tensor_tensor(y[:, 0:16], cur[:, 16:32], C_[:, 480 + 16 * g:496 + 16 * g], ALU.mult))
                    do(vec.tensor_tensor(y[:, 0:16], y[:, 0:16], u[:, 16:32], ALU.subtract))
                    split(y, G[:, g, wide], G[:, 4 + g, wide], "f_ready")
                for j in range(4):
                    await_unit()
                    from_act()
                    z = R[:, 4 + j, wide]
                    do(vec.tensor_tensor(cut(z, PIECES2), acc_view(j % 2, PIECES2), cut(z, PIECES2), ALU.mult),
                       f"free{j % 2}")
                for j in range(4):
                    if j < 3:
                        await_ready(j % 2)
                    else:
                        await_unit()
                    y = X[:, 2, :]
                    do(vec.scalar_tensor_tensor(cut(y, PIECES2), acc_view(j % 2, PIECES2), param(f"ps_{l}", j),
                                                cut(R[:, 4 + j, :], PIECES2), ALU.mult, ALU.mult), f"free{j % 2}")
                    split(y, G[:, j, wide], G[:, 4 + j, wide], "f_ready")
                for j in range(4):
                    for s in range(2):
                        unit.step()
                        await_free(s)
                    for s in range(2):
                        if s == 0:
                            await_ready(0)
                        else:
                            await_unit()
                        do(vec.tensor_tensor(cut(X[:, 2 * j + s, :], PIECES2), acc_view(s, PIECES2),
                                             cut(R[:, s, :], PIECES2), ALU.mult), f"free{s}")
                for j in range(8):
                    unit.step()
                    free[j % 2].step()
                unit.step()
                await_free(0)
                for j in range(4):
                    s = 1 - j % 2
                    await_unit()
                    from_act()
                    z = X[:, j, :]
                    do(vec.tensor_tensor(cut(z, PIECES2), acc_view(s, PIECES2), cut(z, PIECES2), ALU.mult),
                       f"free{s}")
                for s, c0, n, gain, rs in ((1, 0, 6, f"qa_{l}", R[:, 4, wide]), (0, 6, 2, f"kva_{l}", R[:, 5, wide])):
                    ready[s].step()
                    free[s].step()
                    c["rs_ready"].step()
                    c["rs_ready"].wait(dve)
                    for j in range(n):
                        y = R[:, 8 + c0 + j, wide]
                        do(vec.scalar_tensor_tensor(y, y, param(gain, j), rs, ALU.mult, ALU.mult),
                           "to_act" if (s == 0 and j == 1) else "dve_step")
                rr = slice(NOPE, QKD)
                await_ready(1)
                do(vec.tensor_tensor(X[rr, 5, :], X[rr, 7, :], R[rr, 16, wide], ALU.mult))
                do(vec.tensor_tensor(cut(X[rr, 4, :], PIECES2), acc_view(1, PIECES2, rr),
                                     cut(R[rr, 17, :], PIECES2), ALU.mult), "free1")
                do(vec.tensor_tensor(X[rr, 5, :], X[rr, 5, :], X[rr, 4, :], ALU.add))
                for j in range(8):
                    unit.step()
                    await_free(j % 2)
                do(vec.tensor_copy(S_[:, 40:41], S_[:, 60:61]), "to_act")
                for j in range(8):
                    split(R[:, 8 + j, wide], Ah[:, j, :], Al[:, j, :], "a_ready")
                do(vec.tensor_copy(R[rr, 14, wide], X[rr, 5, :]))
                do(vec.tensor_copy(R[rr, 15, wide], X[rr, 6, :]), "to_act")
                q96 = slice(0, QKD)
                for h in range(MH):
                    ready[0].step()
                    free[0].step()
                    unit.step()
                    free[1].step()
                    free[0].wait(dve)
                    free[1].wait(dve)
                    ready[0].step()
                    ready[1].step()
                    free[0].step()
                    free[1].step()
                    if h == 0:
                        dve.wait_ge(sems["g_spilled"], 16 * (l + 1))
                    do(vec.tensor_tensor(R[q96, 2, wide], R[q96, 8, wide], R[q96, 16, wide], ALU.mult))
                    await_ready(0)
                    do(vec.tensor_tensor(cut(R[q96, 3, :], PIECES2), acc_view(0, PIECES2, q96),
                                         cut(R[q96, 17, :], PIECES2), ALU.mult), "free0")
                    do(vec.tensor_tensor(R[q96, 2, wide], R[q96, 2, wide], R[q96, 3, wide], ALU.add))
                    from_act()
                    do(vec.scalar_tensor_tensor(R[q96, 10, wide], R[q96, 2, wide], QKD ** -0.5, R[q96, 0, wide],
                                                ALU.mult, ALU.mult))
                    from_act()
                    do(vec.tensor_tensor(R[q96, 11, wide], R[q96, 14, wide], R[q96, 1, wide], ALU.mult), "to_pe")
                    for half in range(2):
                        aux_ready[half].step()
                        aux_free[half].step()

                    def max_block(i):
                        s = i % 2
                        nq, nk = min(P, TP - P * i), min(P * (i + 1), TP)
                        flat = acc[0:nq, s, :, :].rearrange("p a b -> p (a b)")
                        await_ready(s)
                        diag = flat[:, P * i:P * i + nq]
                        do(vec.tensor_tensor(diag, diag, causal[0:nq, 0:nq], ALU.add))
                        do(vec.tensor_reduce(S_[0:nq, 16 + s:17 + s], flat[:, 0:nk], AX, ALU.max, negate=True),
                           "to_act")

                    max_block(0)
                    for i in range(TB):
                        s = i % 2
                        nq, nk = min(P, TP - P * i), min(P * (i + 1), TP)
                        await_free(s)
                        do(vec.reciprocal(S_[0:nq, 20 + s:21 + s], S_[0:nq, 18 + s:19 + s]))
                        pr = R[0:nq, 4 + s, 0:nk]
                        do(vec.tensor_scalar(pr, pr, S_[0:nq, 20 + s:21 + s], None, ALU.mult), "to_pe")
                        if i + 1 < TB:
                            max_block(i + 1)
                        await_ready(s)
                        rows = slice(64 * (h % 2), 64 * (h % 2) + 64)
                        cols = slice(P * i, P * i + nq)
                        do(vec.tensor_tensor(X[rows, 4 + h // 2, cols], acc[rows, s, 2, 128:128 + nq],
                                             X[rows, h // 2, cols], ALU.mult), f"free{s}")
                do(vec.tensor_copy(S_[:, 40:41], S_[:, 60:61]), "to_act")
                for j in range(4):
                    split(X[:, 4 + j, :], G[:, j, wide], G[:, 4 + j, wide], "f_ready")
                do(vec.tensor_copy(S_[:, 40:41], S_[:, 60:61]), "to_act")
                dve.wait_ge(sems["sg_in"], 16 * (l + 1))
                dve.wait_ge(sems["mg_in"], 16 * (l + 1))
                for j in range(KC):
                    s = j % 2
                    if s == 0:
                        await_ready(0)
                    else:
                        await_unit()
                    y = R[:, j, wide]
                    do(vec.tensor_tensor(cut(y, PIECES2), acc_view(s, PIECES2), cut(y, PIECES2), ALU.mult),
                       f"free{s}")
                    do(vec.tensor_tensor(y, y, X[:, j, :], ALU.add))
                    split(y, Ah[:, j, :], Al[:, j, :], "a_ready")
                do(vec.tensor_copy(S_[:, 40:41], S_[:, 60:61]), "to_act")
                dve.wait_ge(sems["xre_in"], 16 * (l + 2))
                for j in range(KC):
                    await_unit()
                    add_to_residual(j, j % 2, PIECES2, 0, TP)


def weight_stream(w):
    units = []

    def rows(m, order=None):
        k = m.shape[0] // P
        m = m.reshape(k, P, m.shape[1])
        return m if order is None else m[list(order)]

    def unit(*blocks):
        u = np.zeros((P, UW), np.float32)
        at = 0
        for b in blocks:
            k, _, m = b.shape
            u[:, at:at + k * m] = b.transpose(1, 0, 2).reshape(P, k * m)
            at += k * m
        units.append(u)

    A, C, L = ATTN_HEADS * HD, 256, 384
    w_in = rows(w["w_in"][0])
    q0, k0, v0 = 0, A, 2 * A
    ca, cg = 3 * A, 3 * A + C
    lg = 3 * A + 2 * C
    lx = lg + L
    cols = [cg, cg + P, ca, ca + P] + [lx + P * j for j in range(3)] + [lg + P * j for j in range(3)]
    for g in range(3):
        cols += [q0 + P * g, k0 + P * g, v0 + P * g]
    for col in cols:
        unit(w_in[:, :, col:col + P])
    w_out = rows(w["w_out"][0], (5, 6, 7, 3, 4, 0, 1, 2))
    for j in range(KC):
        unit(w_out[:, :, P * j:P * j + P])
    up, down = rows(w["w_up"][0]), rows(w["w_down"][0])
    for g in range(GROUPS):
        for j in range(FG):
            col = P * (FG * g + j)
            unit(up[:, :, col:col + P])
        d = down[FG * g:FG * g + FG]
        for j in range(4):
            unit(d[:, :, 256 * j:256 * j + P], d[:, :, 256 * j + P:256 * j + 256])
    for l in range(LAYERS):
        wi = rows(w["w_in_2"][l])
        for j in range(8):
            unit(wi[:, :, P * j:P * j + P])
        unit(*[w["pool_w_group_2"][l][g][None] for g in range(4)])
        pu = rows(w["pool_w_up_2"][l])
        for j in range(4):
            for s in range(2):
                col = 2592 + P * (2 * j + s)
                unit(wi[:, :, col:col + P])
            unit(pu[:, :, 256 * j:256 * j + P], pu[:, :, 256 * j + P:256 * j + 256])
        for j in range(8):
            unit(wi[:, :, 1024 + P * j:1024 + P * j + P])
        rope = np.zeros((KC, P, QKD), np.float32)
        rope[:, :, NOPE:] = wi[:, :, 2048:2080]
        unit(rope)
        for j in range(4):
            unit(wi[:, :, 2080 + P * j:2080 + P * j + P])
        for j in range(8):
            unit(wi[:, :, 3616 + P * j:3616 + P * j + P])
        wq, wkv = rows(w["w_q_b_2"][l]), rows(w["w_kv_b_2"][l])
        for h in range(MH):
            unit(wq[:, :, QKD * h:QKD * h + QKD], wkv[:, :, P * h:P * h + P])
        mu = rows(w["mla_w_up_2"][l])
        for j in range(4):
            unit(mu[:, :, 256 * j:256 * j + P], mu[:, :, 256 * j + P:256 * j + 256])
        wo = rows(w["w_out_2"][l])
        for j in range(8):
            unit(wo[:, :, P * j:P * j + P])
    assert len(units) == N_UNITS, (len(units), N_UNITS)
    return np.stack(units)


def param_table(w):
    t = np.zeros((P, NPARAM), np.float32)

    def put(name, v, i=0):
        t[:, PARAM_COLS[name] + i:PARAM_COLS[name] + i + v.shape[1]] = v

    def col(v):
        return v.reshape(-1, P).T

    put("norm1", col(w["norm1_g"][0]))
    for j in range(2):
        put("cdw", w["conv_dw_w"][0][:, P * j:P * j + P].T, CONV_TAPS * j)
    for j in range(3):
        put("lcw", w["lru_conv_w"][0][:, P * j:P * j + P].T, LRU_TAPS * j)
    for name, src in (("cdb", "conv_dw_b"), ("clg", "conv_ln_g"), ("clb", "conv_ln_b"), ("lcb", "lru_conv_b"),
                      ("lba", "lru_ba"), ("lbx", "lru_bx"), ("lam", "lru_lambda"), ("norm2", "norm2_g")):
        put(name, col(w[src][0]))
    put("final", col(w["final_g"]))
    for l in range(LAYERS):
        put(f"n2_{l}", col(w["norm_gain_2"][l]))
        put(f"ps_{l}", col(w["pool_scale_2"][l]))
        put(f"qa_{l}", col(w["q_a_norm_gain_2"][l]))
        put(f"kva_{l}", col(w["kv_a_norm_gain_2"][l]))
        t[0:QKD, PARAM_COLS[f"qn_{l}"]] = w["q_norm_gain_2"][l]
        t[0:QKD, PARAM_COLS[f"kn_{l}"]] = w["k_norm_gain_2"][l]
    half = ROPE // 2
    inv = (np.float32(10000.0) ** (-np.arange(half, dtype=np.float32) / np.float32(half))).astype(np.float32)
    t[NOPE:NOPE + half, PARAM_COLS["freq"]] = inv
    t[NOPE + half:QKD, PARAM_COLS["freq"]] = inv
    return t


def recurrent_gates(w):
    t = np.zeros((P, 2, 3, P), np.float32)
    for m, name in enumerate(("lru_wa", "lru_wx")):
        for h in range(6):
            o = 64 * (h % 2)
            t[o:o + 64, m, h // 2, o:o + 64] = w[name][0][h]
    return t.reshape(P, -1)


def kernel(**inputs):
    import concourse.bacc as bacc
    from concourse.bass_utils import run_bass_kernel_spmd

    w = {k: np.asarray(v) for k, v in inputs.items()}
    consts, bands = shape_constants()
    arrays = {
        "xT": np.ascontiguousarray(w["x"][0].T),
        "metaT": np.ascontiguousarray(w["meta_tokens_2"].T),
        "pos": np.ascontiguousarray(np.broadcast_to(w["positions_2"], (P, T1))),
        "params": param_table(w),
        "consts": consts,
        "bands": bands,
        "lru_w": recurrent_gates(w),
        "wstream": weight_stream(w),
    }
    nc = bacc.Bacc("TRN2", target_bir_lowering=False, num_devices=1)
    args = [nc.dram_tensor("in_" + k, a.shape, mybir.dt.from_np(a.dtype), kind="ExternalInput").ap()
            for k, a in arrays.items()]
    out = nc.dram_tensor("outT", (DM, T1), F32, kind="ExternalOutput")
    build(nc, *args, out.ap())
    r = run_bass_kernel_spmd(nc, [{"in_" + k: a for k, a in arrays.items()}], core_ids=[0])
    return np.ascontiguousarray(r.results[0]["outT"].T)[None]
```

```python
from contextlib import ExitStack

import numpy as np

import concourse.bass as bass
from concourse import mybir

F32 = mybir.dt.float32
F32R = mybir.dt.float32r
I32 = mybir.dt.int32
ALU = mybir.AluOpType
ACT = mybir.ActivationFunctionType
AX = mybir.AxisListType.X

P = 128
DM = 1024
KC = DM // P
T1 = 1024
META = 16
T2 = T1 + META
TP = 1044
TB = -(-TP // P)
LAYERS = 2
PIECES1 = (2, 512)
PIECES2 = (3, 348)
RW = 1060
NR = 19
NEG = -1e30

ATTN_HEADS, HD = 6, 64
PATTERNS = ((128, 1), (512, 4), (2048, 16))
CONV_TAPS, LRU_TAPS = 31, 4
DFF = 4096
FG = 4
GROUPS = DFF // P // FG

MH, NOPE, ROPE, VD = 8, 64, 32, 64
QKD = NOPE + ROPE
QR, KVR = 768, 256
POOLW = (2, 4, 8, 16)

UW = 1024

PARAM_COLS = {}


def _columns():
    at = 0
    for name, n in (("norm1", 8), ("cdw", 62), ("cdb", 2), ("clg", 2), ("clb", 2), ("lcw", 12), ("lcb", 3),
                    ("lba", 3), ("lbx", 3), ("lam", 3), ("norm2", 8), ("final", 8),
                    ("n2_0", 8), ("n2_1", 8), ("ps_0", 4), ("ps_1", 4), ("qa_0", 6), ("qa_1", 6),
                    ("kva_0", 2), ("kva_1", 2), ("qn_0", 1), ("qn_1", 1), ("kn_0", 1), ("kn_1", 1),
                    ("freq", 1), ("sign", 1), ("rows96", 1), ("rows20", 1)):
        PARAM_COLS[name] = at
        at += n
    return at


NPARAM = _columns()

CONST_COLS = dict(ident=0, ones=128, ones96=256, causal=384, after=512, invcnt=640, meta=704)
NCONST = 720


def shape_constants():
    c = np.zeros((P, NCONST), np.float32)
    c[:, 0:128] = np.eye(P)
    c[:, 128:256] = 1.0
    c[:, 256:384] = 1.0
    c[ROPE:2 * ROPE, 256:384] = 0.0
    q, k = np.arange(P)[:, None], np.arange(P)[None, :]
    c[:, 384:512] = np.where(k <= q, 0.0, NEG)
    c[:, 512:640] = np.where(q <= k, 0.0, NEG)
    for g, w in enumerate(POOLW):
        c[:, 640 + 16 * g:640 + 16 * g + 16] = 1.0 / np.minimum(np.arange(16) + 1, w)
    c[:, 704:720] = np.arange(META)
    slopes = 2.0 ** (-8.0 * np.arange(1, ATTN_HEADS + 1) / ATTN_HEADS)
    band = np.full((P, ATTN_HEADS, 2 * P), NEG, np.float32)
    for h in range(ATTN_HEADS):
        g = h // 2
        d = PATTERNS[g][1]
        dist = q + P - np.arange(2 * P)[None, :]
        ok = (dist >= 0) & (dist <= P)
        if g == 2:
            own = np.arange(2 * P)[None, :] - P
            ok = (own >= 0) & (own <= q) & (own // 64 == q // 64)
        band[:, h] = np.where(ok, -np.float32(slopes[h]) * (d * dist).astype(np.float32), NEG)
    return c, band.reshape(P, -1)


class Count:

    def __init__(self, sem):
        self.sem, self.n, self.reg, self.per = sem, 0, None, 0

    def step(self, k=1):
        self.n += k

    def value(self, back=0):
        n = self.n - back
        return n if self.reg is None else self.reg * self.per + n

    def wait(self, eng, back=0):
        if self.reg is None and self.n - back <= 0:
            return
        eng.wait_ge(self.sem, self.value(back))


class Loop:

    def __init__(self, reg, times, counts):
        self.times, self.counts = times, counts
        for c, per in counts:
            c.reg, c.per, c.start = reg, per, c.n

    def end(self):
        for c, per in self.counts:
            assert c.n - c.start == per, (c.sem, c.n - c.start, per)
            c.reg, c.n = None, c.start + per * self.times


UNITS_Z = 19
N_UNITS1 = UNITS_Z + KC + GROUPS * (FG + 4)
N_UNITS2 = 4 + 4 + 1 + 12 + 6 + 2 + 1 + 4 + 8 + 8 + 4 + 8
N_UNITS = N_UNITS1 + LAYERS * N_UNITS2


def build(nc, xT, metaT, pos, params, consts, bands, lru_w, wstream, outT):
    with ExitStack() as ctx:
        def sem(name):
            return ctx.enter_context(nc.semaphore(name))

        start = -(-nc.sbuf_base // 64) * 64
        at = [start]

        def place(name, cols, dt=F32, offset=None):
            if offset is None:
                offset = at[0] = -(-at[0] // 32) * 32
                at[0] += 4 * cols
            return nc.alloc_sbuf_tensor_at(name, [P, cols], dt, offset=offset), offset

        def chunks(t, n, w):
            return t[:].rearrange("p (c t) -> p c t", c=n)

        X_, _ = place("residual", KC * TP)
        Ah_, _ = place("act_hi", KC * TP, F32R)
        Al_, _ = place("act_lo", KC * TP, F32R)
        Wraw_, _ = place("w_raw", 2 * UW)
        Wh_, _ = place("w_hi", 2 * UW, F32R)
        Wl_, _ = place("w_lo", 2 * UW, F32R)
        C_, _ = place("shape_consts", NCONST)
        V_, _ = place("params", NPARAM)
        S_, _ = place("small", 64)
        R_, r_at = place("work", NR * RW)
        U_, _ = place("head_out", 512)
        F_, _ = place("ff_split", 8 * RW, F32R, offset=r_at)
        G_, _ = place("pool_split", 8 * RW, F32R, offset=r_at + 4 * 8 * RW)
        assert at[0] <= nc.sbuf_usable_end, (at[0], nc.sbuf_usable_end)
        X, Ah, Al = chunks(X_, KC, TP), chunks(Ah_, KC, TP), chunks(Al_, KC, TP)
        Wraw, Wh, Wl = chunks(Wraw_, 2, UW), chunks(Wh_, 2, UW), chunks(Wl_, 2, UW)
        R, F, G = chunks(R_, NR, RW), chunks(F_, 8, RW), chunks(G_, 8, RW)
        ident, ones = C_[:, 0:128], C_[:, 128:256]
        ones96 = C_[:, 256:384]

        def param(name, i=0, rows=slice(0, P)):
            c = PARAM_COLS[name] + i
            return V_[rows, c:c + 1]

        V1 = G_[:, 0:TB * P].rearrange("p (t c) -> p t c", c=P)
        V2 = G_[:, TB * P:2 * TB * P].rearrange("p (t c) -> p t c", c=P)
        ring0 = 2 * TB * P
        PRING = 4

        def prob(n, part):
            o = ring0 + 1024 * (n % PRING) + 512 * part
            return G_[:, o:o + 512]

        idr0 = ring0 + 1024 * PRING
        ident_r, causal_r, after_r = (G_[:, idr0 + P * i:idr0 + P * i + P] for i in range(3))
        rsk = R_[:, 16 * RW - TP:16 * RW]
        assert idr0 + 3 * P <= 8 * RW - TP
        Q0, K0 = 0, 2
        LASTQ = TP - P
        ITEMS = [(0, j) for j in range(4)] + [(1, j) for j in range(8)] + [(2, None)]
        BATCHES = [(0, 1, 2), (3, 4, 5), (6, 7, 8), (9, 10, 11), (12,)]

        def head_inv(rows, pc):
            return U_[rows, :] if pc < 2 else R[rows, 18, 1024:TP]

        def item_cols(n):
            pc, j = ITEMS[n]
            lo = max(512 * pc, P * j)
            return lo, 512 * (pc + 1) - lo

        acc = ctx.enter_context(nc.psum_tensor("acc", [P, 2, 3, 512], F32))
        aux = ctx.enter_context(nc.psum_tensor("aux", [P, 2, 512], F32))

        spill_x = nc.dram_tensor("spill_x", (P, KC * TP), F32, kind="Internal").ap()
        spill_m = nc.dram_tensor("spill_m", (P, KC * TP), F32, kind="Internal").ap()
        spill_t = nc.dram_tensor("spill_t", (P, TP), F32, kind="Internal").ap()
        spill_g = nc.dram_tensor("spill_g", (P, KC * TP), F32, kind="Internal").ap()

        sems = {}
        for name in (
            "consts_in", "x_in", "meta_in", "lru_in", "bands_in", "xre_in",
            "w_in0", "w_in1", "w_hi_done", "w_lo_done", "unit_done",
            "ready0", "ready1", "free0", "free1",
            "aux_ready0", "aux_ready1", "aux_free0", "aux_free1",
            "a_ready",
            "f_ready",
            "sq_ready", "sq_free", "rs_ready", "x_ready",
            "dve_step", "act_step",
            "to_dve", "to_act", "to_pe",
            "act_to_pe", "pe_read",
            "spilled", "m_spilled", "g_spilled", "mg_in", "sg_in", "stored", "pos_in", "t_spilled", "t_in",
            "inv_ready",
            "lo_ready",
        ):
            sems[name] = sem(name)
        block = ctx.enter_context(nc.Block())

        def counts():
            return {k: Count(v) for k, v in sems.items()}

        def acc_view(s, pieces, rows=slice(0, P)):
            n, w = pieces
            return acc[rows, s, 0:n, 0:w]

        def cut(ap, pieces):
            n, w = pieces
            return ap[:, 0:n * w].rearrange("p (a b) -> p a b", a=n)

        z_order = ["gate0", "gate1", "a0", "a1", "lx0", "lx1", "lx2", "lg0", "lg1", "lg2"] + \
            [f"{m}{g}" for g in range(3) for m in "qkv"]

        @block.sync
        def _(sp):
            c = counts()
            sp.dma_start(C_[:], consts).then_inc(sems["consts_in"], 16)
            sp.dma_start(V_[:], params).then_inc(sems["consts_in"], 16)
            w_in = (sems["w_in0"], sems["w_in1"])

            def load(n, s):
                sp.dma_start(Wraw[:, s, :], wstream[n, :, :] if isinstance(n, int) else
                             wstream[bass.ds(n, 1), :, :].rearrange("o p f -> (o p) f")).then_inc(w_in[s], 16)

            load(0, 0)
            load(1, 1)
            with sp.Fori(1, N_UNITS // 2) as i:
                for s in range(2):
                    sp.wait_ge(sems["w_lo_done"], i * 2 + (s - 1))
                    load(i * 2 + s, s)
            if N_UNITS % 2:
                sp.wait_ge(sems["w_lo_done"], N_UNITS - 2)
                load(N_UNITS - 1, 0)

        @block.gpsimd
        def _(pool):
            w_in = (sems["w_in0"], sems["w_in1"])

            def split(n, s, landed):
                pool.wait_ge(w_in[s], landed)
                if not isinstance(n, int) or n >= 2:
                    pool.wait_ge(sems["unit_done"], n - 1)
                nc.gpsimd.tensor_copy(Wh[:, s, :], Wraw[:, s, :]).then_inc(sems["w_hi_done"], 1)
                pool.wait_ge(sems["w_hi_done"], n + 1)
                nc.gpsimd.tensor_tensor(Wl[:, s, :], Wraw[:, s, :], Wh[:, s, :].bitcast(F32),
                                        ALU.subtract).then_inc(sems["w_lo_done"], 1)

            pool.wait_ge(sems["consts_in"], 32)
            split(0, 0, 16)
            split(1, 1, 16)
            with pool.Fori(1, N_UNITS // 2) as i:
                for s in range(2):
                    pool.wait_ge(w_in[s], i * 16 + 16)
                    pool.wait_ge(sems["unit_done"], i * 2 + (s - 1))
                    nc.gpsimd.tensor_tensor(S_[:, 62:63], C_[:, 128:129], C_[:, 128:129], ALU.add)
                    nc.gpsimd.tensor_copy(Wh[:, s, :], Wraw[:, s, :]).then_inc(sems["w_hi_done"], 1)
                    pool.wait_ge(sems["w_hi_done"], i * 2 + (s + 1))
                    nc.gpsimd.tensor_tensor(Wl[:, s, :], Wraw[:, s, :], Wh[:, s, :].bitcast(F32),
                                            ALU.subtract).then_inc(sems["w_lo_done"], 1)
            if N_UNITS % 2:
                split(N_UNITS - 1, 0, 16 * (N_UNITS // 2 + 1))

        @block.tensor
        def _(pe):
            c = counts()
            free = (c["free0"], c["free1"])
            ready = (sems["ready0"], sems["ready1"])
            aux_free = (c["aux_free0"], c["aux_free1"])
            aux_ready = (sems["aux_ready0"], sems["aux_ready1"])
            unit = Count(sems["w_lo_done"])

            def take(s):
                free[s].wait(pe)
                free[s].step()

            def take_aux(s):
                aux_free[s].wait(pe)
                aux_free[s].step()

            def matrix(s, ws, w0, ks, m, hi, lo, pieces, arrive=None, last=None):
                n, w = pieces
                take(s)
                for j, k in enumerate(ks):
                    if arrive is not None:
                        pe.wait_ge(arrive[0], arrive[1] + j + 1)
                    for t, (wt, x) in enumerate(((Wh, hi), (Wh, lo), (Wl, hi))):
                        for p in range(n):
                            ins = nc.tensor.matmul(
                                acc[0:m, s, p, 0:w], wt[:, ws, w0 + j * m:w0 + j * m + m],
                                x[:, k, p * w:p * w + w],
                                start=(j == 0 and t == 0), stop=(j == len(ks) - 1 and t == 2))
                ins.then_inc(last if last is not None else ready[s], 1)

            def next_unit():
                unit.step()
                unit.wait(pe)

            def wide(s, ws, pieces, arrive=None, ks=range(KC), m=P):
                next_unit()
                matrix(s, ws, 0, ks, m, Ah, Al, pieces, arrive, sems["unit_done"])

            def narrow_pair(ws, lo_hi, pieces, arrive=None):
                next_unit()
                for s in range(2):
                    matrix(s, ws, s * 512, range(4), P, lo_hi, lo_hi_lo(lo_hi), pieces,
                           arrive, None if s == 0 else sems["unit_done"])

            def lo_hi_lo(t):
                return t[:, 4:8, :]

            def norm_sum(s, n, pieces, rows=P, slots=None):
                take(s)
                np_, w = pieces
                for j in range(n):
                    c["sq_ready"].step()
                    c["sq_ready"].wait(pe)
                    for p in range(np_):
                        ins = nc.tensor.matmul(acc[:, s, p, 0:w], ones, slots[j % 2][:, p * w:p * w + w],
                                               start=(j == 0), stop=(j == n - 1))
                    if j < n - 1:
                        ins.then_inc(sems["sq_free"], 1)
                ins.then_inc(ready[s], 1)

            pe.wait_ge(sems["consts_in"], 32)
            a0 = 0
            norm_sum(0, KC, PIECES1, slots=(R[:, 8, :], R[:, 9, :]))
            for s in range(2):
                wide(s, s, PIECES1, (sems["a_ready"], a0) if s == 0 else None)
            with pe.Fori(0, UNITS_Z // 2 - 1) as i:
                loop = Loop(i, UNITS_Z // 2 - 1, [(unit, 2), (free[0], 1), (free[1], 1)])
                for s in range(2):
                    wide(s, s, PIECES1)
                loop.end()
            wide(0, 0, PIECES1)
            pe.wait_ge(sems["lru_in"], 16)
            for j in range(3):
                c["to_pe"].step()
                c["to_pe"].wait(pe)
                for s, col in ((1, 0), (0, 384)):
                    take(s)
                    for p in range(2):
                        ins = nc.tensor.matmul(acc[:, s, p, :], R[:, 17, col + 128 * j:col + 128 * j + 128],
                                               X[:, 4 + j, p * 512:p * 512 + 512], start=True, stop=True)
                    ins.then_inc(ready[s], 1)
            for rnd in range(2):
                c["to_pe"].step()
                c["to_pe"].wait(pe)
                take(rnd)
                for j in range(2):
                    src = X[:, 2 + j, :] if rnd == 0 else R[:, 2 + j, :]
                    for p in range(2):
                        ins = nc.tensor.matmul(acc[:, rnd, p, :], ones, src[:, p * 512:p * 512 + 512],
                                               start=(j == 0), stop=(j == 1))
                ins.then_inc(ready[rnd], 1)
            PT, Vt = X[:, 3, :], X[:, 0, :]
            DG = X[:, 5, :]

            def scores(g, j, b):
                rows = slice(64 * j, 64 * j + 64)
                take(b)
                q, k = R[:, 8 + 3 * g, :], R[:, 9 + 3 * g, :]
                for i in range(4):
                    t = 4 * b + i
                    bank = acc[:, b, i // 2, 256 * (i % 2):256 * (i % 2) + 256]
                    has = (t > 0) if g == 0 else (t % 2 == 1)
                    if g < 2:
                        kt = t - 1 if has else t
                        nc.tensor.matmul(bank[:, 0:128], q[rows, 128 * t:128 * t + 128],
                                         k[rows, 128 * kt:128 * kt + 128], start=True, stop=True)
                    ins = nc.tensor.matmul(bank[:, 128:256], q[rows, 128 * t:128 * t + 128],
                                           k[rows, 128 * t:128 * t + 128], start=True, stop=True)
                ins.then_inc(ready[b], 1)

            for g in range(3):
                for half in range(2):
                    take_aux(half)
                    for i in range(4):
                        t = 4 * half + i
                        ins = nc.tensor.transpose(aux[:, half, 128 * i:128 * i + 128],
                                                  R[:, 10 + 3 * g, 128 * t:128 * t + 128], ident)
                    ins.then_inc(aux_ready[half], 1)
                for j in range(2):
                    for b in range(2):
                        scores(g, j, b)
                    for b in range(2):
                        c["to_pe"].step()
                        c["to_pe"].wait(pe)
                        parts = (0, 1) if g < 2 else (1,)
                        for part in parts:
                            take_aux(part)
                            for i in range(4):
                                ins = nc.tensor.transpose(
                                    aux[:, part, 128 * i:128 * i + 128],
                                    X[:, 1 + b, 256 * i + 128 * part:256 * i + 128 * part + 128], ident)
                            ins.then_inc(aux_ready[part], 1)
                        for part in range(2):
                            aux_free[part].wait(pe)
                        take(b)
                        for i in range(4):
                            t = 4 * b + i
                            has = g < 2
                            kt = (t - 1 if ((t > 0) if g == 0 else (t % 2 == 1)) else t)
                            out = acc[64 * j:64 * j + 64, b, 2, 128 * i:128 * i + 128]
                            if has:
                                nc.tensor.matmul(out, Vt[:, 128 * kt + 64 * j:128 * kt + 64 * j + 64],
                                                 PT[:, 128 * i:128 * i + 128], start=True, stop=False)
                            ins = nc.tensor.matmul(out, Vt[:, 128 * t + 64 * j:128 * t + 64 * j + 64],
                                                   PT[:, 512 + 128 * i:512 + 128 * i + 128],
                                                   start=not has, stop=True)
                        ins.then_inc(ready[b], 1)
                        c["to_pe"].step()
                        c["to_pe"].wait(pe)
                        take_aux(0)
                        nc.tensor.matmul(aux[64 * j:64 * j + 64, 0, :], ones[:, 0:64], DG[:, 0:512],
                                         start=True, stop=True).then_inc(aux_ready[0], 1)
            for j in range(KC):
                wide((j + 1) % 2, (j + 1) % 2, PIECES1, (sems["a_ready"], 8) if j == 0 else None)
            norm_sum(1, KC, PIECES1, slots=(R[:, 8, :], R[:, 9, :]))
            with pe.Fori(0, GROUPS) as i:
                loop = Loop(i, GROUPS, [(unit, FG + 4), (free[0], FG // 2 + 4), (free[1], FG // 2 + 4),
                                        (c["f_ready"], FG)])
                for j in range(FG):
                    wide((j + 1) % 2, (j + 1) % 2, PIECES1, (sems["a_ready"], 16) if j == 0 else None)
                for j in range(4):
                    next_unit()
                    ws = (j + 1) % 2
                    for s in range(2):
                        if j == 0 and s == 0:
                            c["f_ready"].step(FG)
                            c["f_ready"].wait(pe)
                        matrix(s, ws, s * 512, range(4), P, F, F[:, 4:8, :], PIECES1, None,
                               None if s == 0 else sems["unit_done"])
                loop.end()
            norm_sum(0, KC, PIECES1, slots=(R[:, 8, :], R[:, 9, :]))
            a_count = 24
            ws0 = N_UNITS1 % 2
            for l in range(LAYERS):
                u = [ws0]

                def ws():
                    u[0] ^= 1
                    return u[0] ^ 1

                norm_sum(0, KC, PIECES2, slots=(R[:, 8, :], R[:, 9, :]))
                for j in range(8):
                    wide(j % 2, ws(), PIECES2, (sems["a_ready"], a_count) if j == 0 else None)
                a_count += 8
                next_unit()
                w = ws()
                for j in range(4):
                    c["f_ready"].step()
                    c["f_ready"].wait(pe)
                    matrix(j % 2, w, j * 128, [j], P, G, G[:, 4:8, :], PIECES2, None,
                           None if j < 3 else sems["unit_done"])
                for j in range(4):
                    wide(0, ws(), PIECES2)
                    wide(1, ws(), PIECES2)
                    if j == 0:
                        c["f_ready"].step(4)
                        c["f_ready"].wait(pe)
                    next_unit()
                    w = ws()
                    for s in range(2):
                        matrix(s, w, s * 512, range(4), P, G, G[:, 4:8, :], PIECES2, None,
                               None if s == 0 else sems["unit_done"])
                for j in range(8):
                    wide(j % 2, ws(), PIECES2)
                wide(0, ws(), PIECES2)
                for j in range(4):
                    wide(1 - j % 2, ws(), PIECES2)
                norm_sum(1, 6, PIECES2, slots=(R[:, 6, :], R[:, 7, :]))
                norm_sum(0, 2, PIECES2, slots=(R[:, 6, :], R[:, 7, :]))
                for j in range(8):
                    wide(j % 2, ws(), PIECES2)

                def head_key_value(h):
                    next_unit()
                    matrix(1, w_head[0], 6 * P, (6, 7), P, Ah, Al, PIECES2,
                           (sems["a_ready"], a_count + 6) if h == 0 else None)

                def head_query(h):
                    matrix(0, w_head[0], 0, range(6), P, Ah, Al, PIECES2, None, sems["unit_done"])

                def head_sum(s):
                    take(s)
                    for p in range(3):
                        ins = nc.tensor.matmul(acc[:, s, p, 0:348], ones96,
                                               X[:, 5 + s, p * 348:p * 348 + 348], start=True, stop=True)
                    ins.then_inc(ready[s], 1)

                def head_values():
                    for half in range(2):
                        take_aux(half)
                        for t in (range(8) if half == 0 else (8,)):
                            c0 = min(P * t, LASTQ)
                            ins = nc.tensor.transpose(aux[:, half, 64 * (t % 8):64 * (t % 8) + 64],
                                                      R[64:128, 16, c0:c0 + P], ident[64:128, 64:128])
                        ins.then_inc(aux_ready[half], 1)

                def rough_scores(i, qh, kh):
                    s = i % 2
                    nk = min(P * (i + 1), TP)
                    take(s)
                    for p in range(-(-nk // 512)):
                        n = min(512, nk - 512 * p)
                        diag = p == P * i // 512
                        ins = nc.tensor.matmul(acc[:, s, p, 0:n], qh[:, min(P * i, LASTQ):min(P * i, LASTQ) + P],
                                               kh[:, 512 * p:512 * p + n], start=True, stop=not diag)
                    o = P * i - 512 * p
                    n = nk - P * i
                    nc.tensor.matmul(acc[:, s, p, o:o + n], ident_r, causal_r[:, P - n:P],
                                     start=False, stop=True).then_inc(ready[s], 1)

                def scores_t(n, s, b, q2, k2):
                    pc, j = ITEMS[n]
                    tiles = [j] if j is not None else range(TB)
                    for t in tiles:
                        if j is not None:
                            lo, w = item_cols(n)
                            out = acc[:, s, b, 0:w]
                        else:
                            lo, w = P * (TB - 1), TP - P * (TB - 1)
                            out = acc[:, s, b, w * t:w * t + w]
                        c0 = min(P * t, LASTQ)
                        diag = P * t == lo
                        for m, (kt, qt) in enumerate(((0, 0), (0, 1), (1, 0))):
                            ins = nc.tensor.matmul(out, k2[kt][:, c0:c0 + P], q2[qt][:, lo:lo + w],
                                                   start=m == 0, stop=(m == 2 and not diag))
                        if diag:
                            n_ = min(P, w)
                            ins = nc.tensor.matmul(out[:, 0:n_], ident_r, after_r[:, P - n_:P],
                                                   start=False, stop=True)
                    return ins

                def weigh_values(n):
                    pc, j = ITEMS[n]
                    if j in (0, None):
                        take_aux(pc % 2)
                    c["lo_ready"].step()
                    c["lo_ready"].wait(pe)
                    tiles = [j] if j is not None else range(TB)
                    for t in tiles:
                        if j is not None:
                            lo, w = item_cols(n)
                            src = slice(0, w)
                            out = aux[:, pc % 2, lo - 512 * pc:512]
                        else:
                            w = TP - P * (TB - 1)
                            src = slice(w * t, w * t + w)
                            out = aux[:, 0, 0:w]
                        end = j == 4 * pc + 3 if j is not None else t == TB - 1
                        for m, (v, part) in enumerate(((V1, 0), (V1, 1), (V2, 0))):
                            ins = nc.tensor.matmul(out, v[:, t, :], prob(n, part)[:, src],
                                                   start=(t == 0 and m == 0), stop=(end and m == 2))
                    ins.then_inc(aux_ready[pc % 2] if end else sems["pe_read"], 1)

                w_head = [ws()]
                head_key_value(0)
                head_query(0)
                head_sum(1)
                head_sum(0)
                for h in range(MH):
                    more = h + 1 < MH
                    f0 = 4 * (h % 2)
                    q2 = (F[:, f0 + Q0, :], F[:, f0 + Q0 + 1, :])
                    k2 = (F[:, f0 + K0, :], F[:, f0 + K0 + 1, :])
                    c["to_pe"].step()
                    c["to_pe"].wait(pe)
                    for i in range(TB):
                        rough_scores(i, q2[0], k2[0])
                        if h and i == 1:
                            for n in BATCHES[3]:
                                weigh_values(n)
                            weigh_values(12)
                    if more:
                        w_head[0] = ws()
                        head_key_value(h + 1)
                    head_values()
                    if more:
                        head_query(h + 1)
                        head_sum(1)
                    else:
                        for s in range(2):
                            free[s].wait(pe)
                    for half in range(2):
                        take_aux(half)
                    for i in range(TB):
                        n = min(P, TP - P * i)
                        out = aux[32:33, i // 4, P * (i % 4):P * (i % 4) + n] if i < 8 else aux[64:65, 1, 0:n]
                        ins = nc.tensor.matmul(out, S_[:, 16 + i:17 + i], ident[:, P - n:P], start=True, stop=True)
                        if i in (3, 8):
                            ins.then_inc(aux_ready[i // 8], 1)
                    if more:
                        head_sum(0)
                    for half in range(2):
                        aux_free[half].wait(pe)
                    for b, batch in enumerate(BATCHES):
                        s = 1 - b % 2
                        take(s)
                        for o, n in enumerate(batch):
                            ins = scores_t(n, s, o, q2, k2)
                        ins.then_inc(ready[s], 1)
                        if 1 <= b <= 3:
                            for n in BATCHES[b - 1]:
                                weigh_values(n)
                for n in BATCHES[3]:
                    weigh_values(n)
                weigh_values(12)
                a_count += 8
                for j in range(4):
                    next_unit()
                    w = ws()
                    for s in range(2):
                        if j == 0 and s == 0:
                            c["f_ready"].step(4)
                            c["f_ready"].wait(pe)
                        matrix(s, w, s * 512, range(4), P, G, G[:, 4:8, :], PIECES2, None,
                               None if s == 0 else sems["unit_done"])
                for j in range(KC):
                    wide(j % 2, ws(), PIECES2, (sems["a_ready"], a_count) if j == 0 else None)
                a_count += 8
                ws0 = u[0]

        @block.scalar
        def _(act):
            c = counts()
            free = (c["free0"], c["free1"])
            ready = (c["ready0"], c["ready1"])
            aux_free = (c["aux_free0"], c["aux_free1"])
            aux_ready = (c["aux_ready0"], c["aux_ready1"])
            unit = c["unit_done"]

            def do(ins, name="act_step"):
                ins.then_inc(sems[name], 1)
                c[name].step()

            def after(name="act_step"):
                c[name].wait(act)

            def await_unit(s):
                unit.step()
                unit.wait(act)

            def await_ready(s):
                ready[s].step()
                ready[s].wait(act)

            def release(ins, s):
                do(ins, f"free{s}")

            def copy(out, in_, scale=1.0):
                return nc.scalar.activation(out, in_, ACT.Copy, scale=scale)

            def log_and_exp():
                nc.scalar.preload_act_table_set("natural_log_exp_and_others")

            def norm_stats(src, n, width, pieces, s, slots, rs, dim, eps, arrive):
                for j in range(n):
                    arrive(j)
                    if j >= 2:
                        c["sq_free"].step()
                        c["sq_free"].wait(act)
                    do(nc.scalar.activation(slots[j % 2][:, 0:width], src(j), ACT.Square), "sq_ready")
                c["sq_free"].step(1 if n >= 2 else 0)
                await_ready(s)
                release(nc.scalar.activation(cut(rs, pieces), acc_view(s, pieces), ACT.Ln,
                                             scale=1.0 / dim, bias=eps_col(eps, P)), s)
                after(f"free{s}")
                do(nc.scalar.activation(rs[:, 0:width], rs[:, 0:width], ACT.Exp, scale=-0.5), "rs_ready")

            def eps_col(eps, rows):
                col = 60 if eps == 1e-6 else 61
                return S_[0:rows, col:col + 1]

            act.dma_start(X[:, :, META:T2], xT.rearrange("(c p) t -> p c t", p=P)).then_inc(sems["x_in"], 16)
            act.dma_start(R[:, 17, 0:768], lru_w).then_inc(sems["lru_in"], 16)
            act.wait_ge(sems["consts_in"], 32)
            c["to_act"].step()
            c["to_act"].wait(act)
            do(nc.scalar.activation(S_[:, 6:9], V_[:, PARAM_COLS["lam"]:PARAM_COLS["lam"] + 3], ACT.Abs))
            after()
            do(nc.scalar.activation(S_[:, 6:9], S_[:, 6:9], ACT.Exp, scale=-1.0))
            after()
            do(nc.scalar.activation(S_[:, 6:9], S_[:, 6:9], ACT.Ln, bias=1.0), "to_dve")
            log_and_exp()
            act.wait_ge(sems["x_in"], 16)
            norm_stats(lambda j: X[:, j, META:T2], KC, T1, PIECES1, 0, (R[:, 8, :], R[:, 9, :]), R[:, 10, :],
                       DM, 1e-6, lambda j: None)
            for n, what in enumerate(z_order):
                s = n % 2
                await_unit(s)
                if what.startswith("gate"):
                    release(nc.scalar.activation(cut(X[:, n, :], PIECES1), acc_view(s, PIECES1),
                                                 ACT.Sigmoid), s)
                elif what[0] == "a":
                    free[s].step()
                elif what.startswith("lx"):
                    j = int(what[2])
                    release(copy(cut(R[:, 2 + j, LRU_TAPS - 1:], PIECES1), acc_view(s, PIECES1)), s)
                elif what.startswith("lg"):
                    release(copy(cut(R[:, 5 + int(what[2]), :], PIECES1), acc_view(s, PIECES1)), s)
                else:
                    g = int(what[1])
                    d = PATTERNS[g][1]
                    slot = R[:, 8 + 3 * g + "qkv".index(what[0]), 0:T1]
                    if d == 1:
                        release(copy(cut(slot, PIECES1), acc_view(s, PIECES1)), s)
                    else:
                        u = 512 // d
                        to = slot.rearrange("p (r u) -> p u r", r=d)
                        for p in range(2):
                            ins = copy(to[:, u * p:u * p + u, :],
                                       acc[:, s, p, :].rearrange("p (u r) -> p u r", r=d))
                            if p == 0:
                                do(ins)
                        release(ins, s)
            for j in range(3):
                if j:
                    act.wait_ge(sems["a_ready"], 8 + j)
                await_ready(1)
                release(nc.scalar.activation(cut(X[:, 7, :], PIECES1), acc_view(1, PIECES1), ACT.Sigmoid,
                                             bias=param("lba", j)), 1)
                await_ready(0)
                release(nc.scalar.activation(cut(X[:, 0, :], PIECES1), acc_view(0, PIECES1), ACT.Sigmoid,
                                             bias=param("lbx", j)), 0)
                if j == 0:
                    c["to_act"].step()
                    c["to_act"].wait(act)
                do(nc.scalar.activation(R[:, 1, 0:T1], R[:, 5 + j, 0:T1], ACT.Gelu_apprx_tanh), "to_dve")
                c["to_act"].step()
                c["to_act"].wait(act)
                do(nc.scalar.activation(R[:, 0, 0:T1], X[:, 1, 0:T1], ACT.Exp, scale=-1.0))
                do(nc.scalar.activation(R[:, 2, 0:T1], X[:, 1, 0:T1], ACT.Tanh), "to_dve")
                c["to_act"].step()
                c["to_act"].wait(act)
                do(nc.scalar.activation(R[:, 3, 0:T1], R[:, 2, 0:T1], ACT.Sqrt), "to_dve")
            log_and_exp()
            await_ready_only = ready[0]
            await_ready_only.step()
            free[0].step()
            await_ready(1)
            release(nc.scalar.activation(cut(R[:, 4, :], PIECES1), acc_view(1, PIECES1), ACT.Ln,
                                         scale=1.0 / 256, bias=eps_col(1e-5, P)), 1)
            after("free1")
            do(nc.scalar.activation(R[:, 4, 0:T1], R[:, 4, 0:T1], ACT.Exp, scale=-0.5), "rs_ready")
            for j in range(2):
                c["to_act"].step()
                c["to_act"].wait(act)
                do(nc.scalar.activation(R[:, 2 + j, 0:T1], X[:, 2 + j, 0:T1], ACT.Sigmoid), "to_dve")
            log_and_exp()
            act.wait_ge(sems["a_ready"], 8 + 3)
            act.dma_start(X_[:, 6 * TP:6 * TP + 6 * 256], bands).then_inc(sems["bands_in"], 16)
            for g in range(3):
                for half in range(2):
                    aux_ready[half].step()
                    aux_ready[half].wait(act)
                    if half == 0 and g:
                        ready[1].wait(act)
                    do(copy(X[:, 0, 512 * half:512 * half + 512], aux[:, half, :]), f"aux_free{half}")
                for j in range(2):
                    for b in range(2):
                        ready[b].step()
                        free[b].step()

                    def exps(b):
                        c["to_act"].step()
                        c["to_act"].wait(act)
                        lo, hi = (0, 256) if g < 2 else (128, 256)
                        for i in range(4):
                            do(nc.scalar.activation(X[:, 1 + b, 256 * i + lo:256 * i + hi],
                                                    X[:, 1 + b, 256 * i + lo:256 * i + hi], ACT.Exp,
                                                    bias=S_[:, 16 + 4 * b + i:17 + 4 * b + i],
                                                    accum_out=S_[:, 24 + 4 * b + i:25 + 4 * b + i]))
                        after()
                        do(nc.scalar.activation(S_[:, 32 + 4 * b:36 + 4 * b], S_[:, 24 + 4 * b:28 + 4 * b],
                                                ACT.Ln), "to_dve")

                    exps(0)
                    exps(1)
                    for b in range(2):
                        if not (g == 0 and j == 0 and b == 0):
                            ready[1 - b].wait(act)
                        for part in ((0, 1) if g < 2 else (1,)):
                            aux_ready[part].step()
                            aux_ready[part].wait(act)
                            do(copy(X[:, 3, 512 * part:512 * part + 512], aux[:, part, :]), f"aux_free{part}")
                        await_ready(b)
                        rows = slice(64 * j, 64 * j + 64)
                        d = PATTERNS[g][1]
                        nat = R[rows, g, 0:T1]
                        src = acc[rows, b, 2, :]
                        if d == 1:
                            release(copy(nat[:, 512 * b:512 * b + 512], src), b)
                        else:
                            release(copy(nat.rearrange("p (u r) -> p r u", r=d)[:, b * d // 2:(b + 1) * d // 2, :],
                                         src.rearrange("p (r u) -> p r u", r=d // 2)), b)
                        aux_ready[0].step()
                        aux_free[0].step()
            c["to_act"].step()
            c["to_act"].wait(act)
            act.dma_start(X[:, :, META:T2], xT.rearrange("(c p) t -> p c t", p=P)).then_inc(sems["xre_in"], 16)
            for g in range(3):
                ins = nc.scalar.activation(R[:, 3 + g, 0:T1], R[:, 3 + g, 0:T1], ACT.Exp)
                do(ins, "to_dve" if g == 2 else "act_step")

            def updated(s):
                unit.step()
                free[s].step()
                free[s].wait(act)

            norm_stats(lambda j: X[:, j, META:T2], KC, T1, PIECES1, 1, (R[:, 8, :], R[:, 9, :]), R[:, 10, :],
                       DM, 1e-6, lambda j: updated((j + 1) % 2))
            act.dma_start(X[:, :, 0:META], metaT.rearrange("(c p) t -> p c t", p=P)).then_inc(sems["meta_in"], 16)
            act.wait_ge(sems["a_ready"], 24)
            act.dma_start(R[:, 8, META:T2].bitcast(I32), pos).then_inc(sems["pos_in"], 16)
            c["to_act"].step()
            c["to_act"].wait(act)
            do(nc.scalar.activation(R[:, 16, 0:TP], R[:, 16, 0:TP], ACT.Sin))
            after()
            rot = slice(ROPE, 2 * ROPE)
            do(nc.scalar.activation(R[rot, 16, 0:TP], R[rot, 17, 0:TP], ACT.Sin, scale=param("sign", 0, rot)),
               "act_step")
            after()
            act.dma_start(spill_t, R[:, 16, 0:TP]).then_inc(sems["t_spilled"], 16)
            with act.Fori(0, GROUPS) as i:
                loop = Loop(i, GROUPS, [(unit, FG + 4), (free[0], FG // 2 + 4), (free[1], FG // 2 + 4),
                                        (ready[0], 4)])
                for j in range(FG):
                    s = (j + 1) % 2
                    await_unit(s)
                    release(nc.scalar.activation(cut(R[:, 12 + j, :], PIECES1), acc_view(s, PIECES1),
                                                 ACT.Relu), s)
                unit.step(4)
                ready[0].step(4)
                free[0].step(4)
                free[1].step(4)
                loop.end()

            def both_free():
                for s in range(2):
                    free[s].wait(act)

            log_and_exp()
            both_free()
            norm_stats(lambda j: X[:, j, META:T2], KC, T1, PIECES1, 0, (R[:, 8, :], R[:, 9, :]), R[:, 10, :],
                       DM, 1e-6, lambda j: None)

            def by_signal(j):
                c["to_act"].step()
                c["to_act"].wait(act)

            for l in range(LAYERS):
                last = l == LAYERS - 1
                if l == 0:
                    act.wait_ge(sems["meta_in"], 16)
                norm_stats(lambda j: X[:, j, :], KC, TP, PIECES2, 0, (R[:, 8, :], R[:, 9, :]), R[:, 10, :],
                           DM, 1e-6, by_signal if l == 0 else lambda j: updated(j % 2))
                act.dma_start(spill_x, X_[:]).then_inc(sems["spilled"], 16)
                act.wait_ge(sems["t_spilled"], 16)
                act.dma_start(R[:, 17, 0:TP], spill_t).then_inc(sems["t_in"], 16)
                for j in range(4):
                    await_unit(j % 2)
                    if j == 0:
                        by_signal(0)
                    release(copy(cut(R[:, j, 16:], PIECES2), acc_view(j % 2, PIECES2)), j % 2)
                for j in range(4):
                    await_unit(j % 2)
                    do(nc.scalar.activation(cut(R[:, 4 + j, :], PIECES2), acc_view(j % 2, PIECES2),
                                            ACT.Sigmoid), "to_dve")
                    free[j % 2].step()
                for j in range(4):
                    if j < 3:
                        ready[j % 2].step()
                    free[j % 2].step()
                unit.step()
                for j in range(4):
                    for s in range(2):
                        await_unit(s)
                        if j:
                            free[s].wait(act)
                        release(nc.scalar.activation(cut(R[:, s, :], PIECES2), acc_view(s, PIECES2),
                                                     ACT.Sigmoid), s)
                    unit.step()
                    ready[0].step()
                    for s in range(2):
                        free[s].step()
                for s in range(2):
                    free[s].wait(act)
                act.dma_start(spill_m, X_[:]).then_inc(sems["m_spilled"], 16)
                for j in range(8):
                    await_unit(j % 2)
                    release(copy(cut(R[:, 8 + j, :], PIECES2), acc_view(j % 2, PIECES2)), j % 2)
                await_unit(0)
                act.wait_ge(sems["m_spilled"], 16 * (l + 1))
                rr = slice(0, 2 * ROPE)
                do(nc.scalar.activation(cut(X[rr, 6, :], PIECES2), acc_view(0, PIECES2, rr), ACT.Square), "to_dve")
                free[0].step()
                for j in range(4):
                    s = 1 - j % 2
                    await_unit(s)
                    do(nc.scalar.activation(cut(X[:, j, :], PIECES2), acc_view(s, PIECES2), ACT.Sigmoid),
                       "to_dve")
                    free[s].step()
                log_and_exp()
                norm_stats(lambda j: R[:, 8 + j, 0:TP], 6, TP, PIECES2, 1, (R[:, 6, :], R[:, 7, :]), R[:, 4, :],
                           QR, 1e-6, lambda j: None)
                norm_stats(lambda j: R[:, 14 + j, 0:TP], 2, TP, PIECES2, 0, (R[:, 6, :], R[:, 7, :]), R[:, 5, :],
                           KVR, 1e-6, lambda j: None)
                by_signal(0)
                for j in range(8):
                    await_unit(j % 2)
                    release(nc.scalar.activation(cut(R[:, j, :], PIECES2), acc_view(j % 2, PIECES2),
                                                 ACT.Sigmoid), j % 2)
                by_signal(0)
                act.dma_start(spill_g, R[:, 0:8, 0:TP]).then_inc(sems["g_spilled"], 16)

                top, low = slice(64, 128), slice(0, 64)

                def head_key_squares(values):
                    await_ready(1)
                    do(nc.scalar.activation(cut(X[top, 6, :], PIECES2), acc_view(1, PIECES2, top), ACT.Square))
                    do(copy(cut(X[top, 7, :], PIECES2), acc_view(1, PIECES2, top), param(f"kn_{l}", 0, top)))
                    if values:
                        head_values()
                    release(copy(cut(R[top, 16, :], PIECES2), acc_view(1, PIECES2, low)), 1)

                def head_query_squares():
                    await_unit(0)
                    do(nc.scalar.activation(cut(X[:, 5, :], PIECES2), acc_view(0, PIECES2), ACT.Square), "to_dve")
                    free[0].step()

                def head_scale(s, rs):
                    await_ready(s)
                    release(nc.scalar.activation(cut(rs, PIECES2), acc_view(s, PIECES2), ACT.Ln,
                                                 scale=1.0 / QKD, bias=eps_col(1e-6, P)), s)
                    after(f"free{s}")
                    do(nc.scalar.activation(rs, rs, ACT.Exp, scale=-0.5), "rs_ready")

                def head_values():
                    for half in range(2):
                        aux_ready[half].step()
                        aux_ready[half].wait(act)
                        if half == 0:
                            do(copy(V1[:, 0:8, 0:64], aux[:, 0, :].rearrange("p (t v) -> p t v", v=64)), "to_dve")
                        else:
                            do(copy(V1[:, 8, 0:64], aux[:, 1, 0:64], param("rows20")), "to_dve")
                        aux_free[half].step()

                def head_inverse(h, pc):
                    aux_ready[pc % 2].step()
                    aux_ready[pc % 2].wait(act)
                    if pc == 1:
                        aux_free[0].wait(act)
                    rows = slice(64 * (h % 2), 64 * (h % 2) + 64)
                    u = head_inv(rows, pc)
                    do(nc.scalar.activation(u, aux[64:128, pc % 2, 0:512 if pc < 2 else TP - 1024], ACT.Ln))
                    after()
                    do(nc.scalar.activation(u, u, ACT.Exp, scale=-1.0), "inv_ready")
                    aux_free[pc % 2].step()

                log_and_exp()
                by_signal(0)
                head_key_squares(False)
                head_query_squares()
                head_scale(1, rsk)
                head_scale(0, X[:, 5, :])
                items_done = l * MH * len(ITEMS)
                for h in range(MH):
                    more = h + 1 < MH
                    for i in range(TB):
                        ready[i % 2].step()
                        free[i % 2].step()
                    if h:
                        head_inverse(h - 1, 1)
                        head_inverse(h - 1, 2)
                    if more:
                        head_key_squares(True)
                        head_query_squares()
                        head_scale(1, rsk)
                    else:
                        head_values()
                    qh = F[32:33, 4 * (h % 2) + Q0, 0:TP]
                    for half in range(2):
                        aux_ready[half].step()
                        aux_ready[half].wait(act)
                        do(copy(qh[:, 512 * half:512 * half + 512], aux[32:33, half, :]),
                           "aux_free0" if half == 0 else "act_step")
                    do(copy(qh[:, 1024:TP], aux[64:65, 1, 0:TP - 1024]), "aux_free1")
                    if more:
                        head_scale(0, X[:, 5, :])
                    for b, batch in enumerate(BATCHES):
                        s = 1 - b % 2
                        await_ready(s)
                        for o, n in enumerate(batch):
                            if n == PRING + 3:
                                act.wait_ge(sems["aux_ready0"], aux_ready[0].value() + 1)
                            elif n >= PRING:
                                before = sum(1 for m in range(n - PRING + 1) if m != 3)
                                act.wait_ge(sems["pe_read"], 10 * (l * MH + h) + before)
                            if items_done >= 2:
                                act.wait_ge(sems["lo_ready"], items_done - 1)
                            w = item_cols(n)[1] if ITEMS[n][1] is not None else TB * (TP - P * (TB - 1))
                            src = acc[:, s, o, 0:w]
                            p32 = R[:, 18, 512 * (items_done % 2):512 * (items_done % 2) + w]
                            do(nc.scalar.activation(p32, src, ACT.Exp))
                            ins = nc.scalar.activation(prob(n, 0)[:, 0:w], src, ACT.Exp)
                            do(ins, f"free{s}" if o == len(batch) - 1 else "to_dve")
                            items_done += 1
                        if b == 3:
                            head_inverse(h, 0)
                head_inverse(MH - 1, 1)
                head_inverse(MH - 1, 2)
                by_signal(0)
                act.dma_start(R[:, 0:8, 0:TP], spill_g.rearrange("p (c t) -> p c t", c=8)) \
                   .then_inc(sems["sg_in"], 16)
                by_signal(0)
                act.dma_start(X_[:], spill_m).then_inc(sems["mg_in"], 16)
                for j in range(4):
                    unit.step()
                    ready[0].step()
                    free[0].step()
                    free[1].step()
                by_signal(0)
                act.wait_ge(sems["spilled"], 16 * (l + 1))
                act.dma_start(X_[:], spill_x).then_inc(sems["xre_in"], 16)
                if last:
                    for j in range(KC):
                        updated(j % 2)
                        act.dma_start(outT[P * j:P * j + P, :], X[:, j, META:T2]).then_inc(sems["stored"], 16)
                    act.wait_ge(sems["stored"], 16 * KC)

        @block.vector
        def _(dve):
            c = counts()
            free = (c["free0"], c["free1"])
            ready = (c["ready0"], c["ready1"])
            aux_free = (c["aux_free0"], c["aux_free1"])
            aux_ready = (c["aux_ready0"], c["aux_ready1"])
            unit = c["unit_done"]
            vec = nc.vector

            def do(ins, name="dve_step"):
                ins.then_inc(sems[name], 1)
                c[name].step()
                c[name].wait(dve)

            def await_unit():
                unit.step()
                unit.wait(dve)

            def await_ready(s):
                ready[s].step()
                ready[s].wait(dve)

            def await_free(s):
                free[s].step()
                free[s].wait(dve)

            def from_act():
                c["to_dve"].step()
                c["to_dve"].wait(dve)

            def split(src, hi, lo, name):
                do(vec.tensor_copy(hi, src))
                do(vec.tensor_tensor(lo, src, hi.bitcast(F32), ALU.subtract), name)

            def normalise(n, src, gain, rs, y, width):
                c["rs_ready"].step()
                c["rs_ready"].wait(dve)
                for j in range(n):
                    do(vec.scalar_tensor_tensor(y[:, 0:width], src(j), param(gain, j), rs[:, 0:width],
                                                ALU.mult, ALU.mult))
                    split(y[:, 0:width], Ah[:, j, 0:width], Al[:, j, 0:width], "a_ready")

            dve.wait_ge(sems["consts_in"], 32)
            do(vec.memset(S_[:, 0:62], 1e-6))
            do(vec.memset(S_[:, 61:62], 1e-5), "to_act")
            do(vec.tensor_scalar(S_[:, 9:12], V_[:, PARAM_COLS["lam"]:PARAM_COLS["lam"] + 3], -1.0, 0.0,
                                 ALU.mult, ALU.max))
            from_act()
            do(vec.tensor_tensor(S_[:, 9:12], S_[:, 9:12], S_[:, 6:9], ALU.add))
            do(vec.tensor_scalar_mul(S_[:, 9:12], S_[:, 9:12], 8.0))
            do(vec.memset(R[:, 0:2, 0:CONV_TAPS - 1], 0.0))
            do(vec.memset(R[:, 2:5, 0:LRU_TAPS - 1], 0.0))
            dve.wait_ge(sems["x_in"], 16)
            ready[0].step()
            free[0].step()
            normalise(KC, lambda j: X[:, j, META:T2], "norm1", R[:, 10, :], R[:, 11, :], T1)
            for n in range(2):
                unit.step()
                await_free(n)
            for n in range(2):
                await_unit()
                do(vec.tensor_tensor(cut(R[:, n, CONV_TAPS - 1:], PIECES1), acc_view(n, PIECES1),
                                     cut(X[:, n, :], PIECES1), ALU.mult), f"free{n}")

            def convolve(out, src, taps, w, b, name):
                do(vec.tensor_scalar(out, src[:, 0:T1], V_[:, w:w + 1], b, ALU.mult, ALU.add))
                for k in range(1, taps):
                    do(vec.scalar_tensor_tensor(out, src[:, k:k + T1], V_[:, w + k:w + k + 1], out,
                                                ALU.mult, ALU.add), name if k == taps - 1 else "dve_step")

            for n in range(4, 7):
                unit.step()
                await_free(n % 2)
                j = n - 4
                convolve(X[:, 4 + j, 0:T1], R[:, 2 + j, :], LRU_TAPS, PARAM_COLS["lcw"] + LRU_TAPS * j,
                         param("lcb", j), "to_pe")
            for j in range(2):
                convolve(X[:, 2 + j, 0:T1], R[:, j, :], CONV_TAPS, PARAM_COLS["cdw"] + CONV_TAPS * j,
                         param("cdb", j), "dve_step" if j == 0 else "to_act")
            for n in range(7, UNITS_Z):
                unit.step()
                free[n % 2].step()
            for s in range(2):
                free[s].wait(dve)
            full = slice(0, T1)
            for j in range(3):
                ready[1].step()
                await_free(1)
                do(vec.tensor_scalar(X[:, 1, full], X[:, 7, full], S_[:, 9 + j:10 + j], None, ALU.mult), "to_act")
                ready[0].step()
                await_free(0)
                do(vec.tensor_tensor(X[:, 0, full], X[:, 0, full], X[:, 4 + j, full], ALU.mult))
                from_act()
                from_act()
                do(vec.tensor_scalar_add(X[:, 1, full], R[:, 2, full], 1.0))
                do(vec.reciprocal(X[:, 1, full], X[:, 1, full]))
                do(vec.scalar_tensor_tensor(R[:, 2, full], R[:, 2, full], 2.0, X[:, 1, full], ALU.mult, ALU.mult),
                   "to_act")
                from_act()
                do(vec.tensor_tensor(X[:, 0, full], X[:, 0, full], R[:, 3, full], ALU.mult))
                do(vec.tensor_tensor_scan(X[:, 1, full], R[:, 0, full], X[:, 0, full], 0.0, ALU.mult, ALU.add))
                do(vec.tensor_tensor(R[:, 4, full], R[:, 1, full], X[:, 1, full], ALU.mult))
                split(R[:, 4, full], Ah[:, j, full], Al[:, j, full], "a_ready")
                if j == 2:
                    do(vec.tensor_copy(S_[:, 40:41], S_[:, 60:61]), "to_pe")
            await_ready(0)
            for j in range(2):
                do(vec.scalar_tensor_tensor(cut(X[:, 2 + j, :], PIECES1), acc_view(0, PIECES1), -1.0 / 256,
                                            cut(X[:, 2 + j, :], PIECES1), ALU.mult, ALU.add),
                   "dve_step" if j == 0 else "free0")
            for j in range(2):
                do(vec.tensor_tensor(R[:, 2 + j, full], X[:, 2 + j, full], X[:, 2 + j, full], ALU.mult),
                   "dve_step" if j == 0 else "to_pe")
            ready[1].step()
            free[1].step()
            c["rs_ready"].step()
            c["rs_ready"].wait(dve)
            for j in range(2):
                y = X[:, 2 + j, full]
                do(vec.scalar_tensor_tensor(y, y, param("clg", j), R[:, 4, full], ALU.mult, ALU.mult))
                do(vec.tensor_scalar(y, y, param("clb", j), None, ALU.add), "to_act")
            for j in range(2):
                y = X[:, 2 + j, full]
                from_act()
                do(vec.tensor_tensor(y, y, R[:, 2 + j, full], ALU.mult))
                split(y, Ah[:, 3 + j, full], Al[:, 3 + j, full], "a_ready")
            dve.wait_ge(sems["bands_in"], 16)
            pend = []

            def take_lse():
                g, j, b = pend.pop()
                aux_ready[0].step()
                aux_ready[0].wait(dve)
                rows = slice(64 * j, 64 * j + 64)
                d = PATTERNS[g][1]
                nat = R[rows, 3 + g, full]
                src = aux[rows, 0, :]
                if d == 1:
                    ins = vec.tensor_copy(nat[:, 512 * b:512 * b + 512], src)
                else:
                    ins = vec.tensor_copy(nat.rearrange("p (u r) -> p r u", r=d)[:, b * d // 2:(b + 1) * d // 2, :],
                                          src.rearrange("p (r u) -> p r u", r=d // 2))
                do(ins, "aux_free0")

            for g in range(3):
                lo = 0 if g < 2 else 128
                for half in range(2):
                    aux_ready[half].step()
                    aux_free[half].step()
                for j in range(2):
                    def stats(b):
                        await_ready(b)
                        pb = X[:, 1 + b, 0:1024].rearrange("p (i k) -> p i k", k=256)
                        if pend:
                            pass
                        sc = acc[:, b, 0:2, :].rearrange("p a (c k) -> p (a c) k", c=2)
                        h = 2 * g + j
                        band = X_[:, 6 * TP + 256 * h + lo:6 * TP + 256 * h + 256].unsqueeze(1) \
                            .to_broadcast([P, 4, 256 - lo])
                        do(vec.scalar_tensor_tensor(pb[:, :, lo:256], sc[:, :, lo:256], HD ** -0.5, band,
                                                    ALU.mult, ALU.add), f"free{b}")
                        if g == 0 and b == 0:
                            do(vec.memset(pb[:, 0:1, 0:128], NEG))
                        if g == 1:
                            do(vec.memset(X[:, 1 + b, 0:1024].rearrange("p (a x) -> p a x", x=512)[:, :, 0:128],
                                          NEG))
                        do(vec.tensor_reduce(S_[:, 16 + 4 * b:20 + 4 * b], pb[:, :, lo:256], AX, ALU.max,
                                             negate=True), "to_act")

                    def finish(b):
                        from_act()
                        pb = X[:, 1 + b, 0:1024].rearrange("p (i k) -> p i k", k=256)[:, :, lo:256]
                        do(vec.reciprocal(S_[:, 44 + 4 * b:48 + 4 * b], S_[:, 24 + 4 * b:28 + 4 * b]))
                        rl = S_[:, 44 + 4 * b:48 + 4 * b].unsqueeze(2).to_broadcast([P, 4, 256 - lo])
                        do(vec.tensor_tensor(pb, pb, rl, ALU.mult), "to_pe")
                        lse = S_[:, 32 + 4 * b:36 + 4 * b]
                        do(vec.tensor_tensor(lse, lse, S_[:, 16 + 4 * b:20 + 4 * b], ALU.subtract))
                        if pend:
                            take_lse()
                        do(vec.tensor_tensor(X[:, 5, 0:512].rearrange("p (i q) -> p i q", q=P),
                                             ident.unsqueeze(1).to_broadcast([P, 4, P]),
                                             lse.unsqueeze(2).to_broadcast([P, 4, P]), ALU.mult), "to_pe")
                        pend.append((g, j, b))

                    stats(0)
                    stats(1)
                    for b in range(2):
                        finish(b)
                        for part in ((0, 1) if g < 2 else (1,)):
                            aux_ready[part].step()
                            aux_free[part].step()
                        ready[b].step()
                        free[b].step()
                    take_lse()
            for b in range(2):
                free[b].wait(dve)
            top = R[:, 6, full]
            do(vec.tensor_tensor(top, R[:, 3, full], R[:, 4, full], ALU.max))
            do(vec.tensor_tensor(top, top, R[:, 5, full], ALU.max))
            for g in range(3):
                do(vec.tensor_tensor(R[:, 3 + g, full], R[:, 3 + g, full], top, ALU.subtract),
                   "to_act" if g == 2 else "dve_step")
            from_act()
            do(vec.tensor_tensor(top, R[:, 3, full], R[:, 4, full], ALU.add))
            do(vec.tensor_tensor(top, top, R[:, 5, full], ALU.add))
            do(vec.reciprocal(top, top))
            for g in range(3):
                do(vec.tensor_tensor(R[:, 3 + g, full], R[:, 3 + g, full], top, ALU.mult))
                do(vec.tensor_tensor(R[:, g, full], R[:, g, full], R[:, 3 + g, full], ALU.mult))
                split(R[:, g, full], Ah[:, 5 + g, full], Al[:, 5 + g, full], "a_ready")

            def add_to_residual(j, s, pieces, c0, width):
                x = X[:, j, c0:c0 + width].rearrange("p (a b) -> p a b", a=pieces[0])
                do(vec.tensor_tensor(x, acc_view(s, pieces), x, ALU.add), f"free{s}")

            dve.wait_ge(sems["xre_in"], 16)
            for j in range(KC):
                await_unit()
                add_to_residual(j, (j + 1) % 2, PIECES1, META, T1)
            ready[1].step()
            free[1].step()
            normalise(KC, lambda j: X[:, j, META:T2], "norm2", R[:, 10, :], R[:, 11, :], T1)
            dve.wait_ge(sems["pos_in"], 16)
            do(vec.tensor_scalar(R[:, 9, META:T2], R[:, 8, META:T2].bitcast(I32), float(META), None, ALU.add))
            do(vec.tensor_copy(R[:, 9, 0:META], C_[:, 704:720]))
            do(vec.memset(R[:, 9, T2:TP], 0.0))
            ang, k, sn, cs = R[:, 9, 0:TP], R[:, 8, 0:TP], R[:, 17, 0:TP], R[:, 16, 0:TP]
            magic, pi = 12582912.0, 3.1415925
            do(vec.tensor_scalar(ang, ang, param("freq"), None, ALU.mult))
            do(vec.tensor_scalar(k, ang, float(1 / (2 * np.pi)), magic, ALU.mult, ALU.add))
            do(vec.tensor_scalar_add(k, k, -magic))
            c1, c2 = 6.28125, 2029 / 2 ** 20
            c3 = float(2 * np.pi - c1 - c2)
            do(vec.scalar_tensor_tensor(ang, k, -c1, ang, ALU.mult, ALU.add))
            do(vec.scalar_tensor_tensor(ang, k, -c2, ang, ALU.mult, ALU.add))
            do(vec.scalar_tensor_tensor(ang, k, -c3, ang, ALU.mult, ALU.add))
            do(vec.tensor_scalar(sn, ang, pi, -pi, ALU.min, ALU.max))
            do(vec.tensor_scalar_add(ang, ang, float(np.pi / 2)))
            do(vec.tensor_scalar(k, ang, float(np.pi), float(-2 * np.pi), ALU.is_gt, ALU.mult))
            do(vec.tensor_tensor(ang, ang, k, ALU.add))
            do(vec.tensor_scalar(cs, ang, pi, -pi, ALU.min, ALU.max), "to_act")
            with dve.Fori(0, GROUPS) as i:
                loop = Loop(i, GROUPS, [(unit, FG + 4), (free[0], FG // 2 + 4), (free[1], FG // 2 + 4),
                                        (ready[0], 4), (c["f_ready"], FG), (c["dve_step"], 2 * FG)])
                for j in range(FG):
                    unit.step()
                    await_free((j + 1) % 2)
                    do(vec.tensor_tensor(R[:, 11, full], R[:, 12 + j, full], R[:, 12 + j, full], ALU.mult))
                    split(R[:, 11, full], F[:, j, full], F[:, 4 + j, full], "f_ready")
                for j in range(KC):
                    if j % 2:
                        await_unit()
                    else:
                        await_ready(0)
                    add_to_residual(j, j % 2, PIECES1, META, T1)
                loop.end()
            ready[0].step()
            free[0].step()
            c["rs_ready"].step()
            c["rs_ready"].wait(dve)
            do(vec.memset(X[:, :, T2:TP], 0.0))
            for j in range(KC):
                do(vec.scalar_tensor_tensor(X[:, j, META:T2], X[:, j, META:T2], param("final", j),
                                            R[:, 10, full], ALU.mult, ALU.mult), "to_act")
            wide = slice(0, TP)
            dve.wait_ge(sems["meta_in"], 16)
            for l in range(LAYERS):
                last = l == LAYERS - 1
                ready[0].step()
                free[0].step()
                normalise(KC, lambda j: X[:, j, :], f"n2_{l}", R[:, 10, :], R[:, 11, :], TP)
                do(vec.memset(R[:, 0:4, 0:16], 0.0), "to_act")
                dve.wait_ge(sems["spilled"], 16 * (l + 1))
                for g in range(4):
                    unit.step()
                    await_free(g % 2)
                    u = R[:, g, :]
                    bufs = (X_[:, 4 * TP:4 * TP + 1060], X_[:, 6 * TP:6 * TP + 1060])
                    cur, first = u, 0
                    for k in range(g + 1):
                        first += 2 ** k
                        to = bufs[k % 2]
                        do(vec.tensor_tensor(to[:, first:1060], cur[:, first:1060],
                                             cur[:, first - 2 ** k:1060 - 2 ** k], ALU.add))
                        cur = to
                    w = POOLW[g]
                    y = X[:, 2, :]
                    do(vec.scalar_tensor_tensor(y, cur[:, 16:1060], 1.0 / w, u[:, 16:1060], ALU.mult,
                                                ALU.subtract))
                    do(vec.tensor_tensor(y[:, 0:16], cur[:, 16:32], C_[:, 640 + 16 * g:656 + 16 * g], ALU.mult))
                    do(vec.tensor_tensor(y[:, 0:16], y[:, 0:16], u[:, 16:32], ALU.subtract))
                    split(y, G[:, g, wide], G[:, 4 + g, wide], "f_ready")
                for j in range(4):
                    await_unit()
                    from_act()
                    z = R[:, 4 + j, wide]
                    do(vec.tensor_tensor(cut(z, PIECES2), acc_view(j % 2, PIECES2), cut(z, PIECES2), ALU.mult),
                       f"free{j % 2}")
                for j in range(4):
                    if j < 3:
                        await_ready(j % 2)
                    else:
                        await_unit()
                    y = X[:, 2, :]
                    do(vec.scalar_tensor_tensor(cut(y, PIECES2), acc_view(j % 2, PIECES2), param(f"ps_{l}", j),
                                                cut(R[:, 4 + j, :], PIECES2), ALU.mult, ALU.mult), f"free{j % 2}")
                    split(y, G[:, j, wide], G[:, 4 + j, wide], "f_ready")
                for j in range(4):
                    for s in range(2):
                        unit.step()
                        await_free(s)
                    for s in range(2):
                        if s == 0:
                            await_ready(0)
                        else:
                            await_unit()
                        do(vec.tensor_tensor(cut(X[:, 2 * j + s, :], PIECES2), acc_view(s, PIECES2),
                                             cut(R[:, s, :], PIECES2), ALU.mult), f"free{s}")
                for j in range(8):
                    unit.step()
                    free[j % 2].step()
                unit.step()
                from_act()
                dve.wait_ge(sems["t_in"], 16 * (l + 1))
                dve.wait_ge(sems["m_spilled"], 16 * (l + 1))
                rr, rope = slice(0, 2 * ROPE), slice(0, ROPE)
                do(vec.scalar_tensor_tensor(cut(X[rr, 4, :], PIECES2), acc_view(0, PIECES2, rr),
                                            param(f"kn_{l}", 0, rr), cut(R[rr, 17, :], PIECES2),
                                            ALU.mult, ALU.mult), "free0")
                free[0].step(0)
                do(vec.tensor_copy(X[rope, 7, :], X[ROPE:2 * ROPE, 4, :]))
                do(vec.tensor_tensor(R[rope, 16, 0:TP], X[rope, 4, :], X[rope, 7, :], ALU.add))
                do(vec.tensor_scalar(R[:, 17, 0:TP], R[:, 17, 0:TP], param(f"qn_{l}"), QKD ** -0.5,
                                     ALU.mult, ALU.mult))
                for j in range(4):
                    s = 1 - j % 2
                    await_unit()
                    from_act()
                    z = X[:, j, :]
                    do(vec.tensor_tensor(cut(z, PIECES2), acc_view(s, PIECES2), cut(z, PIECES2), ALU.mult),
                       f"free{s}")
                for s, c0, n, gain, rs in ((1, 0, 6, f"qa_{l}", R[:, 4, wide]), (0, 6, 2, f"kva_{l}", R[:, 5, wide])):
                    ready[s].step()
                    free[s].step()
                    c["rs_ready"].step()
                    c["rs_ready"].wait(dve)
                    for j in range(n):
                        y = R[:, 8 + c0 + j, wide]
                        do(vec.scalar_tensor_tensor(y, y, param(gain, j), rs, ALU.mult, ALU.mult),
                           "to_act" if (s == 0 and j == 1) else "dve_step")
                for j in range(8):
                    unit.step()
                    await_free(j % 2)
                do(vec.tensor_copy(S_[:, 40:41], S_[:, 60:61]), "to_act")
                for j in range(8):
                    split(R[:, 8 + j, wide], Ah[:, j, :], Al[:, j, :], "a_ready")
                dve.wait_ge(sems["g_spilled"], 16 * (l + 1))
                do(vec.tensor_copy(V1[:, 0:8, 64:128], ones[:, 0:64].unsqueeze(1).to_broadcast([P, 8, 64])))
                do(vec.tensor_scalar(V1[:, 8, 64:128], ones[:, 0:64], param("rows20"), None, ALU.mult))
                do(vec.tensor_scalar(V2[:, 0:8, 64:128], ones[:, 0:64].unsqueeze(1).to_broadcast([P, 8, 64]), 0.0,
                                     None, ALU.mult))
                do(vec.tensor_scalar(V2[:, 8, 64:128], ones[:, 0:64], 0.0, None, ALU.mult))
                do(vec.tensor_copy(ident_r, ident))
                do(vec.tensor_copy(causal_r, C_[:, 384:512]))
                do(vec.tensor_copy(after_r, C_[:, 512:640]))
                do(vec.memset(X[32:64, 7, :], 0.0))
                do(vec.memset(X[32:33, 7, :], 1.0), "to_act")
                top = slice(64, 128)

                def head_table():
                    unit.step()
                    from_act()
                    do(vec.tensor_tensor(cut(X[:, 4, :], PIECES2), acc_view(0, PIECES2), cut(R[:, 17, :], PIECES2),
                                         ALU.mult), "free0")
                    do(vec.tensor_copy(X[rope, 7, :], X[ROPE:2 * ROPE, 4, :]))
                    do(vec.tensor_tensor(X[rope, 4, :], X[rope, 4, :], X[rope, 7, :], ALU.add))

                def head_query(h):
                    f = 4 * (h % 2)
                    c["rs_ready"].step(2)
                    c["rs_ready"].wait(dve)
                    do(vec.scalar_tensor_tensor(X[:, 4, :], X[:, 4, :], param("rows96"), X[:, 5, :],
                                                ALU.mult, ALU.mult))
                    split(X[:, 4, :], F[:, f + Q0, 0:TP], F[:, f + Q0 + 1, 0:TP], "dve_step")

                def head_key(h):
                    f = 4 * (h % 2)
                    do(vec.tensor_tensor(X[rope, 7, :], R[rope, 16, 0:TP], rsk[rope, :], ALU.mult))
                    do(vec.tensor_tensor(X[top, 7, :], X[top, 7, :], rsk[top, :], ALU.mult))
                    split(X[:, 7, :], F[:, f + K0, 0:TP], F[:, f + K0 + 1, 0:TP], "to_pe")

                def head_values():
                    for half in range(2):
                        aux_ready[half].step()
                        from_act()
                        if half == 0:
                            do(vec.tensor_tensor(V2[:, 0:8, 0:64], aux[:, 0, :].rearrange("p (t v) -> p t v", v=64),
                                                 V1[:, 0:8, 0:64].bitcast(F32), ALU.subtract), "aux_free0")
                        else:
                            do(vec.scalar_tensor_tensor(V2[:, 8, 0:64], aux[:, 1, 0:64], param("rows20"),
                                                        V1[:, 8, 0:64].bitcast(F32), ALU.mult, ALU.subtract),
                               "aux_free1")

                def low_parts(b):
                    s = 1 - b % 2
                    if b < 4:
                        ready[s].step()
                    for o, n in enumerate(BATCHES[b]):
                        if b == 4:
                            free[1].wait(dve)
                        elif o == len(BATCHES[b]) - 1:
                            await_free(s)
                        else:
                            from_act()
                        w = item_cols(n)[1] if ITEMS[n][1] is not None else TB * (TP - P * (TB - 1))
                        k = c["lo_ready"].n % 2
                        do(vec.tensor_tensor(prob(n, 1)[:, 0:w], R[:, 18, 512 * k:512 * k + w],
                                             prob(n, 0)[:, 0:w].bitcast(F32), ALU.subtract), "lo_ready")

                def head_out(h, pc):
                    aux_ready[pc % 2].step()
                    c["inv_ready"].step()
                    c["inv_ready"].wait(dve)
                    w = 512 if pc < 2 else TP - 1024
                    rows = slice(64 * (h % 2), 64 * (h % 2) + 64)
                    y = X[rows, h // 2, 512 * pc:512 * pc + w]
                    do(vec.tensor_tensor(y, y, head_inv(rows, pc), ALU.mult))
                    do(vec.tensor_tensor(y, aux[0:64, pc % 2, 0:w], y, ALU.mult), f"aux_free{pc % 2}")

                def maxima(i):
                    s = i % 2
                    await_ready(s)
                    do(vec.tensor_reduce(S_[:, 16 + i:17 + i],
                                         acc[:, s, :, :].rearrange("p a b -> p (a b)")[:, 0:min(P * (i + 1), TP)],
                                         AX, ALU.max, negate=True), f"free{s}")

                def linear_counts():
                    for s in (1, 1, 0):
                        ready[s].step()
                        free[s].step()

                head_table()
                linear_counts()
                head_query(0)
                head_key(0)
                for h in range(MH):
                    more = h + 1 < MH
                    for i in range(2):
                        maxima(i)
                    if h:
                        low_parts(4)
                        head_out(h - 1, 1)
                    for i in range(2, TB):
                        maxima(i)
                        if h and i == 4:
                            head_out(h - 1, 2)
                    head_values()
                    if more:
                        head_table()
                        linear_counts()
                    for half in range(2):
                        aux_ready[half].step()
                        aux_free[half].step()
                    low_parts(0)
                    low_parts(1)
                    if more:
                        head_query(h + 1)
                    low_parts(2)
                    if more:
                        head_key(h + 1)
                    low_parts(3)
                    ready[1].step()
                    free[1].step()
                    head_out(h, 0)
                low_parts(4)
                head_out(MH - 1, 1)
                head_out(MH - 1, 2)
                do(vec.tensor_copy(S_[:, 40:41], S_[:, 60:61]), "to_act")
                for j in range(4):
                    split(X[:, j, :], G[:, j, wide], G[:, 4 + j, wide], "f_ready")
                do(vec.tensor_copy(S_[:, 40:41], S_[:, 60:61]), "to_act")
                dve.wait_ge(sems["sg_in"], 16 * (l + 1))
                dve.wait_ge(sems["mg_in"], 16 * (l + 1))
                for j in range(KC):
                    s = j % 2
                    if s == 0:
                        await_ready(0)
                    else:
                        await_unit()
                    y = R[:, j, wide]
                    do(vec.tensor_tensor(cut(y, PIECES2), acc_view(s, PIECES2), cut(y, PIECES2), ALU.mult),
                       f"free{s}")
                    do(vec.tensor_tensor(y, y, X[:, j, :], ALU.add))
                    split(y, Ah[:, j, :], Al[:, j, :], "a_ready")
                do(vec.tensor_copy(S_[:, 40:41], S_[:, 60:61]), "to_act")
                dve.wait_ge(sems["xre_in"], 16 * (l + 2))
                for j in range(KC):
                    await_unit()
                    add_to_residual(j, j % 2, PIECES2, 0, TP)


def weight_stream(w):
    units = []

    def rows(m, order=None):
        k = m.shape[0] // P
        m = m.reshape(k, P, m.shape[1])
        return m if order is None else m[list(order)]

    def unit(*blocks):
        u = np.zeros((P, UW), np.float32)
        at = 0
        for b in blocks:
            k, _, m = b.shape
            u[:, at:at + k * m] = b.transpose(1, 0, 2).reshape(P, k * m)
            at += k * m
        units.append(u)

    A, C, L = ATTN_HEADS * HD, 256, 384
    w_in = rows(w["w_in"][0])
    q0, k0, v0 = 0, A, 2 * A
    ca, cg = 3 * A, 3 * A + C
    lg = 3 * A + 2 * C
    lx = lg + L
    cols = [cg, cg + P, ca, ca + P] + [lx + P * j for j in range(3)] + [lg + P * j for j in range(3)]
    for g in range(3):
        cols += [q0 + P * g, k0 + P * g, v0 + P * g]
    for col in cols:
        unit(w_in[:, :, col:col + P])
    w_out = rows(w["w_out"][0], (5, 6, 7, 3, 4, 0, 1, 2))
    for j in range(KC):
        unit(w_out[:, :, P * j:P * j + P])
    up, down = rows(w["w_up"][0]), rows(w["w_down"][0])
    for g in range(GROUPS):
        for j in range(FG):
            col = P * (FG * g + j)
            unit(up[:, :, col:col + P])
        d = down[FG * g:FG * g + FG]
        for j in range(4):
            unit(d[:, :, 256 * j:256 * j + P], d[:, :, 256 * j + P:256 * j + 256])
    for l in range(LAYERS):
        wi = rows(w["w_in_2"][l])
        for j in range(8):
            unit(wi[:, :, P * j:P * j + P])
        unit(*[w["pool_w_group_2"][l][g][None] for g in range(4)])
        pu = rows(w["pool_w_up_2"][l])
        for j in range(4):
            for s in range(2):
                col = 2592 + P * (2 * j + s)
                unit(wi[:, :, col:col + P])
            unit(pu[:, :, 256 * j:256 * j + P], pu[:, :, 256 * j + P:256 * j + 256])
        for j in range(8):
            unit(wi[:, :, 1024 + P * j:1024 + P * j + P])
        rope = np.zeros((KC, P, P), np.float32)
        rope[:, :, 0:ROPE] = wi[:, :, 2048:2080]
        rope[:, :, ROPE:2 * ROPE] = np.roll(wi[:, :, 2048:2080], ROPE // 2, axis=2)
        unit(rope)
        for j in range(4):
            unit(wi[:, :, 2080 + P * j:2080 + P * j + P])
        for j in range(8):
            unit(wi[:, :, 3616 + P * j:3616 + P * j + P])
        wq, wkv = rows(w["w_q_b_2"][l]), rows(w["w_kv_b_2"][l])
        for h in range(MH):
            q, kv = wq[:, :, QKD * h:QKD * h + QKD], wkv[:, :, P * h:P * h + P]
            q = np.concatenate([q[:, :, NOPE:], np.roll(q[:, :, NOPE:], ROPE // 2, axis=2), q[:, :, :NOPE]], axis=2)
            kv = np.concatenate([kv[:, :, NOPE:], kv[:, :, :NOPE]], axis=2)
            unit(q, kv)
        mu = rows(w["mla_w_up_2"][l])
        for j in range(4):
            unit(mu[:, :, 256 * j:256 * j + P], mu[:, :, 256 * j + P:256 * j + 256])
        wo = rows(w["w_out_2"][l])
        for j in range(8):
            unit(wo[:, :, P * j:P * j + P])
    assert len(units) == N_UNITS, (len(units), N_UNITS)
    return np.stack(units)


def param_table(w):
    t = np.zeros((P, NPARAM), np.float32)

    def put(name, v, i=0):
        t[:, PARAM_COLS[name] + i:PARAM_COLS[name] + i + v.shape[1]] = v

    def col(v):
        return v.reshape(-1, P).T

    put("norm1", col(w["norm1_g"][0]))
    for j in range(2):
        put("cdw", w["conv_dw_w"][0][:, P * j:P * j + P].T, CONV_TAPS * j)
    for j in range(3):
        put("lcw", w["lru_conv_w"][0][:, P * j:P * j + P].T, LRU_TAPS * j)
    for name, src in (("cdb", "conv_dw_b"), ("clg", "conv_ln_g"), ("clb", "conv_ln_b"), ("lcb", "lru_conv_b"),
                      ("lba", "lru_ba"), ("lbx", "lru_bx"), ("lam", "lru_lambda"), ("norm2", "norm2_g")):
        put(name, col(w[src][0]))
    put("final", col(w["final_g"]))
    for l in range(LAYERS):
        put(f"n2_{l}", col(w["norm_gain_2"][l]))
        put(f"ps_{l}", col(w["pool_scale_2"][l]))
        put(f"qa_{l}", col(w["q_a_norm_gain_2"][l]))
        put(f"kva_{l}", col(w["kv_a_norm_gain_2"][l]))
        for name, g in (("qn", w["q_norm_gain_2"][l]), ("kn", w["k_norm_gain_2"][l])):
            at = PARAM_COLS[f"{name}_{l}"]
            t[0:ROPE, at] = g[NOPE:]
            t[ROPE:2 * ROPE, at] = np.roll(g[NOPE:], ROPE // 2)
            t[2 * ROPE:, at] = g[:NOPE]
    half = ROPE // 2
    inv = (np.float32(10000.0) ** (-np.arange(half, dtype=np.float32) / np.float32(half))).astype(np.float32)
    for i in range(4):
        t[half * i:half * i + half, PARAM_COLS["freq"]] = inv
    t[ROPE:ROPE + half, PARAM_COLS["sign"]] = -1.0
    t[ROPE + half:2 * ROPE, PARAM_COLS["sign"]] = 1.0
    t[:, PARAM_COLS["rows96"]] = 1.0
    t[ROPE:2 * ROPE, PARAM_COLS["rows96"]] = 0.0
    t[P - (TP - P * (TB - 1)):, PARAM_COLS["rows20"]] = 1.0
    return t


def recurrent_gates(w):
    t = np.zeros((P, 2, 3, P), np.float32)
    for m, name in enumerate(("lru_wa", "lru_wx")):
        for h in range(6):
            o = 64 * (h % 2)
            t[o:o + 64, m, h // 2, o:o + 64] = w[name][0][h]
    return t.reshape(P, -1)


def kernel(**inputs):
    import concourse.bacc as bacc
    from concourse.bass_utils import run_bass_kernel_spmd

    w = {k: np.asarray(v) for k, v in inputs.items()}
    consts, bands = shape_constants()
    arrays = {
        "xT": np.ascontiguousarray(w["x"][0].T),
        "metaT": np.ascontiguousarray(w["meta_tokens_2"].T),
        "pos": np.ascontiguousarray(np.broadcast_to(w["positions_2"], (P, T1))),
        "params": param_table(w),
        "consts": consts,
        "bands": bands,
        "lru_w": recurrent_gates(w),
        "wstream": weight_stream(w),
    }
    nc = bacc.Bacc("TRN2", target_bir_lowering=False, num_devices=1)
    args = [nc.dram_tensor("in_" + k, a.shape, mybir.dt.from_np(a.dtype), kind="ExternalInput").ap()
            for k, a in arrays.items()]
    out = nc.dram_tensor("outT", (DM, T1), F32, kind="ExternalOutput")
    build(nc, *args, out.ap())
    r = run_bass_kernel_spmd(nc, [{"in_" + k: a for k, a in arrays.items()}], core_ids=[0])
    return np.ascontiguousarray(r.results[0]["outT"].T)[None]
```

```python
from contextlib import ExitStack

import numpy as np

import concourse.bass as bass
from concourse import mybir

F32 = mybir.dt.float32
F32R = mybir.dt.float32r
I32 = mybir.dt.int32
ALU = mybir.AluOpType
ACT = mybir.ActivationFunctionType
AX = mybir.AxisListType.X

P = 128
DM = 1024
KC = DM // P
T1 = 1024
META = 16
T2 = T1 + META
TP = 1044
TB = -(-TP // P)
LAYERS = 2
PIECES1 = (2, 512)
PIECES2 = (3, 348)
RW = 1060
NR = 19
NEG = -1e30

ATTN_HEADS, HD = 6, 64
PATTERNS = ((128, 1), (512, 4), (2048, 16))
CONV_TAPS, LRU_TAPS = 31, 4
DFF = 4096
FG = 4
GROUPS = DFF // P // FG

MH, NOPE, ROPE, VD = 8, 64, 32, 64
QKD = NOPE + ROPE
QR, KVR = 768, 256
POOLW = (2, 4, 8, 16)

UW = 1024

PARAM_COLS = {}


def _columns():
    at = 0
    for name, n in (("norm1", 8), ("cdw", 62), ("cdb", 2), ("clg", 2), ("clb", 2), ("lcw", 12), ("lcb", 3),
                    ("lba", 3), ("lbx", 3), ("lam", 3), ("norm2", 8), ("final", 8),
                    ("n2_0", 8), ("n2_1", 8), ("ps_0", 4), ("ps_1", 4), ("qa_0", 6), ("qa_1", 6),
                    ("kva_0", 2), ("kva_1", 2), ("qn_0", 1), ("qn_1", 1), ("kn_0", 1), ("kn_1", 1),
                    ("freq", 1), ("sign", 1), ("rows96", 1), ("rows20", 1)):
        PARAM_COLS[name] = at
        at += n
    return at


NPARAM = _columns()

CONST_COLS = dict(ident=0, ones=128, ones96=256, causal=384, after=512, invcnt=640, meta=704)
NCONST = 720


def shape_constants():
    c = np.zeros((P, NCONST), np.float32)
    c[:, 0:128] = np.eye(P)
    c[:, 128:256] = 1.0
    c[:, 256:384] = 1.0
    c[ROPE:2 * ROPE, 256:384] = 0.0
    q, k = np.arange(P)[:, None], np.arange(P)[None, :]
    c[:, 384:512] = np.where(k <= q, 0.0, NEG)
    c[:, 512:640] = np.where(q <= k, 0.0, NEG)
    for g, w in enumerate(POOLW):
        c[:, 640 + 16 * g:640 + 16 * g + 16] = 1.0 / np.minimum(np.arange(16) + 1, w)
    c[:, 704:720] = np.arange(META)
    slopes = 2.0 ** (-8.0 * np.arange(1, ATTN_HEADS + 1) / ATTN_HEADS)
    band = np.full((P, ATTN_HEADS, 2 * P), NEG, np.float32)
    for h in range(ATTN_HEADS):
        g = h // 2
        d = PATTERNS[g][1]
        dist = q + P - np.arange(2 * P)[None, :]
        ok = (dist >= 0) & (dist <= P)
        if g == 2:
            own = np.arange(2 * P)[None, :] - P
            ok = (own >= 0) & (own <= q) & (own // 64 == q // 64)
        band[:, h] = np.where(ok, -np.float32(slopes[h]) * (d * dist).astype(np.float32), NEG)
    return c, band.reshape(P, -1)


class Count:

    def __init__(self, sem):
        self.sem, self.n, self.reg, self.per = sem, 0, None, 0

    def step(self, k=1):
        self.n += k

    def value(self, back=0):
        n = self.n - back
        return n if self.reg is None else self.reg * self.per + n

    def wait(self, eng, back=0):
        if self.reg is None and self.n - back <= 0:
            return
        eng.wait_ge(self.sem, self.value(back))


class Loop:

    def __init__(self, reg, times, counts):
        self.times, self.counts = times, counts
        for c, per in counts:
            c.reg, c.per, c.start = reg, per, c.n

    def end(self):
        for c, per in self.counts:
            assert c.n - c.start == per, (c.sem, c.n - c.start, per)
            c.reg, c.n = None, c.start + per * self.times


UNITS_Z = 19
Z_BEFORE = 10
N_UNITS1 = UNITS_Z + KC + GROUPS * (FG + 4)
N_UNITS2 = 4 + 4 + 1 + 12 + 6 + 2 + 1 + 4 + 8 + 8 + 4 + 8
N_UNITS = N_UNITS1 + LAYERS * N_UNITS2


def build(nc, xT, metaT, pos, params, consts, bands, lru_w, wstream, outT):
    with ExitStack() as ctx:
        def sem(name):
            return ctx.enter_context(nc.semaphore(name))

        start = -(-nc.sbuf_base // 64) * 64
        at = [start]

        def place(name, cols, dt=F32, offset=None):
            if offset is None:
                offset = at[0] = -(-at[0] // 32) * 32
                at[0] += 4 * cols
            return nc.alloc_sbuf_tensor_at(name, [P, cols], dt, offset=offset), offset

        def chunks(t, n, w):
            return t[:].rearrange("p (c t) -> p c t", c=n)

        X_, _ = place("residual", KC * TP)
        Ah_, _ = place("act_hi", KC * TP, F32R)
        Al_, _ = place("act_lo", KC * TP, F32R)
        Wraw_, _ = place("w_raw", 2 * UW)
        Wh_, _ = place("w_hi", 2 * UW, F32R)
        Wl_, _ = place("w_lo", 2 * UW, F32R)
        C_, _ = place("shape_consts", NCONST)
        V_, _ = place("params", NPARAM)
        S_, _ = place("small", 64)
        R_, r_at = place("work", NR * RW)
        U_, _ = place("head_out", 384)
        F_, _ = place("ff_split", 8 * RW, F32R, offset=r_at)
        G_, _ = place("pool_split", 8 * RW, F32R, offset=r_at + 4 * 8 * RW)
        assert at[0] <= nc.sbuf_usable_end, (at[0], nc.sbuf_usable_end)
        X, Ah, Al = chunks(X_, KC, TP), chunks(Ah_, KC, TP), chunks(Al_, KC, TP)
        Wraw, Wh, Wl = chunks(Wraw_, 2, UW), chunks(Wh_, 2, UW), chunks(Wl_, 2, UW)
        R, F, G = chunks(R_, NR, RW), chunks(F_, 8, RW), chunks(G_, 8, RW)
        ident, ones = C_[:, 0:128], C_[:, 128:256]
        ones96 = C_[:, 256:384]

        def param(name, i=0, rows=slice(0, P)):
            c = PARAM_COLS[name] + i
            return V_[rows, c:c + 1]

        V1 = G_[:, 0:TB * P].rearrange("p (t c) -> p t c", c=P)
        V2 = G_[:, TB * P:2 * TB * P].rearrange("p (t c) -> p t c", c=P)
        ring0 = 2 * TB * P
        PW = 384
        PRING = 5

        def prob(n, part):
            o = ring0 + PW * (2 * (n % PRING) + part)
            return G_[:, o:o + PW]

        idr0 = ring0 + 2 * PW * PRING
        ident_r, causal_r, after_r = (G_[:, idr0 + P * i:idr0 + P * i + P] for i in range(3))
        extra0 = idr0 + 3 * P
        extra = R_[:, 8 * RW + extra0:8 * RW + extra0 + 2 * PW]
        rsk = R_[:, 16 * RW - TP:16 * RW]
        assert extra0 + 2 * PW <= 8 * RW - TP
        prob32 = (R[:, 18, 0:PW], R[:, 18, PW:2 * PW], extra[:, 0:PW])
        Q0, K0 = 0, 2
        Fy = [F_[:].rearrange("p (c s t) -> p s c t", s=2, t=RW)[:, i] for i in range(2)]
        LASTQ = TP - P
        QP = 3 * P
        NQP = -(-TP // QP)
        BLOCKS = []
        for pc in range(NQP):
            end = min(QP * (pc + 1), TP)
            for j in range(-(-end // P)):
                lo = max(QP * pc, P * j)
                if BLOCKS and BLOCKS[-1][0] == pc and j > 3 * pc and \
                        sum(t[2] for t in BLOCKS[-1][1]) + end - lo <= QP and end - lo < min(QP, end - QP * pc):
                    BLOCKS[-1][1].append((j, lo, end - lo))
                else:
                    BLOCKS.append((pc, [(j, lo, end - lo)]))
        NB = len(BLOCKS)
        BATCHES = [tuple(range(n, n + 3)) for n in range(0, NB, 3)]
        ENDS = [max(n for n in range(NB) if BLOCKS[n][0] == pc) for pc in range(NQP)]
        assert NB == 15 and [e // 3 for e in ENDS] == [0, 2, 4]

        def block_width(n):
            return sum(t[2] for t in BLOCKS[n][1])

        def piece_width(pc):
            return min(QP, TP - QP * pc)

        def head_inv(rows, pc):
            return extra[rows, PW:PW + QP] if pc == 1 else U_[rows, 0:piece_width(pc)]

        acc = ctx.enter_context(nc.psum_tensor("acc", [P, 2, 3, 512], F32))
        aux = ctx.enter_context(nc.psum_tensor("aux", [P, 2, 512], F32))

        spill_x = nc.dram_tensor("spill_x", (P, KC * TP), F32, kind="Internal").ap()
        spill_m = nc.dram_tensor("spill_m", (P, KC * TP), F32, kind="Internal").ap()
        spill_t = nc.dram_tensor("spill_t", (P, TP), F32, kind="Internal").ap()
        spill_g = nc.dram_tensor("spill_g", (P, KC * TP), F32, kind="Internal").ap()

        sems = {}
        for name in tuple(f"x_in{j}" for j in range(KC)) + tuple(f"reload{j}" for j in range(KC)) + (
            "consts_in", "meta_in", "lru_in", "bands_in", "xre_in",
            "w_in0", "w_in1", "w_hi_done", "w_lo_done", "unit_done",
            "ready0", "ready1", "free0", "free1",
            "aux_ready0", "aux_ready1", "aux_free0", "aux_free1",
            "a_ready", "a_used",
            "f_ready",
            "sq_ready", "sq_free", "sum_ready", "rs_ready", "x_ready",
            "dve_step", "act_step",
            "to_dve", "to_act", "to_pe",
            "act_to_pe", "pe_read",
            "spilled", "m_spilled", "g_spilled", "stored", "pos_in", "t_spilled", "t_in",
            "inv_ready",
            "lo_ready",
        ):
            sems[name] = sem(name)
        block = ctx.enter_context(nc.Block())

        SQ = (R[:, 8, :], R[:, 9, :], R[:, 12, :])
        SQL = ((R[:, 6, :], R[:, 3, :], R[:, 2, :]), (R[:, 7, :], R[:, 1, :], R[:, 0, :]))

        def counts():
            return {k: Count(v) for k, v in sems.items()}

        def acc_view(s, pieces, rows=slice(0, P)):
            n, w = pieces
            return acc[rows, s, 0:n, 0:w]

        def cut(ap, pieces):
            n, w = pieces
            return ap[:, 0:n * w].rearrange("p (a b) -> p a b", a=n)

        z_order = ["gate0", "gate1", "a0", "a1", "lx0", "lx1", "lx2", "lg0", "lg1", "lg2"] + \
            [f"{m}{g}" for g in range(3) for m in "qkv"]

        @block.sync
        def _(sp):
            c = counts()
            sp.dma_start(C_[:], consts).then_inc(sems["consts_in"], 16)
            sp.dma_start(V_[:], params).then_inc(sems["consts_in"], 16)
            w_in = (sems["w_in0"], sems["w_in1"])

            def load(n, s):
                sp.dma_start(Wraw[:, s, :], wstream[n, :, :] if isinstance(n, int) else
                             wstream[bass.ds(n, 1), :, :].rearrange("o p f -> (o p) f")).then_inc(w_in[s], 16)

            load(0, 0)
            load(1, 1)
            with sp.Fori(1, N_UNITS // 2) as i:
                for s in range(2):
                    sp.wait_ge(sems["w_lo_done"], i * 2 + (s - 1))
                    load(i * 2 + s, s)
            if N_UNITS % 2:
                sp.wait_ge(sems["w_lo_done"], N_UNITS - 2)
                load(N_UNITS - 1, 0)

        @block.gpsimd
        def _(pool):
            w_in = (sems["w_in0"], sems["w_in1"])

            def split(n, s, landed):
                pool.wait_ge(w_in[s], landed)
                if not isinstance(n, int) or n >= 2:
                    pool.wait_ge(sems["unit_done"], n - 1)
                nc.gpsimd.tensor_copy(Wh[:, s, :], Wraw[:, s, :]).then_inc(sems["w_hi_done"], 1)
                pool.wait_ge(sems["w_hi_done"], n + 1)
                nc.gpsimd.tensor_tensor(Wl[:, s, :], Wraw[:, s, :], Wh[:, s, :].bitcast(F32),
                                        ALU.subtract).then_inc(sems["w_lo_done"], 1)

            pool.wait_ge(sems["consts_in"], 32)
            split(0, 0, 16)
            split(1, 1, 16)
            with pool.Fori(1, N_UNITS // 2) as i:
                for s in range(2):
                    pool.wait_ge(w_in[s], i * 16 + 16)
                    pool.wait_ge(sems["unit_done"], i * 2 + (s - 1))
                    nc.gpsimd.tensor_tensor(S_[:, 62:63], C_[:, 128:129], C_[:, 128:129], ALU.add)
                    nc.gpsimd.tensor_copy(Wh[:, s, :], Wraw[:, s, :]).then_inc(sems["w_hi_done"], 1)
                    pool.wait_ge(sems["w_hi_done"], i * 2 + (s + 1))
                    nc.gpsimd.tensor_tensor(Wl[:, s, :], Wraw[:, s, :], Wh[:, s, :].bitcast(F32),
                                            ALU.subtract).then_inc(sems["w_lo_done"], 1)
            if N_UNITS % 2:
                split(N_UNITS - 1, 0, 16 * (N_UNITS // 2 + 1))

        @block.tensor
        def _(pe):
            c = counts()
            free = (c["free0"], c["free1"])
            ready = (sems["ready0"], sems["ready1"])
            aux_free = (c["aux_free0"], c["aux_free1"])
            aux_ready = (sems["aux_ready0"], sems["aux_ready1"])
            unit = Count(sems["w_lo_done"])

            def take(s):
                free[s].wait(pe)
                free[s].step()

            def take_aux(s):
                aux_free[s].wait(pe)
                aux_free[s].step()

            def chunk_products(s, ws, w0, j, k, m, hi, lo, pieces, first, end):
                n, w = pieces
                for t, (wt, x) in enumerate(((Wh, hi), (Wh, lo), (Wl, hi))):
                    for p in range(n):
                        ins = nc.tensor.matmul(
                            acc[0:m, s, p, 0:w], wt[:, ws, w0 + j * m:w0 + j * m + m],
                            x[:, k, p * w:p * w + w], start=(first and t == 0), stop=(end and t == 2))
                return ins

            def matrix(s, ws, w0, ks, m, hi, lo, pieces, arrive=None, last=None, used=None):
                take(s)
                for j, k in enumerate(ks):
                    if arrive is not None:
                        if isinstance(arrive, Count):
                            arrive.wait(pe, len(ks) - 1 - j)
                        else:
                            pe.wait_ge(arrive[0], arrive[1] + j + 1)
                    ins = chunk_products(s, ws, w0, k if used is not None else j, k, m, hi, lo, pieces, j == 0,
                                         j == len(ks) - 1)
                    if used is not None and j < len(ks) - 1:
                        ins.then_inc(used, 1)
                ins.then_inc(last if last is not None else ready[s], 1)

            def wide_two(pieces, arrive, ws):
                for s in range(2):
                    unit.step()
                    take(s)
                for k in range(KC):
                    pe.wait_ge(arrive[0], arrive[1] + k + 1)
                    for s in range(2):
                        if k == 0:
                            pe.wait_ge(unit.sem, unit.value(1 - s))
                        ins = chunk_products(s, ws[s], 0, k, k, P, Ah, Al, pieces, k == 0, k == KC - 1)
                        if k == KC - 1:
                            ins.then_inc(sems["unit_done"], 1)

            def next_unit():
                unit.step()
                pe.wait_ge(unit.sem, unit.value())

            def wide(s, ws, pieces, arrive=None, ks=range(KC), m=P):
                next_unit()
                matrix(s, ws, 0, ks, m, Ah, Al, pieces, arrive, sems["unit_done"])

            def norm_sum(s, pieces, squares):
                take(s)
                c["sum_ready"].step()
                pe.wait_ge(sems["sum_ready"], c["sum_ready"].value())
                n, w = pieces
                for p in range(n):
                    ins = nc.tensor.matmul(acc[:, s, p, 0:w], ones, squares[:, p * w:p * w + w],
                                           start=True, stop=True)
                ins.then_inc(ready[s], 1)

            pe.wait_ge(sems["consts_in"], 32)
            a0 = 0
            norm_sum(0, PIECES1, R[:, 8, :])
            wide_two(PIECES1, (sems["a_ready"], a0), (0, 1))
            with pe.Fori(0, Z_BEFORE // 2 - 1) as i:
                loop = Loop(i, Z_BEFORE // 2 - 1, [(unit, 2), (free[0], 1), (free[1], 1)])
                for s in range(2):
                    wide(s, s, PIECES1)
                loop.end()
            pe.wait_ge(sems["lru_in"], 16)
            for j in range(3):
                c["to_pe"].step()
                pe.wait_ge(sems["to_pe"], c["to_pe"].value())
                for s, col in ((0, 384), (1, 0)):
                    take(s)
                    for p in range(2):
                        ins = nc.tensor.matmul(acc[:, s, p, :], R[:, 17, col + 128 * j:col + 128 * j + 128],
                                               X[:, 4 + j, p * 512:p * 512 + 512], start=True, stop=True)
                    ins.then_inc(ready[s], 1)
                for s in range(2):
                    wide(s, s, PIECES1)
            for n in range(Z_BEFORE + 6, UNITS_Z):
                wide(n % 2, n % 2, PIECES1)
            for rnd in range(2):
                c["to_pe"].step()
                pe.wait_ge(sems["to_pe"], c["to_pe"].value())
                take(rnd)
                for j in range(2):
                    src = X[:, 2 + j, :] if rnd == 0 else R[:, 2 + j, :]
                    for p in range(2):
                        ins = nc.tensor.matmul(acc[:, rnd, p, :], ones, src[:, p * 512:p * 512 + 512],
                                               start=(j == 0), stop=(j == 1))
                ins.then_inc(ready[rnd], 1)
            PT, Vt = X[:, 3, :], X[:, 0, :]
            DG = X[:, 5, :]

            def scores(g, j, b):
                rows = slice(64 * j, 64 * j + 64)
                take(b)
                q, k = R[:, 8 + 3 * g, :], R[:, 9 + 3 * g, :]
                for i in range(4):
                    t = 4 * b + i
                    bank = acc[:, b, i // 2, 256 * (i % 2):256 * (i % 2) + 256]
                    has = (t > 0) if g == 0 else (t % 2 == 1)
                    if g < 2:
                        kt = t - 1 if has else t
                        nc.tensor.matmul(bank[:, 0:128], q[rows, 128 * t:128 * t + 128],
                                         k[rows, 128 * kt:128 * kt + 128], start=True, stop=True)
                    ins = nc.tensor.matmul(bank[:, 128:256], q[rows, 128 * t:128 * t + 128],
                                           k[rows, 128 * t:128 * t + 128], start=True, stop=True)
                ins.then_inc(ready[b], 1)

            for g in range(3):
                for half in range(2):
                    take_aux(half)
                    for i in range(4):
                        t = 4 * half + i
                        ins = nc.tensor.transpose(aux[:, half, 128 * i:128 * i + 128],
                                                  R[:, 10 + 3 * g, 128 * t:128 * t + 128], ident)
                    ins.then_inc(aux_ready[half], 1)
                for j in range(2):
                    for b in range(2):
                        scores(g, j, b)
                    for b in range(2):
                        c["to_pe"].step()
                        pe.wait_ge(sems["to_pe"], c["to_pe"].value())
                        parts = (0, 1) if g < 2 else (1,)
                        for part in parts:
                            take_aux(part)
                            for i in range(4):
                                ins = nc.tensor.transpose(
                                    aux[:, part, 128 * i:128 * i + 128],
                                    X[:, 1 + b, 256 * i + 128 * part:256 * i + 128 * part + 128], ident)
                            ins.then_inc(aux_ready[part], 1)
                        for part in range(2):
                            aux_free[part].wait(pe)
                        take(b)
                        for i in range(4):
                            t = 4 * b + i
                            has = g < 2
                            kt = (t - 1 if ((t > 0) if g == 0 else (t % 2 == 1)) else t)
                            out = acc[64 * j:64 * j + 64, b, 2, 128 * i:128 * i + 128]
                            if has:
                                nc.tensor.matmul(out, Vt[:, 128 * kt + 64 * j:128 * kt + 64 * j + 64],
                                                 PT[:, 128 * i:128 * i + 128], start=True, stop=False)
                            ins = nc.tensor.matmul(out, Vt[:, 128 * t + 64 * j:128 * t + 64 * j + 64],
                                                   PT[:, 512 + 128 * i:512 + 128 * i + 128],
                                                   start=not has, stop=True)
                        ins.then_inc(ready[b], 1)
                        c["to_pe"].step()
                        pe.wait_ge(sems["to_pe"], c["to_pe"].value())
                        take_aux(0)
                        nc.tensor.matmul(aux[64 * j:64 * j + 64, 0, :], ones[:, 0:64], DG[:, 0:512],
                                         start=True, stop=True).then_inc(aux_ready[0], 1)
            wide_two(PIECES1, (sems["a_ready"], 8), (1, 0))
            for j in range(2, KC):
                wide(j % 2, (j + 1) % 2, PIECES1)
            norm_sum(1, PIECES1, R[:, 8, :])
            with pe.Fori(0, GROUPS) as i:
                loop = Loop(i, GROUPS, [(unit, FG + 4), (free[0], FG // 2 + 4), (free[1], FG // 2 + 4),
                                        (c["f_ready"], FG)])
                for j in range(FG):
                    wide(j % 2, (j + 1) % 2, PIECES1, (sems["a_ready"], 16) if j == 0 else None)
                for j in range(4):
                    next_unit()
                    ws = (j + 1) % 2
                    for s in range(2):
                        if j == 0 and s == 0:
                            c["f_ready"].step(FG)
                        matrix(s, ws, s * 512, range(4), P, F, F[:, 4:8, :], PIECES1,
                               c["f_ready"] if j == 0 and s == 0 else None,
                               None if s == 0 else sems["unit_done"])
                loop.end()
            norm_sum(0, PIECES1, R[:, 8, :])
            a_count = 24
            ws0 = N_UNITS1 % 2
            for l in range(LAYERS):
                u = [ws0]

                def ws():
                    u[0] ^= 1
                    return u[0] ^ 1

                norm_sum(0, PIECES2, R[:, 8, :])
                wide_two(PIECES2, (sems["a_ready"], a_count), (ws(), ws()))
                for j in range(2, 8):
                    wide(j % 2, ws(), PIECES2)
                a_count += 8
                next_unit()
                w = ws()
                for j in range(4):
                    c["f_ready"].step()
                    pe.wait_ge(sems["f_ready"], c["f_ready"].value())
                    matrix(j % 2, w, j * 128, [j], P, G, G[:, 4:8, :], PIECES2, None,
                           None if j < 3 else sems["unit_done"])
                for j in range(4):
                    wide(0, ws(), PIECES2)
                    wide(1, ws(), PIECES2)
                    if j == 0:
                        c["f_ready"].step(4)
                    next_unit()
                    w = ws()
                    for s in range(2):
                        matrix(s, w, s * 512, range(4), P, G, G[:, 4:8, :], PIECES2,
                               c["f_ready"] if j == 0 and s == 0 else None,
                               None if s == 0 else sems["unit_done"])
                for j in range(8):
                    wide(j % 2, ws(), PIECES2)
                wide(0, ws(), PIECES2)
                for j in range(4):
                    wide(1 - j % 2, ws(), PIECES2)
                norm_sum(1, PIECES2, R[:, 6, :])
                norm_sum(0, PIECES2, R[:, 7, :])
                for j in range(7):
                    wide(j % 2, ws(), PIECES2)
                next_unit()
                matrix(1, ws(), 0, (6, 7, 0, 1, 2, 3, 4, 5), P, Ah, Al, PIECES2, None, sems["unit_done"],
                       sems["a_used"])

                def head_key_value(h):
                    next_unit()
                    matrix(1, w_head[0], 6 * P, (6, 7), P, Ah, Al, PIECES2,
                           (sems["a_ready"], a_count) if h == 0 else None)

                def head_query(h):
                    matrix(0, w_head[0], 0, range(6), P, Ah, Al, PIECES2,
                           (sems["a_ready"], a_count + 2) if h == 0 else None, sems["unit_done"])

                def head_sum(s):
                    take(s)
                    for p in range(3):
                        ins = nc.tensor.matmul(acc[:, s, p, 0:348], ones96,
                                               X[:, 5 + s, p * 348:p * 348 + 348], start=True, stop=True)
                    ins.then_inc(ready[s], 1)

                def head_values():
                    for half in range(2):
                        take_aux(half)
                        for t in (range(8) if half == 0 else (8,)):
                            c0 = min(P * t, LASTQ)
                            ins = nc.tensor.transpose(aux[:, half, 64 * (t % 8):64 * (t % 8) + 64],
                                                      R[64:128, 16, c0:c0 + P], ident[64:128, 64:128])
                        ins.then_inc(aux_ready[half], 1)

                def rough_scores(i, qh, kh):
                    s = i % 2
                    nk = min(P * (i + 1), TP)
                    take(s)
                    for p in range(-(-nk // 512)):
                        n = min(512, nk - 512 * p)
                        diag = p == P * i // 512
                        ins = nc.tensor.matmul(acc[:, s, p, 0:n], qh[:, min(P * i, LASTQ):min(P * i, LASTQ) + P],
                                               kh[:, 512 * p:512 * p + n], start=True, stop=not diag)
                    o = P * i - 512 * p
                    n = nk - P * i
                    nc.tensor.matmul(acc[:, s, p, o:o + n], ident_r, causal_r[:, P - n:P],
                                     start=False, stop=True).then_inc(ready[s], 1)

                def scores_t(n, s, b, q2, k2):
                    at = 0
                    for j, lo, w in BLOCKS[n][1]:
                        out = acc[:, s, b, at:at + w]
                        at += w
                        c0 = min(P * j, LASTQ)
                        diag = P * j == lo
                        for m, (kt, qt) in enumerate(((0, 0), (0, 1), (1, 0))):
                            ins = nc.tensor.matmul(out, k2[kt][:, c0:c0 + P], q2[qt][:, lo:lo + w],
                                                   start=m == 0, stop=(m == 2 and not diag))
                        if diag:
                            n_ = min(P, w)
                            ins = nc.tensor.matmul(out[:, 0:n_], ident_r, after_r[:, P - n_:P],
                                                   start=False, stop=True)
                    return ins

                def weigh_values(n):
                    pc, tiles = BLOCKS[n]
                    if tiles[0][0] == 0:
                        take_aux(pc % 2)
                    c["lo_ready"].step()
                    pe.wait_ge(sems["lo_ready"], c["lo_ready"].value())
                    at = 0
                    for t, lo, w in tiles:
                        end = n in ENDS and t == tiles[-1][0]
                        for m, (v, part) in enumerate(((V1, 0), (V1, 1), (V2, 0))):
                            ins = nc.tensor.matmul(aux[:, pc % 2, lo - QP * pc:lo - QP * pc + w], v[:, t, :],
                                                   prob(n, part)[:, at:at + w],
                                                   start=(t == 0 and m == 0), stop=(end and m == 2))
                        at += w
                    ins.then_inc(aux_ready[pc % 2] if n in ENDS else sems["pe_read"], 1)

                w_head = [ws()]
                head_key_value(0)
                head_query(0)
                head_sum(1)
                head_sum(0)
                for h in range(MH):
                    more = h + 1 < MH
                    f0 = 4 * (h % 2)
                    q2 = (F[:, f0 + Q0, :], F[:, f0 + Q0 + 1, :])
                    k2 = (F[:, f0 + K0, :], F[:, f0 + K0 + 1, :])
                    c["to_pe"].step()
                    pe.wait_ge(sems["to_pe"], c["to_pe"].value())
                    for i in range(TB):
                        rough_scores(i, q2[0], k2[0])
                        if h and i < 2:
                            for n in BATCHES[3 + i]:
                                weigh_values(n)
                    if more:
                        w_head[0] = ws()
                        head_key_value(h + 1)
                    head_values()
                    if more:
                        head_query(h + 1)
                        head_sum(1)
                    else:
                        for s in range(2):
                            free[s].wait(pe)
                    for half in range(2):
                        take_aux(half)
                    for i in range(TB):
                        n = min(P, TP - P * i)
                        out = aux[32:33, i // 4, P * (i % 4):P * (i % 4) + n] if i < 8 else aux[64:65, 1, 0:n]
                        ins = nc.tensor.matmul(out, S_[:, 16 + i:17 + i], ident[:, P - n:P], start=True, stop=True)
                        if i in (3, 8):
                            ins.then_inc(aux_ready[i // 8], 1)
                    if more:
                        head_sum(0)
                    for half in range(2):
                        aux_free[half].wait(pe)
                    for b, batch in enumerate(BATCHES):
                        s = 1 - b % 2
                        take(s)
                        for o, n in enumerate(batch):
                            ins = scores_t(n, s, o, q2, k2)
                        ins.then_inc(ready[s], 1)
                        if 1 <= b <= 3:
                            for n in BATCHES[b - 1]:
                                weigh_values(n)
                for n in BATCHES[3] + BATCHES[4]:
                    weigh_values(n)
                a_count += 8
                for j in range(4):
                    next_unit()
                    w = ws()
                    for s in range(2):
                        if j == 0 and s == 0:
                            c["f_ready"].step(4)
                        matrix(s, w, s * 512, range(4), P, Fy[0], Fy[1], PIECES2,
                               c["f_ready"] if j == 0 and s == 0 else None,
                               None if s == 0 else sems["unit_done"])
                wide_two(PIECES2, (sems["a_ready"], a_count), (ws(), ws()))
                for j in range(2, KC):
                    wide(j % 2, ws(), PIECES2)
                a_count += 8
                ws0 = u[0]

        @block.scalar
        def _(act):
            c = counts()
            free = (c["free0"], c["free1"])
            ready = (c["ready0"], c["ready1"])
            aux_free = (c["aux_free0"], c["aux_free1"])
            aux_ready = (c["aux_ready0"], c["aux_ready1"])
            unit = c["unit_done"]

            def do(ins, name="act_step"):
                ins.then_inc(sems[name], 1)
                c[name].step()

            def after(name="act_step"):
                c[name].wait(act)

            def await_unit(s):
                unit.step()
                act.wait_ge(unit.sem, unit.value())

            def await_ready(s):
                ready[s].step()
                act.wait_ge(ready[s].sem, ready[s].value())

            def release(ins, s):
                do(ins, f"free{s}")

            def copy(out, in_, scale=1.0):
                return nc.scalar.activation(out, in_, ACT.Copy, scale=scale)

            def log_and_exp():
                nc.scalar.preload_act_table_set("natural_log_exp_and_others")

            def square(src, j, slots, part=lambda t: t):
                if j > 2:
                    c["sq_free"].step()
                    act.wait_ge(sems["sq_free"], c["sq_free"].value())
                to = slots[0 if j == 0 else 1 + j % 2]
                do(nc.scalar.activation(part(to), src, ACT.Square), "sq_ready")

            def norm_scale(width, pieces, s, rs, dim, n):
                await_ready(s)
                release(nc.scalar.activation(cut(rs, pieces), acc_view(s, pieces), ACT.Ln,
                                             scale=1.0 / dim, bias=eps_col(1e-6, P)), s)
                after(f"free{s}")
                do(nc.scalar.activation(rs[:, 0:width], rs[:, 0:width], ACT.Exp, scale=-0.5), "rs_ready")

            def norm_stats(src, n, width, pieces, s, slots, rs, dim, eps, arrive):
                for j in range(n):
                    arrive(j)
                    square(src(j), j, [t[:, 0:width] for t in slots])
                norm_scale(width, pieces, s, rs, dim, n)

            def eps_col(eps, rows):
                col = 60 if eps == 1e-6 else 61
                return S_[0:rows, col:col + 1]

            for j in range(KC):
                act.dma_start(X[:, j, META:T2], xT[P * j:P * j + P, :]).then_inc(sems[f"x_in{j}"], 16)
            act.dma_start(R[:, 17, 0:768], lru_w).then_inc(sems["lru_in"], 16)
            act.wait_ge(sems["consts_in"], 32)
            c["to_act"].step()
            act.wait_ge(sems["to_act"], c["to_act"].value())
            do(nc.scalar.activation(S_[:, 6:9], V_[:, PARAM_COLS["lam"]:PARAM_COLS["lam"] + 3], ACT.Abs))
            after()
            do(nc.scalar.activation(S_[:, 6:9], S_[:, 6:9], ACT.Exp, scale=-1.0))
            after()
            do(nc.scalar.activation(S_[:, 6:9], S_[:, 6:9], ACT.Ln, bias=1.0), "to_dve")
            log_and_exp()
            norm_stats(lambda j: X[:, j, META:T2], KC, T1, PIECES1, 0, SQ, R[:, 10, :],
                       DM, 1e-6, lambda j: act.wait_ge(sems[f"x_in{j}"], 16))
            def recurrent_gates(j):
                if j:
                    c["to_act"].step()
                    act.wait_ge(sems["to_act"], c["to_act"].value())
                await_ready(0)
                release(nc.scalar.activation(cut(X[:, 0, :], PIECES1), acc_view(0, PIECES1), ACT.Sigmoid,
                                             bias=param("lbx", j)), 0)
                await_ready(1)
                release(nc.scalar.activation(cut(X[:, 7, :], PIECES1), acc_view(1, PIECES1), ACT.Sigmoid,
                                             bias=param("lba", j)), 1)
                do(nc.scalar.activation(R[:, 5 + j, 0:T1], R[:, 5 + j, 0:T1], ACT.Gelu_apprx_tanh), "to_dve")

            def recurrent_decay():
                c["to_act"].step()
                act.wait_ge(sems["to_act"], c["to_act"].value())
                do(nc.scalar.activation(R[:, 18, 0:T1], X[:, 1, 0:T1], ACT.Exp, scale=-1.0))
                do(nc.scalar.activation(R[:, 2, 0:T1], X[:, 1, 0:T1], ACT.Tanh), "to_dve")

            def recurrent_root():
                c["to_act"].step()
                act.wait_ge(sems["to_act"], c["to_act"].value())
                do(nc.scalar.activation(R[:, 3, 0:T1], R[:, 2, 0:T1], ACT.Sqrt), "to_dve")

            for n, what in enumerate(z_order):
                s = n % 2
                await_unit(s)
                if what.startswith("gate"):
                    release(nc.scalar.activation(cut(X[:, n, :], PIECES1), acc_view(s, PIECES1),
                                                 ACT.Sigmoid), s)
                elif what[0] == "a":
                    free[s].step()
                elif what.startswith("lx"):
                    j = int(what[2])
                    release(copy(cut(R[:, 2 + j, LRU_TAPS - 1:], PIECES1), acc_view(s, PIECES1)), s)
                elif what.startswith("lg"):
                    release(copy(cut(R[:, 5 + int(what[2]), :], PIECES1), acc_view(s, PIECES1)), s)
                else:
                    g = int(what[1])
                    d = PATTERNS[g][1]
                    slot = R[:, 8 + 3 * g + "qkv".index(what[0]), 0:T1]
                    if d == 1:
                        release(copy(cut(slot, PIECES1), acc_view(s, PIECES1)), s)
                    else:
                        u = 512 // d
                        to = slot.rearrange("p (r u) -> p u r", r=d)
                        for p in range(2):
                            ins = copy(to[:, u * p:u * p + u, :],
                                       acc[:, s, p, :].rearrange("p (u r) -> p u r", r=d))
                            if p == 0:
                                do(ins)
                        release(ins, s)
                j, stage = divmod(n - (Z_BEFORE - 1), 2)
                if 0 <= j <= 3 and stage == 0:
                    if j:
                        recurrent_root()
                    if j < 3:
                        recurrent_gates(j)
                elif 0 <= j < 3:
                    recurrent_decay()
            log_and_exp()
            await_ready_only = ready[0]
            await_ready_only.step()
            free[0].step()
            await_ready(1)
            release(nc.scalar.activation(cut(R[:, 4, :], PIECES1), acc_view(1, PIECES1), ACT.Ln,
                                         scale=1.0 / 256, bias=eps_col(1e-5, P)), 1)
            after("free1")
            do(nc.scalar.activation(R[:, 4, 0:T1], R[:, 4, 0:T1], ACT.Exp, scale=-0.5), "rs_ready")
            for j in range(2):
                c["to_act"].step()
                act.wait_ge(sems["to_act"], c["to_act"].value())
                do(nc.scalar.activation(R[:, 2 + j, 0:T1], X[:, 2 + j, 0:T1], ACT.Sigmoid), "to_dve")
            log_and_exp()
            act.wait_ge(sems["a_ready"], 8 + 3)
            act.dma_start(X_[:, 6 * TP:6 * TP + 6 * 256], bands).then_inc(sems["bands_in"], 16)
            for g in range(3):
                for half in range(2):
                    aux_ready[half].step()
                    act.wait_ge(aux_ready[half].sem, aux_ready[half].value())
                    if half == 0 and g:
                        act.wait_ge(ready[1].sem, ready[1].value())
                    do(copy(X[:, 0, 512 * half:512 * half + 512], aux[:, half, :]), f"aux_free{half}")
                for j in range(2):
                    for b in range(2):
                        ready[b].step()
                        free[b].step()

                    def exps(b):
                        c["to_act"].step()
                        act.wait_ge(sems["to_act"], c["to_act"].value())
                        lo, hi = (0, 256) if g < 2 else (128, 256)
                        for i in range(4):
                            do(nc.scalar.activation(X[:, 1 + b, 256 * i + lo:256 * i + hi],
                                                    X[:, 1 + b, 256 * i + lo:256 * i + hi], ACT.Exp,
                                                    bias=S_[:, 16 + 4 * b + i:17 + 4 * b + i],
                                                    accum_out=S_[:, 24 + 4 * b + i:25 + 4 * b + i]))
                        after()
                        do(nc.scalar.activation(S_[:, 32 + 4 * b:36 + 4 * b], S_[:, 24 + 4 * b:28 + 4 * b],
                                                ACT.Ln), "to_dve")

                    exps(0)
                    exps(1)
                    for b in range(2):
                        if not (g == 0 and j == 0 and b == 0):
                            act.wait_ge(ready[1 - b].sem, ready[1 - b].value())
                        for part in ((0, 1) if g < 2 else (1,)):
                            aux_ready[part].step()
                            act.wait_ge(aux_ready[part].sem, aux_ready[part].value())
                            do(copy(X[:, 3, 512 * part:512 * part + 512], aux[:, part, :]), f"aux_free{part}")
                        await_ready(b)
                        rows = slice(64 * j, 64 * j + 64)
                        d = PATTERNS[g][1]
                        nat = R[rows, g, 0:T1]
                        src = acc[rows, b, 2, :]
                        if d == 1:
                            release(copy(nat[:, 512 * b:512 * b + 512], src), b)
                        else:
                            release(copy(nat.rearrange("p (u r) -> p r u", r=d)[:, b * d // 2:(b + 1) * d // 2, :],
                                         src.rearrange("p (r u) -> p r u", r=d // 2)), b)
                        aux_ready[0].step()
                        aux_free[0].step()
            c["to_act"].step()
            act.wait_ge(sems["to_act"], c["to_act"].value())
            act.dma_start(X[:, :, META:T2], xT.rearrange("(c p) t -> p c t", p=P)).then_inc(sems["xre_in"], 16)
            for g in range(3):
                ins = nc.scalar.activation(R[:, 3 + g, 0:T1], R[:, 3 + g, 0:T1], ACT.Exp)
                do(ins, "to_dve" if g == 2 else "act_step")

            def updated(s):
                unit.step()
                free[s].step()
                free[s].wait(act)

            norm_stats(lambda j: X[:, j, META:T2], KC, T1, PIECES1, 1, SQ, R[:, 10, :],
                       DM, 1e-6, lambda j: updated(j % 2))
            act.dma_start(X[:, :, 0:META], metaT.rearrange("(c p) t -> p c t", p=P)).then_inc(sems["meta_in"], 16)
            act.wait_ge(sems["a_ready"], 24)
            act.dma_start(R[:, 8, META:T2].bitcast(I32), pos).then_inc(sems["pos_in"], 16)
            c["to_act"].step()
            act.wait_ge(sems["to_act"], c["to_act"].value())
            do(nc.scalar.activation(R[:, 16, 0:TP], R[:, 16, 0:TP], ACT.Sin))
            after()
            rot = slice(ROPE, 2 * ROPE)
            do(nc.scalar.activation(R[rot, 16, 0:TP], R[rot, 17, 0:TP], ACT.Sin, scale=param("sign", 0, rot)),
               "act_step")
            after()
            act.dma_start(spill_t, R[:, 16, 0:TP]).then_inc(sems["t_spilled"], 16)
            with act.Fori(0, GROUPS) as i:
                loop = Loop(i, GROUPS, [(unit, FG + 4), (free[0], FG // 2 + 4), (free[1], FG // 2 + 4),
                                        (ready[0], 4)])
                for j in range(FG):
                    s = j % 2
                    await_unit(s)
                    release(nc.scalar.activation(cut(R[:, 12 + j, :], PIECES1), acc_view(s, PIECES1),
                                                 ACT.Relu), s)
                unit.step(4)
                ready[0].step(4)
                free[0].step(4)
                free[1].step(4)
                loop.end()

            def both_free():
                for s in range(2):
                    free[s].wait(act)

            log_and_exp()
            both_free()
            norm_stats(lambda j: X[:, j, META:T2], KC, T1, PIECES1, 0, SQ, R[:, 10, :],
                       DM, 1e-6, lambda j: None)

            def by_signal(j):
                c["to_act"].step()
                act.wait_ge(sems["to_act"], c["to_act"].value())

            for l in range(LAYERS):
                last = l == LAYERS - 1
                if l == 0:
                    act.wait_ge(sems["meta_in"], 16)
                norm_stats(lambda j: X[:, j, :], KC, TP, PIECES2, 0, SQ, R[:, 10, :],
                           DM, 1e-6, by_signal if l == 0 else lambda j: updated(j % 2))
                act.dma_start(spill_x, X_[:]).then_inc(sems["spilled"], 16)
                act.wait_ge(sems["t_spilled"], 16)
                act.dma_start(R[:, 17, 0:TP], spill_t).then_inc(sems["t_in"], 16)
                for j in range(4):
                    await_unit(j % 2)
                    if j == 0:
                        by_signal(0)
                    release(copy(cut(R[:, j, 16:], PIECES2), acc_view(j % 2, PIECES2)), j % 2)
                for j in range(4):
                    await_unit(j % 2)
                    do(nc.scalar.activation(cut(R[:, 4 + j, :], PIECES2), acc_view(j % 2, PIECES2),
                                            ACT.Sigmoid), "to_dve")
                    free[j % 2].step()
                for j in range(4):
                    if j < 3:
                        ready[j % 2].step()
                    free[j % 2].step()
                unit.step()
                for j in range(4):
                    for s in range(2):
                        await_unit(s)
                        if j:
                            free[s].wait(act)
                        release(nc.scalar.activation(cut(R[:, s, :], PIECES2), acc_view(s, PIECES2),
                                                     ACT.Sigmoid), s)
                    unit.step()
                    ready[0].step()
                    for s in range(2):
                        free[s].step()
                for s in range(2):
                    free[s].wait(act)
                act.dma_start(spill_m, X_[:]).then_inc(sems["m_spilled"], 16)
                for j in range(8):
                    await_unit(j % 2)
                    part = lambda t: cut(t, PIECES2)
                    square(acc_view(j % 2, PIECES2), j % 6, SQL[j // 6], part)
                    release(copy(cut(R[:, 8 + j, :], PIECES2), acc_view(j % 2, PIECES2)), j % 2)
                await_unit(0)
                act.wait_ge(sems["m_spilled"], 16 * (l + 1))
                rr = slice(0, 2 * ROPE)
                do(nc.scalar.activation(cut(X[rr, 6, :], PIECES2), acc_view(0, PIECES2, rr), ACT.Square), "to_dve")
                free[0].step()
                for j in range(4):
                    s = 1 - j % 2
                    await_unit(s)
                    do(nc.scalar.activation(cut(X[:, j, :], PIECES2), acc_view(s, PIECES2), ACT.Sigmoid),
                       "to_dve")
                    free[s].step()
                log_and_exp()
                norm_scale(TP, PIECES2, 1, R[:, 4, :], QR, 6)
                norm_scale(TP, PIECES2, 0, R[:, 5, :], KVR, 2)
                by_signal(0)
                for j in range(8):
                    await_unit(j % 2)
                    release(nc.scalar.activation(cut(R[:, j, :], PIECES2), acc_view(j % 2, PIECES2),
                                                 ACT.Sigmoid), j % 2)
                by_signal(0)
                act.dma_start(spill_g, R[:, 0:8, 0:TP]).then_inc(sems["g_spilled"], 16)

                top, low = slice(64, 128), slice(0, 64)

                def reload(to, src, j):
                    act.dma_start(to, src[:, TP * j:TP * j + TP]).then_inc(sems[f"reload{j}"], 16)

                def head_key_squares(values):
                    await_ready(1)
                    do(nc.scalar.activation(cut(X[top, 6, :], PIECES2), acc_view(1, PIECES2, top), ACT.Square))
                    do(copy(cut(X[top, 7, :], PIECES2), acc_view(1, PIECES2, top), param(f"kn_{l}", 0, top)))
                    if values:
                        head_values()
                    release(copy(cut(R[top, 16, :], PIECES2), acc_view(1, PIECES2, low)), 1)

                def head_query_squares():
                    await_unit(0)
                    do(nc.scalar.activation(cut(X[:, 5, :], PIECES2), acc_view(0, PIECES2), ACT.Square), "to_dve")
                    free[0].step()

                def head_log(s, rs):
                    await_ready(s)
                    release(nc.scalar.activation(cut(rs, PIECES2), acc_view(s, PIECES2), ACT.Ln,
                                                 scale=1.0 / QKD, bias=eps_col(1e-6, P)), s)
                    after(f"free{s}")

                def head_exp(rs):
                    do(nc.scalar.activation(rs, rs, ACT.Exp, scale=-0.5), "rs_ready")

                def head_values():
                    for half in range(2):
                        aux_ready[half].step()
                        act.wait_ge(aux_ready[half].sem, aux_ready[half].value())
                        if half == 0:
                            do(copy(V1[:, 0:8, 0:64], aux[:, 0, :].rearrange("p (t v) -> p t v", v=64)), "to_dve")
                        else:
                            do(copy(V1[:, 8, 0:64], aux[:, 1, 0:64], param("rows20")), "to_dve")
                        aux_free[half].step()

                def head_inverse(h, pc):
                    aux_ready[pc % 2].step()
                    act.wait_ge(aux_ready[pc % 2].sem, aux_ready[pc % 2].value())
                    rows = slice(64 * (h % 2), 64 * (h % 2) + 64)
                    u = head_inv(rows, pc)
                    do(nc.scalar.activation(u, aux[64:128, pc % 2, 0:piece_width(pc)], ACT.Ln))
                    after()
                    do(nc.scalar.activation(u, u, ACT.Exp, scale=-1.0), "inv_ready")
                    aux_free[pc % 2].step()

                log_and_exp()
                head_key_squares(False)
                head_query_squares()
                head_log(1, rsk)
                head_exp(rsk)
                head_log(0, X[:, 5, :])
                head_exp(X[:, 5, :])
                for h in range(MH):
                    more = h + 1 < MH
                    for i in range(TB):
                        ready[i % 2].step()
                        free[i % 2].step()
                    if h:
                        head_inverse(h - 1, 2)
                    if not more:
                        by_signal(0)
                        for j in range(4, KC):
                            reload(X[:, j, :], spill_m, j)
                    if more:
                        head_key_squares(True)
                        head_query_squares()
                        head_log(1, rsk)
                    else:
                        head_values()
                    qh = F[32:33, 4 * (h % 2) + Q0, 0:TP]
                    for half in range(2):
                        aux_ready[half].step()
                        act.wait_ge(aux_ready[half].sem, aux_ready[half].value())
                        do(copy(qh[:, 512 * half:512 * half + 512], aux[32:33, half, :]),
                           "aux_free0" if half == 0 else "act_step")
                    do(copy(qh[:, 1024:TP], aux[64:65, 1, 0:TP - 1024]), "aux_free1")
                    if more:
                        head_exp(rsk)
                        head_log(0, X[:, 5, :])
                        head_exp(X[:, 5, :])
                    for b, batch in enumerate(BATCHES):
                        s = 1 - b % 2
                        await_ready(s)
                        for o, n in enumerate(batch):
                            back = n - PRING
                            if back == ENDS[1]:
                                act.wait_ge(sems["aux_ready1"], aux_ready[1].value() + 1)
                            elif back >= 0 and back != ENDS[0]:
                                before = sum(1 for m in range(back + 1) if m not in ENDS)
                                act.wait_ge(sems["pe_read"], (NB - NQP) * (l * MH + h) + before)
                            c["lo_ready"].wait(act, len(prob32) - 1)
                            w = block_width(n)
                            src = acc[:, s, o, 0:w]
                            do(nc.scalar.activation(prob32[c["lo_ready"].n % len(prob32)][:, 0:w], src, ACT.Exp))
                            ins = nc.scalar.activation(prob(n, 0)[:, 0:w], src, ACT.Exp)
                            do(ins, f"free{s}" if o == len(batch) - 1 else "to_dve")
                            c["lo_ready"].step()
                        if b == 1:
                            head_inverse(h, 0)
                        if b == 3:
                            head_inverse(h, 1)
                head_inverse(MH - 1, 2)
                by_signal(0)
                for j in range(4):
                    reload(R[:, 8 + j, 0:TP], spill_g, j)
                    if j == 2:
                        by_signal(0)
                    reload(X[:, j, :], spill_m, j)
                for j in range(4, KC):
                    reload(R[:, 8 + j, 0:TP], spill_g, j)
                for j in range(4):
                    unit.step()
                    ready[0].step()
                    free[0].step()
                    free[1].step()
                act.wait_ge(sems["spilled"], 16 * (l + 1))
                for j in range(KC):
                    by_signal(0)
                    reload(X[:, j, :], spill_x, j)
                if last:
                    for j in range(KC):
                        updated(j % 2)
                        act.dma_start(outT[P * j:P * j + P, :], X[:, j, META:T2]).then_inc(sems["stored"], 16)
                    act.wait_ge(sems["stored"], 16 * KC)

        @block.vector
        def _(dve):
            c = counts()
            free = (c["free0"], c["free1"])
            ready = (c["ready0"], c["ready1"])
            aux_free = (c["aux_free0"], c["aux_free1"])
            aux_ready = (c["aux_ready0"], c["aux_ready1"])
            unit = c["unit_done"]
            vec = nc.vector

            def do(ins, name="dve_step"):
                ins.then_inc(sems[name], 1)
                c[name].step()
                c[name].wait(dve)

            def await_unit():
                unit.step()
                dve.wait_ge(unit.sem, unit.value())

            def await_ready(s):
                ready[s].step()
                dve.wait_ge(ready[s].sem, ready[s].value())

            def await_free(s):
                free[s].step()
                free[s].wait(dve)

            def from_act():
                c["to_dve"].step()
                dve.wait_ge(sems["to_dve"], c["to_dve"].value())

            def split(src, hi, lo, name):
                do(vec.tensor_copy(hi, src))
                do(vec.tensor_tensor(lo, src, hi.bitcast(F32), ALU.subtract), name)

            def add_square(j, n, slots, cols):
                c["sq_ready"].step()
                if j == 0:
                    return
                dve.wait_ge(sems["sq_ready"], c["sq_ready"].value())
                total = slots[0][:, cols]
                do(vec.tensor_tensor(total, total, slots[1 + j % 2][:, cols], ALU.add),
                   "sum_ready" if j == n - 1 else "sq_free" if j <= n - 3 else "dve_step")

            def normalise(n, src, gain, rs, y, width):
                c["rs_ready"].step()
                dve.wait_ge(sems["rs_ready"], c["rs_ready"].value())
                for j in range(n):
                    do(vec.scalar_tensor_tensor(y[:, 0:width], src(j), param(gain, j), rs[:, 0:width],
                                                ALU.mult, ALU.mult))
                    split(y[:, 0:width], Ah[:, j, 0:width], Al[:, j, 0:width], "a_ready")

            dve.wait_ge(sems["consts_in"], 32)
            do(vec.memset(S_[:, 0:62], 1e-6))
            do(vec.memset(S_[:, 61:62], 1e-5), "to_act")
            do(vec.tensor_scalar(S_[:, 9:12], V_[:, PARAM_COLS["lam"]:PARAM_COLS["lam"] + 3], -1.0, 0.0,
                                 ALU.mult, ALU.max))
            from_act()
            do(vec.tensor_tensor(S_[:, 9:12], S_[:, 9:12], S_[:, 6:9], ALU.add))
            do(vec.tensor_scalar_mul(S_[:, 9:12], S_[:, 9:12], 8.0))
            do(vec.memset(R[:, 0:2, 0:CONV_TAPS - 1], 0.0))
            do(vec.memset(R[:, 2:5, 0:LRU_TAPS - 1], 0.0))
            ready[0].step()
            free[0].step()
            for j in range(KC):
                add_square(j, KC, SQ, slice(0, T1))
            normalise(KC, lambda j: X[:, j, META:T2], "norm1", R[:, 10, :], R[:, 11, :], T1)
            for n in range(2):
                unit.step()
                await_free(n)
            for n in range(2):
                await_unit()
                do(vec.tensor_tensor(cut(R[:, n, CONV_TAPS - 1:], PIECES1), acc_view(n, PIECES1),
                                     cut(X[:, n, :], PIECES1), ALU.mult), f"free{n}")

            def convolve(out, src, taps, w, b, name):
                do(vec.tensor_scalar(out, src[:, 0:T1], V_[:, w:w + 1], b, ALU.mult, ALU.add))
                for k in range(1, taps):
                    do(vec.scalar_tensor_tensor(out, src[:, k:k + T1], V_[:, w + k:w + k + 1], out,
                                                ALU.mult, ALU.add), name if k == taps - 1 else "dve_step")

            for n in range(4, 7):
                unit.step()
                await_free(n % 2)
                j = n - 4
                convolve(X[:, 4 + j, 0:T1], R[:, 2 + j, :], LRU_TAPS, PARAM_COLS["lcw"] + LRU_TAPS * j,
                         param("lcb", j), "to_pe")
            def conv_taps(t0, t1):
                for t in range(t0, t1):
                    j, k = divmod(t, CONV_TAPS)
                    out, w = X[:, 2 + j, 0:T1], PARAM_COLS["cdw"] + CONV_TAPS * j + k
                    if k == 0:
                        do(vec.tensor_scalar(out, R[:, j, 0:T1], V_[:, w:w + 1], param("cdb", j), ALU.mult, ALU.add))
                    else:
                        do(vec.scalar_tensor_tensor(out, R[:, j, k:k + T1], V_[:, w:w + 1], out,
                                                    ALU.mult, ALU.add))

            for n in range(7, Z_BEFORE):
                unit.step()
                free[n % 2].step()
            full = slice(0, T1)
            conv_taps(0, 15)
            taps = 15
            for j in range(3):
                for s in (0, 1):
                    ready[s].step()
                    await_free(s)
                do(vec.tensor_scalar(X[:, 1, full], X[:, 7, full], S_[:, 9 + j:10 + j], None, ALU.mult), "to_act")
                do(vec.tensor_tensor(X[:, 0, full], X[:, 0, full], X[:, 4 + j, full], ALU.mult))
                for n in range(Z_BEFORE + 2 * j, Z_BEFORE + 2 * j + 2):
                    unit.step()
                    free[n % 2].step()
                conv_taps(taps, taps + 6)
                from_act()
                from_act()
                do(vec.tensor_scalar_add(X[:, 1, full], R[:, 2, full], 1.0))
                do(vec.reciprocal(X[:, 1, full], X[:, 1, full]))
                do(vec.scalar_tensor_tensor(R[:, 2, full], R[:, 2, full], 2.0, X[:, 1, full], ALU.mult, ALU.mult),
                   "to_act")
                conv_taps(taps + 6, taps + 9)
                taps += 9
                from_act()
                do(vec.tensor_tensor(X[:, 0, full], X[:, 0, full], R[:, 3, full], ALU.mult))
                do(vec.tensor_tensor_scan(X[:, 1, full], R[:, 18, full], X[:, 0, full], 0.0, ALU.mult, ALU.add))
                do(vec.tensor_tensor(R[:, 5 + j, full], R[:, 5 + j, full], X[:, 1, full], ALU.mult),
                   "to_act" if j < 2 else "dve_step")
            conv_taps(taps, 2 * CONV_TAPS)
            do(vec.tensor_copy(S_[:, 40:41], S_[:, 60:61]), "to_pe")
            for n in range(Z_BEFORE + 6, UNITS_Z):
                unit.step()
                free[n % 2].step()
            for s in range(2):
                dve.wait_ge(free[s].sem, free[s].value())
            for j in range(3):
                split(R[:, 5 + j, full], Ah[:, j, full], Al[:, j, full], "a_ready")
            await_ready(0)
            for j in range(2):
                do(vec.scalar_tensor_tensor(cut(X[:, 2 + j, :], PIECES1), acc_view(0, PIECES1), -1.0 / 256,
                                            cut(X[:, 2 + j, :], PIECES1), ALU.mult, ALU.add),
                   "dve_step" if j == 0 else "free0")
            for j in range(2):
                do(vec.tensor_tensor(R[:, 2 + j, full], X[:, 2 + j, full], X[:, 2 + j, full], ALU.mult),
                   "dve_step" if j == 0 else "to_pe")
            ready[1].step()
            free[1].step()
            c["rs_ready"].step()
            dve.wait_ge(sems["rs_ready"], c["rs_ready"].value())
            for j in range(2):
                y = X[:, 2 + j, full]
                do(vec.scalar_tensor_tensor(y, y, param("clg", j), R[:, 4, full], ALU.mult, ALU.mult))
                do(vec.tensor_scalar(y, y, param("clb", j), None, ALU.add), "to_act")
            for j in range(2):
                y = X[:, 2 + j, full]
                from_act()
                do(vec.tensor_tensor(y, y, R[:, 2 + j, full], ALU.mult))
                split(y, Ah[:, 3 + j, full], Al[:, 3 + j, full], "a_ready")
            dve.wait_ge(sems["bands_in"], 16)
            pend = []

            def take_lse():
                g, j, b = pend.pop()
                aux_ready[0].step()
                dve.wait_ge(aux_ready[0].sem, aux_ready[0].value())
                rows = slice(64 * j, 64 * j + 64)
                d = PATTERNS[g][1]
                nat = R[rows, 3 + g, full]
                src = aux[rows, 0, :]
                if d == 1:
                    ins = vec.tensor_copy(nat[:, 512 * b:512 * b + 512], src)
                else:
                    ins = vec.tensor_copy(nat.rearrange("p (u r) -> p r u", r=d)[:, b * d // 2:(b + 1) * d // 2, :],
                                          src.rearrange("p (r u) -> p r u", r=d // 2))
                do(ins, "aux_free0")

            for g in range(3):
                lo = 0 if g < 2 else 128
                for half in range(2):
                    aux_ready[half].step()
                    aux_free[half].step()
                for j in range(2):
                    def stats(b):
                        await_ready(b)
                        pb = X[:, 1 + b, 0:1024].rearrange("p (i k) -> p i k", k=256)
                        sc = acc[:, b, 0:2, :].rearrange("p a (c k) -> p (a c) k", c=2)
                        h = 2 * g + j
                        band = X_[:, 6 * TP + 256 * h + lo:6 * TP + 256 * h + 256].unsqueeze(1) \
                            .to_broadcast([P, 4, 256 - lo])
                        do(vec.scalar_tensor_tensor(pb[:, :, lo:256], sc[:, :, lo:256], HD ** -0.5, band,
                                                    ALU.mult, ALU.add), f"free{b}")
                        if g == 0 and b == 0:
                            do(vec.memset(pb[:, 0:1, 0:128], NEG))
                        if g == 1:
                            do(vec.memset(X[:, 1 + b, 0:1024].rearrange("p (a x) -> p a x", x=512)[:, :, 0:128],
                                          NEG))
                        do(vec.tensor_reduce(S_[:, 16 + 4 * b:20 + 4 * b], pb[:, :, lo:256], AX, ALU.max,
                                             negate=True), "to_act")

                    def finish(b):
                        from_act()
                        pb = X[:, 1 + b, 0:1024].rearrange("p (i k) -> p i k", k=256)[:, :, lo:256]
                        do(vec.reciprocal(S_[:, 44 + 4 * b:48 + 4 * b], S_[:, 24 + 4 * b:28 + 4 * b]))
                        rl = S_[:, 44 + 4 * b:48 + 4 * b].unsqueeze(2).to_broadcast([P, 4, 256 - lo])
                        do(vec.tensor_tensor(pb, pb, rl, ALU.mult), "to_pe")
                        lse = S_[:, 32 + 4 * b:36 + 4 * b]
                        do(vec.tensor_tensor(lse, lse, S_[:, 16 + 4 * b:20 + 4 * b], ALU.subtract))
                        if pend:
                            take_lse()
                        do(vec.tensor_tensor(X[:, 5, 0:512].rearrange("p (i q) -> p i q", q=P),
                                             ident.unsqueeze(1).to_broadcast([P, 4, P]),
                                             lse.unsqueeze(2).to_broadcast([P, 4, P]), ALU.mult), "to_pe")
                        pend.append((g, j, b))

                    stats(0)
                    stats(1)
                    for b in range(2):
                        finish(b)
                        for part in ((0, 1) if g < 2 else (1,)):
                            aux_ready[part].step()
                            aux_free[part].step()
                        ready[b].step()
                        free[b].step()
                    take_lse()
            for b in range(2):
                free[b].wait(dve)
            top = R[:, 6, full]
            do(vec.tensor_tensor(top, R[:, 3, full], R[:, 4, full], ALU.max))
            do(vec.tensor_tensor(top, top, R[:, 5, full], ALU.max))
            for g in range(3):
                do(vec.tensor_tensor(R[:, 3 + g, full], R[:, 3 + g, full], top, ALU.subtract),
                   "to_act" if g == 2 else "dve_step")
            from_act()
            do(vec.tensor_tensor(top, R[:, 3, full], R[:, 4, full], ALU.add))
            do(vec.tensor_tensor(top, top, R[:, 5, full], ALU.add))
            do(vec.reciprocal(top, top))
            for g in range(3):
                do(vec.tensor_tensor(R[:, 3 + g, full], R[:, 3 + g, full], top, ALU.mult))
                do(vec.tensor_tensor(R[:, g, full], R[:, g, full], R[:, 3 + g, full], ALU.mult))
                split(R[:, g, full], Ah[:, 5 + g, full], Al[:, 5 + g, full], "a_ready")

            def add_to_residual(j, s, pieces, c0, width):
                x = X[:, j, c0:c0 + width].rearrange("p (a b) -> p a b", a=pieces[0])
                do(vec.tensor_tensor(x, acc_view(s, pieces), x, ALU.add), f"free{s}")

            dve.wait_ge(sems["xre_in"], 16)
            for j in range(KC):
                await_unit()
                add_to_residual(j, j % 2, PIECES1, META, T1)
                if j:
                    add_square(j - 1, KC, SQ, full)
            add_square(KC - 1, KC, SQ, full)
            ready[1].step()
            free[1].step()
            normalise(KC, lambda j: X[:, j, META:T2], "norm2", R[:, 10, :], R[:, 11, :], T1)
            dve.wait_ge(sems["pos_in"], 16)
            do(vec.tensor_scalar(R[:, 9, META:T2], R[:, 8, META:T2].bitcast(I32), float(META), None, ALU.add))
            do(vec.tensor_copy(R[:, 9, 0:META], C_[:, 704:720]))
            do(vec.memset(R[:, 9, T2:TP], 0.0))
            ang, k, sn, cs = R[:, 9, 0:TP], R[:, 8, 0:TP], R[:, 17, 0:TP], R[:, 16, 0:TP]
            magic, pi = 12582912.0, 3.1415925
            do(vec.tensor_scalar(ang, ang, param("freq"), None, ALU.mult))
            do(vec.tensor_scalar(k, ang, float(1 / (2 * np.pi)), magic, ALU.mult, ALU.add))
            do(vec.tensor_scalar_add(k, k, -magic))
            c1, c2 = 6.28125, 2029 / 2 ** 20
            c3 = float(2 * np.pi - c1 - c2)
            do(vec.scalar_tensor_tensor(ang, k, -c1, ang, ALU.mult, ALU.add))
            do(vec.scalar_tensor_tensor(ang, k, -c2, ang, ALU.mult, ALU.add))
            do(vec.scalar_tensor_tensor(ang, k, -c3, ang, ALU.mult, ALU.add))
            do(vec.tensor_scalar(sn, ang, pi, -pi, ALU.min, ALU.max))
            do(vec.tensor_scalar_add(ang, ang, float(np.pi / 2)))
            do(vec.tensor_scalar(k, ang, float(np.pi), float(-2 * np.pi), ALU.is_gt, ALU.mult))
            do(vec.tensor_tensor(ang, ang, k, ALU.add))
            do(vec.tensor_scalar(cs, ang, pi, -pi, ALU.min, ALU.max), "to_act")
            with dve.Fori(0, GROUPS) as i:
                loop = Loop(i, GROUPS, [(unit, FG + 4), (free[0], FG // 2 + 4), (free[1], FG // 2 + 4),
                                        (ready[0], 4), (c["f_ready"], FG), (c["dve_step"], 2 * FG)])
                for j in range(FG):
                    unit.step()
                    await_free(j % 2)
                    do(vec.tensor_tensor(R[:, 11, full], R[:, 12 + j, full], R[:, 12 + j, full], ALU.mult))
                    split(R[:, 11, full], F[:, j, full], F[:, 4 + j, full], "f_ready")
                for j in range(KC):
                    if j % 2:
                        await_unit()
                    else:
                        await_ready(0)
                    add_to_residual(j, j % 2, PIECES1, META, T1)
                loop.end()
            ready[0].step()
            free[0].step()
            do(vec.memset(X[:, :, T2:TP], 0.0))
            for j in range(KC):
                add_square(j, KC, SQ, full)
            c["rs_ready"].step()
            dve.wait_ge(sems["rs_ready"], c["rs_ready"].value())
            for j in range(KC):
                do(vec.scalar_tensor_tensor(X[:, j, META:T2], X[:, j, META:T2], param("final", j),
                                            R[:, 10, full], ALU.mult, ALU.mult), "to_act")
                if j:
                    add_square(j - 1, KC, SQ, slice(0, TP))
            add_square(KC - 1, KC, SQ, slice(0, TP))
            wide = slice(0, TP)
            dve.wait_ge(sems["meta_in"], 16)
            for l in range(LAYERS):
                last = l == LAYERS - 1
                ready[0].step()
                free[0].step()
                normalise(KC, lambda j: X[:, j, :], f"n2_{l}", R[:, 10, :], R[:, 11, :], TP)
                do(vec.memset(R[:, 0:4, 0:16], 0.0), "to_act")
                dve.wait_ge(sems["spilled"], 16 * (l + 1))
                for g in range(4):
                    unit.step()
                    await_free(g % 2)
                    u = R[:, g, :]
                    bufs = (X_[:, 4 * TP:4 * TP + 1060], X_[:, 6 * TP:6 * TP + 1060])
                    cur, first = u, 0
                    for k in range(g + 1):
                        first += 2 ** k
                        to = bufs[k % 2]
                        do(vec.tensor_tensor(to[:, first:1060], cur[:, first:1060],
                                             cur[:, first - 2 ** k:1060 - 2 ** k], ALU.add))
                        cur = to
                    w = POOLW[g]
                    y = X[:, 2, :]
                    do(vec.scalar_tensor_tensor(y, cur[:, 16:1060], 1.0 / w, u[:, 16:1060], ALU.mult,
                                                ALU.subtract))
                    do(vec.tensor_tensor(y[:, 0:16], cur[:, 16:32], C_[:, 640 + 16 * g:656 + 16 * g], ALU.mult))
                    do(vec.tensor_tensor(y[:, 0:16], y[:, 0:16], u[:, 16:32], ALU.subtract))
                    split(y, G[:, g, wide], G[:, 4 + g, wide], "f_ready")
                for j in range(4):
                    await_unit()
                    from_act()
                    z = R[:, 4 + j, wide]
                    do(vec.tensor_tensor(cut(z, PIECES2), acc_view(j % 2, PIECES2), cut(z, PIECES2), ALU.mult),
                       f"free{j % 2}")
                for j in range(4):
                    if j < 3:
                        await_ready(j % 2)
                    else:
                        await_unit()
                    y = X[:, 2, :]
                    do(vec.scalar_tensor_tensor(cut(y, PIECES2), acc_view(j % 2, PIECES2), param(f"ps_{l}", j),
                                                cut(R[:, 4 + j, :], PIECES2), ALU.mult, ALU.mult), f"free{j % 2}")
                    split(y, G[:, j, wide], G[:, 4 + j, wide], "f_ready")
                for j in range(4):
                    for s in range(2):
                        unit.step()
                        await_free(s)
                    for s in range(2):
                        if s == 0:
                            await_ready(0)
                        else:
                            await_unit()
                        do(vec.tensor_tensor(cut(X[:, 2 * j + s, :], PIECES2), acc_view(s, PIECES2),
                                             cut(R[:, s, :], PIECES2), ALU.mult), f"free{s}")
                for j in range(8):
                    unit.step()
                    free[j % 2].step()
                    add_square(j % 6, 6 if j < 6 else 2, SQL[j // 6], wide)
                unit.step()
                from_act()
                dve.wait_ge(sems["t_in"], 16 * (l + 1))
                dve.wait_ge(sems["m_spilled"], 16 * (l + 1))
                rr, rope = slice(0, 2 * ROPE), slice(0, ROPE)
                do(vec.scalar_tensor_tensor(cut(X[rr, 4, :], PIECES2), acc_view(0, PIECES2, rr),
                                            param(f"kn_{l}", 0, rr), cut(R[rr, 17, :], PIECES2),
                                            ALU.mult, ALU.mult), "free0")
                do(vec.tensor_copy(X[rope, 7, :], X[ROPE:2 * ROPE, 4, :]))
                do(vec.tensor_tensor(R[rope, 16, 0:TP], X[rope, 4, :], X[rope, 7, :], ALU.add))
                do(vec.tensor_scalar(R[:, 17, 0:TP], R[:, 17, 0:TP], param(f"qn_{l}"), QKD ** -0.5,
                                     ALU.mult, ALU.mult))
                for j in range(4):
                    s = 1 - j % 2
                    await_unit()
                    from_act()
                    z = X[:, j, :]
                    do(vec.tensor_tensor(cut(z, PIECES2), acc_view(s, PIECES2), cut(z, PIECES2), ALU.mult),
                       f"free{s}")
                for s, c0, n, gain, rs in ((1, 0, 6, f"qa_{l}", R[:, 4, wide]), (0, 6, 2, f"kva_{l}", R[:, 5, wide])):
                    ready[s].step()
                    free[s].step()
                    c["rs_ready"].step()
                    dve.wait_ge(sems["rs_ready"], c["rs_ready"].value())
                    for j in range(n):
                        y = R[:, 8 + c0 + j, wide]
                        do(vec.scalar_tensor_tensor(y, y, param(gain, j), rs, ALU.mult, ALU.mult),
                           "to_act" if (s == 0 and j == 1) else "dve_step")
                for j in range(7):
                    unit.step()
                    await_free(j % 2)
                do(vec.memset(X[32:64, 7, :], 0.0))
                do(vec.memset(X[32:33, 7, :], 1.0))
                for j in (6, 7, 0, 1, 2, 3, 4, 5):
                    if j == 5:
                        await_unit()
                    else:
                        c["a_used"].step()
                        dve.wait_ge(sems["a_used"], c["a_used"].value())
                    split(R[:, 8 + j, wide], Ah[:, j, :], Al[:, j, :], "a_ready")
                await_free(1)
                do(vec.tensor_copy(S_[:, 40:41], S_[:, 60:61]), "to_act")
                top = slice(64, 128)

                def head_table():
                    unit.step()
                    from_act()
                    do(vec.tensor_tensor(cut(X[:, 4, :], PIECES2), acc_view(0, PIECES2), cut(R[:, 17, :], PIECES2),
                                         ALU.mult), "free0")
                    do(vec.tensor_copy(X[rope, 7, :], X[ROPE:2 * ROPE, 4, :]))
                    do(vec.tensor_tensor(X[rope, 4, :], X[rope, 4, :], X[rope, 7, :], ALU.add))

                def head_query(h):
                    f = 4 * (h % 2)
                    c["rs_ready"].step()
                    dve.wait_ge(sems["rs_ready"], c["rs_ready"].value())
                    do(vec.scalar_tensor_tensor(X[:, 4, :], X[:, 4, :], param("rows96"), X[:, 5, :],
                                                ALU.mult, ALU.mult))
                    split(X[:, 4, :], F[:, f + Q0, 0:TP], F[:, f + Q0 + 1, 0:TP], "to_pe")

                def head_key(h):
                    f = 4 * (h % 2)
                    c["rs_ready"].step()
                    dve.wait_ge(sems["rs_ready"], c["rs_ready"].value())
                    do(vec.tensor_tensor(X[rope, 7, :], R[rope, 16, 0:TP], rsk[rope, :], ALU.mult))
                    do(vec.tensor_tensor(X[top, 7, :], X[top, 7, :], rsk[top, :], ALU.mult))
                    split(X[:, 7, :], F[:, f + K0, 0:TP], F[:, f + K0 + 1, 0:TP], "dve_step")

                def head_values():
                    for half in range(2):
                        aux_ready[half].step()
                        from_act()
                        if half == 0:
                            do(vec.tensor_tensor(V2[:, 0:8, 0:64], aux[:, 0, :].rearrange("p (t v) -> p t v", v=64),
                                                 V1[:, 0:8, 0:64].bitcast(F32), ALU.subtract), "aux_free0")
                        else:
                            do(vec.scalar_tensor_tensor(V2[:, 8, 0:64], aux[:, 1, 0:64], param("rows20"),
                                                        V1[:, 8, 0:64].bitcast(F32), ALU.mult, ALU.subtract),
                               "aux_free1")

                def low_parts(b):
                    s = 1 - b % 2
                    if b < 4:
                        ready[s].step()
                    for o, n in enumerate(BATCHES[b]):
                        if o < len(BATCHES[b]) - 1:
                            from_act()
                        elif b < 4:
                            await_free(s)
                        else:
                            free[1].wait(dve)
                        w = block_width(n)
                        k = c["lo_ready"].n % len(prob32)
                        do(vec.tensor_tensor(prob(n, 1)[:, 0:w], prob32[k][:, 0:w],
                                             prob(n, 0)[:, 0:w].bitcast(F32), ALU.subtract), "lo_ready")

                def head_out(h, pc):
                    aux_ready[pc % 2].step()
                    c["inv_ready"].step()
                    dve.wait_ge(sems["inv_ready"], c["inv_ready"].value())
                    w = piece_width(pc)
                    rows = slice(64 * (h % 2), 64 * (h % 2) + 64)
                    y = X[rows, h // 2, QP * pc:QP * pc + w]
                    do(vec.tensor_tensor(y, y, head_inv(rows, pc), ALU.mult))
                    do(vec.tensor_tensor(y, aux[0:64, pc % 2, 0:w], y, ALU.mult), f"aux_free{pc % 2}")

                def maxima(i):
                    s = i % 2
                    await_ready(s)
                    do(vec.tensor_reduce(S_[:, 16 + i:17 + i],
                                         acc[:, s, :, :].rearrange("p a b -> p (a b)")[:, 0:min(P * (i + 1), TP)],
                                         AX, ALU.max, negate=True), f"free{s}")

                def linear_counts():
                    for s in (1, 1, 0):
                        ready[s].step()
                        free[s].step()

                head_table()
                linear_counts()
                dve.wait_ge(sems["g_spilled"], 16 * (l + 1))
                do(vec.tensor_copy(V1[:, 0:8, 64:128], ones[:, 0:64].unsqueeze(1).to_broadcast([P, 8, 64])))
                do(vec.tensor_scalar(V1[:, 8, 64:128], ones[:, 0:64], param("rows20"), None, ALU.mult))
                do(vec.tensor_scalar(V2[:, 0:8, 64:128], ones[:, 0:64].unsqueeze(1).to_broadcast([P, 8, 64]), 0.0,
                                     None, ALU.mult))
                do(vec.tensor_scalar(V2[:, 8, 64:128], ones[:, 0:64], 0.0, None, ALU.mult))
                do(vec.tensor_copy(ident_r, ident))
                do(vec.tensor_copy(causal_r, C_[:, 384:512]))
                do(vec.tensor_copy(after_r, C_[:, 512:640]))
                head_key(0)
                head_query(0)
                for h in range(MH):
                    more = h + 1 < MH
                    maxima(0)
                    if h:
                        low_parts(4)
                    for i in range(1, TB):
                        maxima(i)
                        if h and i == 1:
                            head_out(h - 1, 1)
                        if not more and i == 1:
                            do(vec.tensor_copy(S_[:, 40:41], S_[:, 60:61]), "to_act")
                        if h and i == 4:
                            head_out(h - 1, 2)
                    head_values()
                    if more:
                        head_table()
                        linear_counts()
                    for half in range(2):
                        aux_ready[half].step()
                        aux_free[half].step()
                    if more:
                        head_key(h + 1)
                    low_parts(0)
                    low_parts(1)
                    head_out(h, 0)
                    if more:
                        head_query(h + 1)
                    else:
                        for j in range(2):
                            split(X[:, j, :], Fy[0][:, j, wide], Fy[1][:, j, wide], "f_ready")
                    low_parts(2)
                    low_parts(3)
                    ready[1].step()
                    free[1].step()
                low_parts(4)
                head_out(MH - 1, 1)
                head_out(MH - 1, 2)
                do(vec.tensor_copy(S_[:, 40:41], S_[:, 60:61]), "to_act")
                for j in range(2, 4):
                    split(X[:, j, :], Fy[0][:, j, wide], Fy[1][:, j, wide], "f_ready")
                do(vec.tensor_copy(S_[:, 40:41], S_[:, 60:61]), "to_act")
                for j in range(KC):
                    s = j % 2
                    if s == 0:
                        await_ready(0)
                    else:
                        await_unit()
                    y = R[:, 8 + j, wide]
                    dve.wait_ge(sems[f"reload{j}"], 48 * l + 32)
                    do(vec.tensor_tensor(cut(y, PIECES2), acc_view(s, PIECES2), cut(y, PIECES2), ALU.mult),
                       f"free{s}")
                    do(vec.tensor_tensor(y, y, X[:, j, :], ALU.add), "to_act")
                    split(y, Ah[:, j, :], Al[:, j, :], "a_ready")
                for j in range(KC):
                    await_unit()
                    dve.wait_ge(sems[f"reload{j}"], 48 * (l + 1))
                    add_to_residual(j, j % 2, PIECES2, 0, TP)
                    if not last and j:
                        add_square(j - 1, KC, SQ, wide)
                if not last:
                    add_square(KC - 1, KC, SQ, wide)


def weight_stream(w):
    units = []

    def rows(m, order=None):
        k = m.shape[0] // P
        m = m.reshape(k, P, m.shape[1])
        return m if order is None else m[list(order)]

    def unit(*blocks):
        u = np.zeros((P, UW), np.float32)
        at = 0
        for b in blocks:
            k, _, m = b.shape
            u[:, at:at + k * m] = b.transpose(1, 0, 2).reshape(P, k * m)
            at += k * m
        units.append(u)

    A, C, L = ATTN_HEADS * HD, 256, 384
    w_in = rows(w["w_in"][0])
    q0, k0, v0 = 0, A, 2 * A
    ca, cg = 3 * A, 3 * A + C
    lg = 3 * A + 2 * C
    lx = lg + L
    cols = [cg, cg + P, ca, ca + P] + [lx + P * j for j in range(3)] + [lg + P * j for j in range(3)]
    for g in range(3):
        cols += [q0 + P * g, k0 + P * g, v0 + P * g]
    for col in cols:
        unit(w_in[:, :, col:col + P])
    w_out = rows(w["w_out"][0], (5, 6, 7, 3, 4, 0, 1, 2))
    for j in range(KC):
        unit(w_out[:, :, P * j:P * j + P])
    up, down = rows(w["w_up"][0]), rows(w["w_down"][0])
    for g in range(GROUPS):
        for j in range(FG):
            col = P * (FG * g + j)
            unit(up[:, :, col:col + P])
        d = down[FG * g:FG * g + FG]
        for j in range(4):
            unit(d[:, :, 256 * j:256 * j + P], d[:, :, 256 * j + P:256 * j + 256])
    for l in range(LAYERS):
        wi = rows(w["w_in_2"][l])
        for j in range(8):
            unit(wi[:, :, P * j:P * j + P])
        unit(*[w["pool_w_group_2"][l][g][None] for g in range(4)])
        pu = rows(w["pool_w_up_2"][l])
        for j in range(4):
            for s in range(2):
                col = 2592 + P * (2 * j + s)
                unit(wi[:, :, col:col + P])
            unit(pu[:, :, 256 * j:256 * j + P], pu[:, :, 256 * j + P:256 * j + 256])
        for j in range(8):
            unit(wi[:, :, 1024 + P * j:1024 + P * j + P])
        rope = np.zeros((KC, P, P), np.float32)
        rope[:, :, 0:ROPE] = wi[:, :, 2048:2080]
        rope[:, :, ROPE:2 * ROPE] = np.roll(wi[:, :, 2048:2080], ROPE // 2, axis=2)
        unit(rope)
        for j in range(4):
            unit(wi[:, :, 2080 + P * j:2080 + P * j + P])
        for j in range(8):
            unit(wi[:, :, 3616 + P * j:3616 + P * j + P])
        wq, wkv = rows(w["w_q_b_2"][l]), rows(w["w_kv_b_2"][l])
        for h in range(MH):
            q, kv = wq[:, :, QKD * h:QKD * h + QKD], wkv[:, :, P * h:P * h + P]
            q = np.concatenate([q[:, :, NOPE:], np.roll(q[:, :, NOPE:], ROPE // 2, axis=2), q[:, :, :NOPE]], axis=2)
            kv = np.concatenate([kv[:, :, NOPE:], kv[:, :, :NOPE]], axis=2)
            unit(q, kv)
        mu = rows(w["mla_w_up_2"][l])
        for j in range(4):
            unit(mu[:, :, 256 * j:256 * j + P], mu[:, :, 256 * j + P:256 * j + 256])
        wo = rows(w["w_out_2"][l])
        for j in range(8):
            unit(wo[:, :, P * j:P * j + P])
    assert len(units) == N_UNITS, (len(units), N_UNITS)
    return np.stack(units)


def param_table(w):
    t = np.zeros((P, NPARAM), np.float32)

    def put(name, v, i=0):
        t[:, PARAM_COLS[name] + i:PARAM_COLS[name] + i + v.shape[1]] = v

    def col(v):
        return v.reshape(-1, P).T

    put("norm1", col(w["norm1_g"][0]))
    for j in range(2):
        put("cdw", w["conv_dw_w"][0][:, P * j:P * j + P].T, CONV_TAPS * j)
    for j in range(3):
        put("lcw", w["lru_conv_w"][0][:, P * j:P * j + P].T, LRU_TAPS * j)
    for name, src in (("cdb", "conv_dw_b"), ("clg", "conv_ln_g"), ("clb", "conv_ln_b"), ("lcb", "lru_conv_b"),
                      ("lba", "lru_ba"), ("lbx", "lru_bx"), ("lam", "lru_lambda"), ("norm2", "norm2_g")):
        put(name, col(w[src][0]))
    put("final", col(w["final_g"]))
    for l in range(LAYERS):
        put(f"n2_{l}", col(w["norm_gain_2"][l]))
        put(f"ps_{l}", col(w["pool_scale_2"][l]))
        put(f"qa_{l}", col(w["q_a_norm_gain_2"][l]))
        put(f"kva_{l}", col(w["kv_a_norm_gain_2"][l]))
        for name, g in (("qn", w["q_norm_gain_2"][l]), ("kn", w["k_norm_gain_2"][l])):
            at = PARAM_COLS[f"{name}_{l}"]
            t[0:ROPE, at] = g[NOPE:]
            t[ROPE:2 * ROPE, at] = np.roll(g[NOPE:], ROPE // 2)
            t[2 * ROPE:, at] = g[:NOPE]
    half = ROPE // 2
    inv = (np.float32(10000.0) ** (-np.arange(half, dtype=np.float32) / np.float32(half))).astype(np.float32)
    for i in range(4):
        t[half * i:half * i + half, PARAM_COLS["freq"]] = inv
    t[ROPE:ROPE + half, PARAM_COLS["sign"]] = -1.0
    t[ROPE + half:2 * ROPE, PARAM_COLS["sign"]] = 1.0
    t[:, PARAM_COLS["rows96"]] = 1.0
    t[ROPE:2 * ROPE, PARAM_COLS["rows96"]] = 0.0
    t[P - (TP - P * (TB - 1)):, PARAM_COLS["rows20"]] = 1.0
    return t


def recurrent_gates(w):
    t = np.zeros((P, 2, 3, P), np.float32)
    for m, name in enumerate(("lru_wa", "lru_wx")):
        for h in range(6):
            o = 64 * (h % 2)
            t[o:o + 64, m, h // 2, o:o + 64] = w[name][0][h]
    return t.reshape(P, -1)


def kernel(**inputs):
    import concourse.bacc as bacc
    from concourse.bass_utils import run_bass_kernel_spmd

    w = {k: np.asarray(v) for k, v in inputs.items()}
    consts, bands = shape_constants()
    arrays = {
        "xT": np.ascontiguousarray(w["x"][0].T),
        "metaT": np.ascontiguousarray(w["meta_tokens_2"].T),
        "pos": np.ascontiguousarray(np.broadcast_to(w["positions_2"], (P, T1))),
        "params": param_table(w),
        "consts": consts,
        "bands": bands,
        "lru_w": recurrent_gates(w),
        "wstream": weight_stream(w),
    }
    nc = bacc.Bacc("TRN2", target_bir_lowering=False, num_devices=1)
    args = [nc.dram_tensor("in_" + k, a.shape, mybir.dt.from_np(a.dtype), kind="ExternalInput").ap()
            for k, a in arrays.items()]
    out = nc.dram_tensor("outT", (DM, T1), F32, kind="ExternalOutput")
    build(nc, *args, out.ap())
    r = run_bass_kernel_spmd(nc, [{"in_" + k: a for k, a in arrays.items()}], core_ids=[0])
    return np.ascontiguousarray(r.results[0]["outT"].T)[None]
```
